# Optimizing a Trainium2 kernel written in Bass

```python
import math
import jax, jax.numpy as jnp
from jax import lax
import numpy as np

D_MODEL = 1024
BATCH = 1
SEQ = 256
DEPTH = 2

PLE_DIM = 256
ROPE_THETA = 500000.0
NORM_EPS = 1e-6
Q_BLOCK = 128

DA_HEADS = 4
DA_DQK = 64
DA_DV = 2 * DA_DQK
DA_ROT = DA_DQK // 4

SSD_HEADS = 8
SSD_HEADDIM = 64
SSD_DINNER = SSD_HEADS * SSD_HEADDIM
SSD_GROUPS = 2
SSD_DSTATE = 128
SSD_CONV = 4
SSD_CHUNK = 128
SSD_CONV_DIM = SSD_DINNER + 2 * SSD_GROUPS * SSD_DSTATE

GLA_HEADS = 4
GLA_DK = 64
GLA_DV = 128
GLA_GATE_RANK = 16
GLA_GATE_NORMALIZER = 16.0
GLA_CHUNK = 64

DA_WIDTH = DA_HEADS * DA_DV
GLA_WIDTH = GLA_HEADS * GLA_DV
MIX_WIDTH = DA_WIDTH + SSD_DINNER + GLA_WIDTH
D_FF = -(-8 * D_MODEL // (3 * 256)) * 256

IN_SIZES = (
    DA_HEADS * 2 * DA_DQK,
    DA_HEADS * 2 * DA_DQK,
    DA_WIDTH,
    SSD_DINNER,
    SSD_CONV_DIM,
    SSD_HEADS,
    GLA_HEADS * GLA_DK,
    GLA_HEADS * GLA_DK,
    GLA_WIDTH,
    GLA_WIDTH,
    GLA_GATE_RANK,
)
IN_COLS = sum(IN_SIZES)
IN_SPLITS = tuple(int(v) for v in np.cumsum(IN_SIZES)[:-1])


def rms_norm(x, gain):
    xf = x.astype(jnp.float32)
    y = xf * lax.rsqrt(jnp.mean(xf * xf, axis=-1, keepdims=True) + NORM_EPS)
    return (y * gain.astype(jnp.float32)).astype(x.dtype)

def rope_tables(positions):
    inv_freq = ROPE_THETA ** (-jnp.arange(0, DA_ROT, 2, dtype=jnp.float32) / DA_ROT)
    ang = positions.astype(jnp.float32)[..., None] * inv_freq
    return jnp.cos(ang), jnp.sin(ang)

def partial_rope(x, cos, sin):
    half = DA_ROT // 2
    x1 = x[..., :half].astype(jnp.float32)
    x2 = x[..., half:DA_ROT].astype(jnp.float32)
    c = cos[:, :, None, :]
    s = sin[:, :, None, :]
    r1 = (x1 * c - x2 * s).astype(x.dtype)
    r2 = (x2 * c + x1 * s).astype(x.dtype)
    return jnp.concatenate([r1, r2, x[..., DA_ROT:]], axis=-1)

def diff_attention(q, k, v, positions, g_q, g_k, lq1, lk1, lq2, lk2, g_sub, lambda_init):
    B, S = q.shape[:2]
    q = rms_norm(q.reshape(B, S, DA_HEADS * 2, DA_DQK), g_q)
    k = rms_norm(k.reshape(B, S, DA_HEADS * 2, DA_DQK), g_k)
    v = v.reshape(B, S, DA_HEADS, DA_DV)
    cos, sin = rope_tables(positions)
    q = partial_rope(q, cos, sin).reshape(B, S, DA_HEADS, 2, DA_DQK)
    k = partial_rope(k, cos, sin).reshape(B, S, DA_HEADS, 2, DA_DQK)
    lam = (jnp.exp(jnp.sum(lq1.astype(jnp.float32) * lk1.astype(jnp.float32)))
           - jnp.exp(jnp.sum(lq2.astype(jnp.float32) * lk2.astype(jnp.float32)))
           + lambda_init)
    scale = DA_DQK ** -0.5
    n_blk = S // Q_BLOCK
    qb = q.reshape(B, n_blk, Q_BLOCK, DA_HEADS, 2, DA_DQK).transpose(1, 0, 2, 3, 4, 5)
    key_idx = jnp.arange(S)

    def one_block(args):
        qi, bi = args
        s = jnp.einsum('bqhcd,bkhcd->bhcqk', qi, k,
                       preferred_element_type=jnp.float32) * scale
        q_idx = bi * Q_BLOCK + jnp.arange(Q_BLOCK)
        causal = key_idx[None, :] <= q_idx[:, None]
        s = jnp.where(causal, s, -jnp.inf)
        pr = jax.nn.softmax(s, axis=-1)
        attn = pr[:, :, 0] - lam * pr[:, :, 1]
        return jnp.einsum('bhqk,bkhd->bqhd', attn.astype(v.dtype), v)

    out = lax.map(one_block, (qb, jnp.arange(n_blk)))
    out = out.transpose(1, 0, 2, 3, 4).reshape(B, S, DA_HEADS, DA_DV)
    out = rms_norm(out, g_sub) * (1.0 - lambda_init)
    return out.reshape(B, S, DA_WIDTH)

def ssd_mixer(z, xbc, dt_raw, conv_w, conv_b, dt_bias, a_log, d_skip, g_norm):
    B, S = z.shape[:2]
    G, R, P, N, L = SSD_GROUPS, SSD_HEADS // SSD_GROUPS, SSD_HEADDIM, SSD_DSTATE, SSD_CHUNK
    nc = S // L
    xbc = lax.conv_general_dilated(
        xbc, conv_w[:, None, :], window_strides=(1,), padding=[(SSD_CONV - 1, 0)],
        dimension_numbers=('NWC', 'WIO', 'NWC'), feature_group_count=SSD_CONV_DIM) + conv_b
    xbc = jax.nn.silu(xbc)
    xs, bs, cs = jnp.split(xbc, [SSD_DINNER, SSD_DINNER + G * N], axis=-1)
    dt = jax.nn.softplus(dt_raw.astype(jnp.float32) + dt_bias.astype(jnp.float32))
    a = -jnp.exp(a_log.astype(jnp.float32))
    xh = xs.astype(jnp.float32).reshape(B, nc, L, G, R, P)
    xdt = xh * dt.reshape(B, nc, L, G, R)[..., None]
    bm = bs.astype(jnp.float32).reshape(B, nc, L, G, N)
    cm = cs.astype(jnp.float32).reshape(B, nc, L, G, N)
    cum = jnp.cumsum((dt * a).reshape(B, nc, L, G, R), axis=2)
    seg = cum[:, :, :, None] - cum[:, :, None, :]
    causal = jnp.tril(jnp.ones((L, L), dtype=bool))[:, :, None, None]
    decay = jnp.exp(jnp.where(causal, seg, -jnp.inf))
    cb = jnp.einsum('bclgn,bcsgn->bclsg', cm, bm)
    y_diag = jnp.einsum('bclsgr,bcsgrp->bclgrp', cb[..., None] * decay, xdt)
    decay_to_end = jnp.exp(cum[:, :, -1:] - cum)
    states = jnp.einsum('bclgn,bclgrp->bcgrpn', bm, xdt * decay_to_end[..., None])
    chunk_decay = jnp.exp(cum[:, :, -1])

    def step(h, inp):
        st, dec = inp
        return dec[..., None, None] * h + st, h

    h0 = jnp.zeros((B, G, R, P, N), jnp.float32)
    _, prev = lax.scan(step, h0, (states.transpose(1, 0, 2, 3, 4, 5),
                                  chunk_decay.transpose(1, 0, 2, 3)))
    prev = prev.transpose(1, 0, 2, 3, 4, 5)
    y_off = jnp.einsum('bclgn,bcgrpn->bclgrp', cm, prev) * jnp.exp(cum)[..., None]
    y = y_diag + y_off + d_skip.astype(jnp.float32).reshape(G, R)[:, :, None] * xh
    y = y.reshape(B, S, SSD_DINNER) * jax.nn.silu(z.astype(jnp.float32))
    y = rms_norm(y.reshape(B, S, G, SSD_DINNER // G), g_norm.reshape(G, SSD_DINNER // G))
    return y.reshape(B, S, SSD_DINNER).astype(z.dtype)

def gla_mixer(q, k, v, g_out, gate_lr, w_gate2, b_gate, g_norm):
    B, S = q.shape[:2]
    H, DK, DV, L = GLA_HEADS, GLA_DK, GLA_DV, GLA_CHUNK
    nc = S // L
    gk = jax.nn.log_sigmoid((gate_lr @ w_gate2 + b_gate).astype(jnp.float32)) / GLA_GATE_NORMALIZER
    qf = q.astype(jnp.float32).reshape(B, nc, L, H, DK) * (DK ** -0.5)
    kf = k.astype(jnp.float32).reshape(B, nc, L, H, DK)
    vf = v.astype(jnp.float32).reshape(B, nc, L, H, DV)
    bcum = jnp.cumsum(gk.reshape(B, nc, L, H, DK), axis=2)
    q_dec = qf * jnp.exp(bcum)
    k_inv = kf * jnp.exp(-bcum)
    att = jnp.einsum('bclhd,bcshd->bchls', q_dec, k_inv)
    att = jnp.where(jnp.tril(jnp.ones((L, L), dtype=bool)), att, 0.0)
    o_intra = jnp.einsum('bchls,bcshv->bclhv', att, vf)
    k_end = kf * jnp.exp(bcum[:, :, -1:] - bcum)
    states = jnp.einsum('bclhd,bclhv->bchdv', k_end, vf)
    chunk_decay = jnp.exp(bcum[:, :, -1])

    def step(st_prev, inp):
        st, dec = inp
        return dec[..., None] * st_prev + st, st_prev

    s0 = jnp.zeros((B, H, DK, DV), jnp.float32)
    _, prev = lax.scan(step, s0, (states.transpose(1, 0, 2, 3, 4),
                                  chunk_decay.transpose(1, 0, 2, 3)))
    prev = prev.transpose(1, 0, 2, 3, 4)
    o_inter = jnp.einsum('bclhd,bchdv->bclhv', q_dec, prev)
    o = (o_intra + o_inter).reshape(B, S, H, DV)
    o = rms_norm(o, g_norm) * jax.nn.silu(g_out.astype(jnp.float32).reshape(B, S, H, DV))
    return o.reshape(B, S, GLA_WIDTH).astype(q.dtype)

def first_inputs(seed: int = 0) -> dict:
    key = jax.random.key(seed)
    ks = iter(jax.random.split(key, 48))

    def nrm(shape, scale):
        return jax.random.normal(next(ks), shape, jnp.float32) * scale

    def gain(shape):
        return 1.0 + nrm(shape, 0.02)

    x = nrm((BATCH, SEQ, D_MODEL), 1.0)
    p = nrm((DEPTH, BATCH, SEQ, PLE_DIM), 1.0)
    positions = jnp.broadcast_to(jnp.arange(SEQ, dtype=jnp.int32)[None, :], (BATCH, SEQ))
    dt0 = jnp.exp(jax.random.uniform(next(ks), (DEPTH, SSD_HEADS), jnp.float32)
                  * (math.log(0.1) - math.log(0.001)) + math.log(0.001))
    ssd_dt_bias = dt0 + jnp.log(-jnp.expm1(-dt0))
    ssd_a_log = jnp.log(jax.random.uniform(next(ks), (DEPTH, SSD_HEADS), jnp.float32,
                                           minval=1.0, maxval=16.0))
    return {
        'x': x,
        'p': p,
        'positions': positions,
        'attn_norm': gain((DEPTH, D_MODEL)),
        'w_in': nrm((DEPTH, D_MODEL, IN_COLS), D_MODEL ** -0.5),
        'da_q_norm': gain((DEPTH, DA_DQK)),
        'da_k_norm': gain((DEPTH, DA_DQK)),
        'da_lambda_q1': nrm((DEPTH, DA_DQK), 0.1),
        'da_lambda_k1': nrm((DEPTH, DA_DQK), 0.1),
        'da_lambda_q2': nrm((DEPTH, DA_DQK), 0.1),
        'da_lambda_k2': nrm((DEPTH, DA_DQK), 0.1),
        'da_sub_norm': gain((DEPTH, DA_DV)),
        'ssd_conv_w': nrm((DEPTH, SSD_CONV, SSD_CONV_DIM), SSD_CONV ** -0.5),
        'ssd_conv_b': nrm((DEPTH, SSD_CONV_DIM), 0.02),
        'ssd_dt_bias': ssd_dt_bias,
        'ssd_a_log': ssd_a_log,
        'ssd_d': 1.0 + nrm((DEPTH, SSD_HEADS), 0.1),
        'ssd_norm': gain((DEPTH, SSD_DINNER)),
        'gla_w_gate2': nrm((DEPTH, GLA_GATE_RANK, GLA_HEADS * GLA_DK), GLA_GATE_RANK ** -0.5),
        'gla_b_gate': nrm((DEPTH, GLA_HEADS * GLA_DK), 0.02),
        'gla_norm': gain((DEPTH, GLA_DV)),
        'w_out': nrm((DEPTH, MIX_WIDTH, D_MODEL), MIX_WIDTH ** -0.5),
        'ffn_norm': gain((DEPTH, D_MODEL)),
        'w_ffn_gate': nrm((DEPTH, D_MODEL, D_FF), D_MODEL ** -0.5),
        'w_ffn_up': nrm((DEPTH, D_MODEL, D_FF), D_MODEL ** -0.5),
        'w_ffn_down': nrm((DEPTH, D_FF, D_MODEL), D_FF ** -0.5),
        'ple_w_proj': nrm((DEPTH, PLE_DIM, D_MODEL), PLE_DIM ** -0.5),
        'ple_w_gate': nrm((DEPTH, D_MODEL, D_MODEL), D_MODEL ** -0.5),
    }

def first_block(x, p, positions, attn_norm, w_in, da_q_norm, da_k_norm, da_lambda_q1,
              da_lambda_k1, da_lambda_q2, da_lambda_k2, da_sub_norm, ssd_conv_w, ssd_conv_b,
              ssd_dt_bias, ssd_a_log, ssd_d, ssd_norm, gla_w_gate2, gla_b_gate, gla_norm,
              w_out, ffn_norm, w_ffn_gate, w_ffn_up, w_ffn_down, ple_w_proj, ple_w_gate):
    h = x
    for i in range(DEPTH):
        lambda_init = 0.8 - 0.6 * math.exp(-0.3 * i)
        a = rms_norm(h, attn_norm[i])
        proj = a @ w_in[i]
        (da_q, da_k, da_v, ssd_z, ssd_xbc, ssd_dt,
         gla_q, gla_k, gla_v, gla_g, gla_lr) = jnp.split(proj, IN_SPLITS, axis=-1)
        y_da = diff_attention(da_q, da_k, da_v, positions, da_q_norm[i], da_k_norm[i],
                              da_lambda_q1[i], da_lambda_k1[i], da_lambda_q2[i],
                              da_lambda_k2[i], da_sub_norm[i], lambda_init)
        y_ssd = ssd_mixer(ssd_z, ssd_xbc, ssd_dt, ssd_conv_w[i], ssd_conv_b[i],
                          ssd_dt_bias[i], ssd_a_log[i], ssd_d[i], ssd_norm[i])
        y_gla = gla_mixer(gla_q, gla_k, gla_v, gla_g, gla_lr, gla_w_gate2[i],
                          gla_b_gate[i], gla_norm[i])
        mix = jnp.concatenate([y_da, y_ssd.astype(y_da.dtype), y_gla.astype(y_da.dtype)], axis=-1)
        h = h + mix @ w_out[i]
        f = rms_norm(h, ffn_norm[i])
        h = h + (jax.nn.silu(f @ w_ffn_gate[i]) * (f @ w_ffn_up[i])) @ w_ffn_down[i]
        h = h + jax.nn.sigmoid(h @ ple_w_gate[i]) * (p[i] @ ple_w_proj[i])
    return h


DEPTH_2 = 4

HEAD_DIM = 64
N_HEADS = D_MODEL // HEAD_DIM
SWA_KV_HEADS = max(1, N_HEADS // 8)
N_MIXERS = 3
SB_BLOCK = 128
MOBA_BLOCK = 256
MOBA_TOPK = 3
MOBA_QCHUNK = 16
SWA_WINDOW = 128
ROPE_THETA_2 = 10000.0
D_FF_2 = -(-8 * D_MODEL // (3 * 256)) * 256
EPS = 1e-6


def rms_norm_2(x, gain):
    xf = x.astype(jnp.float32)
    var = jnp.mean(xf * xf, axis=-1, keepdims=True)
    return (xf * lax.rsqrt(var + EPS)).astype(x.dtype) * gain

def modulate(h, shift, scale):
    return h * (1.0 + scale) + shift

def split_heads(t, n):
    b, s, _ = t.shape
    return t.reshape(b, s, n, HEAD_DIM).transpose(0, 2, 1, 3)

def merge_heads(t):
    b, n, s, d = t.shape
    return t.transpose(0, 2, 1, 3).reshape(b, s, n * d)

def rope_tables_2(seq_len):
    inv_freq = 1.0 / (ROPE_THETA_2 ** (jnp.arange(0, HEAD_DIM, 2, dtype=jnp.float32) / HEAD_DIM))
    ang = jnp.arange(seq_len, dtype=jnp.float32)[:, None] * inv_freq[None, :]
    return jnp.cos(ang), jnp.sin(ang)

def apply_rope(x, cos, sin):
    cos = cos.astype(x.dtype)
    sin = sin.astype(x.dtype)
    x1, x2 = jnp.split(x, 2, axis=-1)
    return jnp.concatenate([x1 * cos - x2 * sin, x2 * cos + x1 * sin], axis=-1)

def stick_breaking_attention(h, w_in, w_out):
    b, s_len, _ = h.shape
    q, k, v = jnp.split(h @ w_in, 3, axis=-1)
    q, k, v = split_heads(q, N_HEADS), split_heads(k, N_HEADS), split_heads(v, N_HEADS)
    nblk = s_len // SB_BLOCK
    q_blocks = q.reshape(b, N_HEADS, nblk, SB_BLOCK, HEAD_DIM).transpose(2, 0, 1, 3, 4)
    k_pos = jnp.arange(s_len)
    scale = HEAD_DIM ** -0.5

    def block(args):
        qb, bi = args
        q_pos = bi * SB_BLOCK + jnp.arange(SB_BLOCK)
        z = jnp.einsum('bhqd,bhkd->bhqk', qb, k).astype(jnp.float32) * scale
        past = k_pos[None, :] < q_pos[:, None]
        log_beta = jax.nn.log_sigmoid(z)
        log_keep = jnp.where(past, jax.nn.log_sigmoid(-z), 0.0)
        later = lax.cumsum(log_keep, axis=3, reverse=True) - log_keep
        a = jnp.where(past, jnp.exp(log_beta + later), 0.0)
        return jnp.einsum('bhqk,bhkd->bhqd', a.astype(v.dtype), v)

    o = lax.map(block, (q_blocks, jnp.arange(nblk)))
    o = o.transpose(1, 2, 0, 3, 4).reshape(b, N_HEADS, s_len, HEAD_DIM)
    return merge_heads(o) @ w_out

def moba_attention(h, w_in, qk_gain, w_out, cos, sin):
    b, s_len, _ = h.shape
    q, k, v = jnp.split(h @ w_in, 3, axis=-1)
    q, k, v = split_heads(q, N_HEADS), split_heads(k, N_HEADS), split_heads(v, N_HEADS)
    q = apply_rope(rms_norm_2(q, qk_gain[0]), cos, sin)
    k = apply_rope(rms_norm_2(k, qk_gain[1]), cos, sin)
    pad = (-s_len) % MOBA_BLOCK
    padw = ((0, 0), (0, 0), (0, pad), (0, 0))
    q, k, v = jnp.pad(q, padw), jnp.pad(k, padw), jnp.pad(v, padw)
    s_pad = s_len + pad
    nb = s_pad // MOBA_BLOCK
    topk = min(MOBA_TOPK, nb)
    k_blk = k.reshape(b, N_HEADS, nb, MOBA_BLOCK, HEAD_DIM)
    v_blk = v.reshape(b, N_HEADS, nb, MOBA_BLOCK, HEAD_DIM)
    k_mean = jnp.mean(k_blk.astype(jnp.float32), axis=3).astype(k.dtype)
    n_chunks = s_pad // MOBA_QCHUNK
    q_chunks = q.reshape(b, N_HEADS, n_chunks, MOBA_QCHUNK, HEAD_DIM).transpose(2, 0, 1, 3, 4)
    b_idx = jnp.arange(b)[:, None, None, None]
    h_idx = jnp.arange(N_HEADS)[None, :, None, None]
    blk_ids = jnp.arange(nb)
    in_blk = jnp.arange(MOBA_BLOCK)
    scale = HEAD_DIM ** -0.5

    def chunk(args):
        qc, ci = args
        q_pos = ci * MOBA_QCHUNK + jnp.arange(MOBA_QCHUNK)
        own = (ci * MOBA_QCHUNK) // MOBA_BLOCK
        gate = jnp.einsum('bhqd,bhnd->bhqn', qc, k_mean).astype(jnp.float32)
        gate = jnp.where(blk_ids < own, gate, -jnp.inf)
        top_val, top_idx = lax.top_k(gate, topk)
        sel_ok = jnp.isfinite(top_val)
        kg = k_blk[b_idx, h_idx, top_idx]
        vg = v_blk[b_idx, h_idx, top_idx]
        s_sel = jnp.einsum('bhqd,bhqnkd->bhqnk', qc, kg).astype(jnp.float32) * scale
        s_sel = jnp.where(sel_ok[..., None], s_sel, -jnp.inf)
        k_own = lax.dynamic_slice_in_dim(k, own * MOBA_BLOCK, MOBA_BLOCK, axis=2)
        v_own = lax.dynamic_slice_in_dim(v, own * MOBA_BLOCK, MOBA_BLOCK, axis=2)
        s_own = jnp.einsum('bhqd,bhkd->bhqk', qc, k_own).astype(jnp.float32) * scale
        own_pos = own * MOBA_BLOCK + in_blk
        s_own = jnp.where(own_pos[None, :] <= q_pos[:, None], s_own, -jnp.inf)
        qn = qc.shape[2]
        logits = jnp.concatenate([s_sel.reshape(b, N_HEADS, qn, topk * MOBA_BLOCK), s_own], axis=-1)
        p = jax.nn.softmax(logits, axis=-1).astype(v.dtype)
        p_sel = p[..., :topk * MOBA_BLOCK].reshape(b, N_HEADS, qn, topk, MOBA_BLOCK)
        p_own = p[..., topk * MOBA_BLOCK:]
        return (jnp.einsum('bhqnk,bhqnkd->bhqd', p_sel, vg)
                + jnp.einsum('bhqk,bhkd->bhqd', p_own, v_own))

    o = lax.map(chunk, (q_chunks, jnp.arange(n_chunks)))
    o = o.transpose(1, 2, 0, 3, 4).reshape(b, N_HEADS, s_pad, HEAD_DIM)[:, :, :s_len]
    return merge_heads(o) @ w_out

def swa_sink_attention(h, w_in, qk_gain, sinks, w_out, cos, sin):
    b, s_len, _ = h.shape
    qd, kvd = N_HEADS * HEAD_DIM, SWA_KV_HEADS * HEAD_DIM
    q, k, v = jnp.split(h @ w_in, [qd, qd + kvd], axis=-1)
    q, k, v = split_heads(q, N_HEADS), split_heads(k, SWA_KV_HEADS), split_heads(v, SWA_KV_HEADS)
    q = apply_rope(rms_norm_2(q, qk_gain[0]), cos, sin)
    k = apply_rope(rms_norm_2(k, qk_gain[1]), cos, sin)
    w = SWA_WINDOW
    nb = s_len // w
    g = N_HEADS // SWA_KV_HEADS
    qb = q.reshape(b, SWA_KV_HEADS, g, nb, w, HEAD_DIM)

    def band(t):
        tb = t.reshape(b, SWA_KV_HEADS, nb, w, HEAD_DIM)
        prev = jnp.pad(tb, ((0, 0), (0, 0), (1, 0), (0, 0), (0, 0)))[:, :, :-1]
        return jnp.concatenate([prev, tb], axis=3)

    kb, vb = band(k), band(v)
    s = jnp.einsum('bkgnqd,bknsd->bkgnqs', qb, kb).astype(jnp.float32) * (HEAD_DIM ** -0.5)
    q_off = jnp.arange(w)[:, None] + w
    k_off = jnp.arange(2 * w)[None, :]
    rel = q_off - k_off
    in_win = (rel >= 0) & (rel < SWA_WINDOW)
    valid = in_win[None] & ((jnp.arange(nb)[:, None, None] > 0) | (k_off >= w)[None])
    s = jnp.where(valid, s, -jnp.inf)
    sink = sinks.astype(jnp.float32).reshape(SWA_KV_HEADS, g)[None, :, :, None, None, None]
    m = jnp.maximum(jnp.max(s, axis=-1, keepdims=True), sink)
    e = jnp.exp(s - m)
    p = e / (jnp.sum(e, axis=-1, keepdims=True) + jnp.exp(sink - m))
    o = jnp.einsum('bkgnqs,bknsd->bkgnqd', p.astype(v.dtype), vb)
    o = o.reshape(b, N_HEADS, s_len, HEAD_DIM)
    return merge_heads(o) @ w_out

def swiglu(h, w_gate, w_up, w_down):
    return (jax.nn.silu(h @ w_gate) * (h @ w_up)) @ w_down

def second_inputs(seed: int = 0) -> dict:
    key = jax.random.key(seed)
    ks = jax.random.split(key, 20)
    d = D_MODEL
    hd = N_HEADS * HEAD_DIM
    n_sb, n_moba, n_swa = (DEPTH_2 + 2) // 3, (DEPTH_2 + 1) // 3, DEPTH_2 // 3

    def nrm(k, shape, scale):
        return jax.random.normal(k, shape, jnp.float32) * scale

    return {
        "x": nrm(ks[0], (BATCH, SEQ, d), 1.0),
        "c": nrm(ks[1], (BATCH, d), 1.0),
        "ada_w": nrm(ks[2], (DEPTH_2, d, 6 * d), 0.5 * d ** -0.5),
        "ada_b": nrm(ks[3], (DEPTH_2, 6 * d), 0.02),
        "norm_gain": 1.0 + nrm(ks[4], (DEPTH_2, 2, d), 0.02),
        "ffn_w_gate": nrm(ks[5], (DEPTH_2, d, D_FF_2), d ** -0.5),
        "ffn_w_up": nrm(ks[6], (DEPTH_2, d, D_FF_2), d ** -0.5),
        "ffn_w_down": nrm(ks[7], (DEPTH_2, D_FF_2, d), D_FF_2 ** -0.5),
        "sb_w_in": nrm(ks[8], (n_sb, d, 3 * hd), d ** -0.5),
        "sb_w_out": nrm(ks[9], (n_sb, hd, d), hd ** -0.5),
        "moba_w_in": nrm(ks[10], (n_moba, d, 3 * hd), d ** -0.5),
        "moba_qk_gain": 1.0 + nrm(ks[11], (n_moba, 2, HEAD_DIM), 0.02),
        "moba_w_out": nrm(ks[12], (n_moba, hd, d), hd ** -0.5),
        "swa_w_in": nrm(ks[13], (n_swa, d, (N_HEADS + 2 * SWA_KV_HEADS) * HEAD_DIM), d ** -0.5),
        "swa_qk_gain": 1.0 + nrm(ks[14], (n_swa, 2, HEAD_DIM), 0.02),
        "swa_sinks": nrm(ks[15], (n_swa, N_HEADS), 0.5),
        "swa_w_out": nrm(ks[16], (n_swa, hd, d), hd ** -0.5),
    }

def second_block(x, c, ada_w, ada_b, norm_gain, ffn_w_gate, ffn_w_up, ffn_w_down,
              sb_w_in, sb_w_out, moba_w_in, moba_qk_gain, moba_w_out,
              swa_w_in, swa_qk_gain, swa_sinks, swa_w_out):
    s_len = x.shape[1]
    cos, sin = rope_tables_2(s_len)
    c_act = jax.nn.silu(c)
    for i in range(DEPTH_2):
        mod = c_act @ ada_w[i] + ada_b[i]
        sh1, sc1, g1, sh2, sc2, g2 = [m[:, None, :] for m in jnp.split(mod, 6, axis=-1)]
        h = modulate(rms_norm_2(x, norm_gain[i, 0]), sh1, sc1)
        kind, j = i % N_MIXERS, i // N_MIXERS
        if kind == 0:
            y = stick_breaking_attention(h, sb_w_in[j], sb_w_out[j])
        elif kind == 1:
            y = moba_attention(h, moba_w_in[j], moba_qk_gain[j], moba_w_out[j], cos, sin)
        else:
            y = swa_sink_attention(h, swa_w_in[j], swa_qk_gain[j], swa_sinks[j], swa_w_out[j], cos, sin)
        x = x + g1 * y
        h = modulate(rms_norm_2(x, norm_gain[i, 1]), sh2, sc2)
        x = x + g2 * swiglu(h, ffn_w_gate[i], ffn_w_up[i], ffn_w_down[i])
    return x


def setup_inputs(seed=0):
    out = dict(first_inputs(seed))
    for name, value in second_inputs(seed + 1).items():
        if name != "x":
            out[name + "_2"] = value
    return out


def reference(
    x, p, positions, attn_norm, w_in, da_q_norm, da_k_norm, da_lambda_q1, da_lambda_k1,
    da_lambda_q2, da_lambda_k2, da_sub_norm, ssd_conv_w, ssd_conv_b, ssd_dt_bias, ssd_a_log,
    ssd_d, ssd_norm, gla_w_gate2, gla_b_gate, gla_norm, w_out, ffn_norm, w_ffn_gate, w_ffn_up,
    w_ffn_down, ple_w_proj, ple_w_gate, c_2, ada_w_2, ada_b_2, norm_gain_2, ffn_w_gate_2,
    ffn_w_up_2, ffn_w_down_2, sb_w_in_2, sb_w_out_2, moba_w_in_2, moba_qk_gain_2, moba_w_out_2,
    swa_w_in_2, swa_qk_gain_2, swa_sinks_2, swa_w_out_2,
):
    x = first_block(
        x, p, positions, attn_norm, w_in, da_q_norm, da_k_norm, da_lambda_q1, da_lambda_k1,
        da_lambda_q2, da_lambda_k2, da_sub_norm, ssd_conv_w, ssd_conv_b, ssd_dt_bias, ssd_a_log,
        ssd_d, ssd_norm, gla_w_gate2, gla_b_gate, gla_norm, w_out, ffn_norm, w_ffn_gate,
        w_ffn_up, w_ffn_down, ple_w_proj, ple_w_gate,
    )
    return second_block(
        x, c_2, ada_w_2, ada_b_2, norm_gain_2, ffn_w_gate_2, ffn_w_up_2, ffn_w_down_2,
        sb_w_in_2, sb_w_out_2, moba_w_in_2, moba_qk_gain_2, moba_w_out_2, swa_w_in_2,
        swa_qk_gain_2, swa_sinks_2, swa_w_out_2,
    )


_drawn_inputs = setup_inputs


def setup_inputs(seed=0):
    import zlib

    import numpy as np

    out = dict(_drawn_inputs(seed))
    spreads = {}
    factors = {'da_q_norm': 5.793,
     'da_k_norm': 5.641,
     'da_lambda_q1': 4.074,
     'da_lambda_k2': 3.647,
     'da_sub_norm': 5.756,
     'ssd_conv_b': 2.928,
     'ssd_norm': 4.26,
     'gla_b_gate': 8.0,
     'gla_norm': 7.303,
     'ffn_norm': 3.312,
     'norm_gain_2': 7.431,
     'moba_qk_gain_2': 8.0,
     'swa_qk_gain_2': 8.0,
     'swa_sinks_2': 200.0}
    for name, (base, spread) in spreads.items():
        noise = np.random.default_rng([zlib.crc32(name.encode()), seed]).standard_normal(out[name].shape)
        drawn = base * np.exp(spread * noise) if base else spread * noise
        out[name] = __import__('jax').numpy.asarray(drawn.astype(out[name].dtype))
    for name, factor in factors.items():
        out[name] = (out[name] * factor).astype(out[name].dtype)
    return out
```

```python
import math
from contextlib import ExitStack

import numpy as np
import concourse.bass as bass
from concourse import mybir

F32 = mybir.dt.float32
BF16 = mybir.dt.bfloat16
I32 = mybir.dt.int32
ALU = mybir.AluOpType
ACT = mybir.ActivationFunctionType
AX = mybir.AxisListType.X

P = 128
D = 1024
KT = D // P
S = 256
TT = S // P
FF = 2816
NF = FF // P
DEPTH = 2
DEPTH_2 = 4
EPS = 1e-6
BIG = 1.0e30
OFF_DA_Q, OFF_DA_K, OFF_DA_V = 0, 512, 1024
OFF_Z, OFF_X, OFF_B, OFF_C, OFF_DT = 1536, 2048, 2560, 2816, 3072
OFF_GQ, OFF_GK, OFF_GV, OFF_GG, OFF_LR = 3080, 3336, 3592, 4104, 4616
HEAD_SCALE = 64 ** -0.5
ADA_TILES = 6 * KT
TWO_PI_PARTS = (6.28125, 0.0019340515136718750, 1.2556659146e-06)


def constants():
    p = np.arange(P)
    q = np.arange(P)
    ident = np.eye(P)
    ones = np.ones((P, P))
    halves = (p[:, None] // 64 == q[None, :] // 64) * 1.0
    later = (p[:, None] > q[None, :]) * 1.0
    upto = (p[:, None] <= q[None, :]) * 1.0

    def turn(half, width):
        m = np.zeros((P, P))
        for b in range(0, P, 64):
            for d in range(half):
                m[b + d + half, b + d] = -1.0
                m[b + d, b + d + half] = 1.0
        return m

    causal = np.where(q[None, :] <= p[:, None], 0.0, -BIG)
    causal_neg = np.concatenate([causal, np.zeros((P, P)), causal], 1)
    window = np.where(q[None, :] > p[:, None], 0.0, -BIG)
    window_neg = np.concatenate([causal, window, causal], 1)
    past = (p[:, None] < q[None, :]) * 1.0
    past01 = np.concatenate([past, np.ones((P, P)), past], 1)
    keep = np.tile((np.arange(S) % 64 != 0) * 1.0, (P, 1))
    tri64 = (p[:, None] % 64 <= np.arange(64)[None, :]) * 1.0
    inv2 = (1.0 / (np.float32(10000.0) ** (np.arange(0, 64, 2, dtype=np.float32) / np.float32(64)))).astype(np.float32)
    ang = (np.arange(S, dtype=np.float32)[None, :] * inv2[p % 32][:, None]).astype(np.float32)
    cos2, sin2 = np.cos(ang.astype(np.float64)), np.sin(ang.astype(np.float64))
    inv1 = (np.float32(500000.0) ** (-np.arange(0, 16, 2, dtype=np.float32) / np.float32(16))).astype(np.float32)
    inv = np.where(p % 64 < 16, inv1[p % 8], 0.0)[:, None]
    parts = dict(ident=ident, ones=ones, halves=halves, later=later, upto=upto, turn_da=turn(8, 16),
                 turn=turn(32, 64), causal=causal_neg, window=window_neg, past=past01, keep=keep,
                 tri64=tri64, cos2=cos2, sin2=sin2, inv=inv)
    at, cols = {}, 0
    for name, a in parts.items():
        at[name] = (cols, cols + a.shape[1])
        cols += a.shape[1]
    return np.concatenate([a.astype(np.float32) for a in parts.values()], 1), at


ATT_STEP = dict(v_copied=1, pv_done=1, y_ready=1, scores=2, qk_ready=1)
NORMED = dict(qk_sq=1, qk_ss=1, qk_rs=1, qk_n=1, qk_rot=1, negmax=2, exps=2)
KINDS = {
    "da": dict(ATT_STEP, **NORMED, p_ready=1, p_tr=1, pt_ready=1, y_sq=1, y_ss=1, y_rs=1),
    "moba": dict(ATT_STEP, **NORMED, p_ready=2, p_tr=2, pt_ready=2),
    "swa": dict(ATT_STEP, **NORMED, p_ready=2, p_tr=2, pt_ready=2),
    "sb": dict(ATT_STEP, s_read=2, sb_log=2, sb_spm=2, sb_later=2, sb_la=2, sb_exp=2, pt_ready=2),
}
SSD = dict.fromkeys("""ssd_conv ssd_u ssd_ln ssd_da ssd_act ssd_cum ssd_cumc ssd_xtok ssd_cb ssd_xe ssd_st
                       ssd_m ssd_stc ssd_y ssd_yg ssd_sq ssd_ss ssd_rs ssd_yn""".split(), 1) | dict(ssd_dif=2, ssd_dec=2)
GLA = dict.fromkeys("""gla_lr gla_pgk gla_u gla_ls gla_scan gla_ked gla_e gla_ev gla_dec gla_kee gla_tr gla_kt gla_att
                       gla_attm gla_states gla_st gla_o gla_sq gla_ss gla_rs gla_yn""".split(), 1)
ADA_SLOTS = 4
SLOT_MIX, SLOT_ADA, SLOT_FF, SLOT_SMALL = 0, 4, 8, 14
N_SLOTS = 18


def schedule():
    phases, at = [], {}

    def phase(kind, counts, **more):
        phases.append((kind, dict(at), more))
        for k, v in counts.items():
            at[k] = at.get(k, 0) + v

    def slots(base, uses):
        return {f"slot{base + n}": u for n, u in enumerate(uses)}

    def norm(**more):
        phase("norm", dict(squares=4, sumsq=1, rstd=1, h_ready=KT), **more)

    def attention(kind, n, **more):
        counts = {k: v * n for k, v in KINDS[kind].items()}
        if kind == "swa":
            counts.update(extra1=n, extra2=n)
        phase("att", dict(counts, **slots(SLOT_MIX, [n] * 4)), att=kind, n=n, **more)

    def add(**more):
        phase("add", dict(x_ready=4), **more)

    def ffn(ada=None, **more):
        counts = dict(silu_ready=NF, mid_ready=NF, **slots(SLOT_FF, [NF // 2] * 6))
        if ada is not None:
            counts.update(ada_rows=1, ada_sums=1, **slots(SLOT_ADA, [ADA_TILES // ADA_SLOTS] * ADA_SLOTS))
        phase("ffn", counts, ada=ada, **more)

    phase("setup", dict(x_ready=4))
    for l in range(DEPTH):
        norm(gain=("attn", l))
        attention("da", 4, layer=l)
        for g in range(2):
            phase("ssd", dict(SSD, **slots(SLOT_MIX, [1] * 8), **slots(SLOT_SMALL, [1])), layer=l, g=g)
        for g in range(2):
            phase("gla", dict(GLA, **slots(SLOT_MIX, [1] * 8), **slots(SLOT_SMALL + 1, [1])), layer=l, g=g)
        add(gate=None, last_slot=7)
        norm(gain=("ffn", l))
        ffn(ada=l, layer=l, stack=1)
        add(gate=None, last_slot=SLOT_FF + 5)
        phase("ple", dict(ple_t=1, ple_tc=1, ple_s=KT, ple_d=KT, x_ready=4,
                          **slots(SLOT_SMALL + 2, [4] * 2), **slots(SLOT_MIX + 4, [4] * 2)), layer=l)
    for l in range(DEPTH_2):
        norm(gain=("two", l, 0))
        attention(("sb", "moba", "swa")[l % 3], 8, layer=l)
        add(gate=(l, 2), last_slot=3)
        norm(gain=("two", l, 1))
        ffn(ada=l + 2 if l + 2 < DEPTH_2 else None, layer=l, stack=2)
        add(gate=(l, 5), last_slot=SLOT_FF + 5)
    phase("store", dict())
    return phases


def two_stacks(nc, a, table_dram, cols, out):
    phases = schedule()
    ctx = ExitStack()
    with ctx:
        ctx.enter_context(nc.allow_non_contiguous_dma(reason="small parameters"))

        def sb(name, shape, dt=F32):
            return ctx.enter_context(nc.sbuf_tensor(name, shape, dt))

        const = sb("const", [P, table_dram.shape[1]])
        xT = sb("xT", [P, KT, S])
        hT = sb("hT", [P, KT, S])
        sqT = sb("sqT", [P, KT, S])
        x_rows = sb("x_rows", [P, TT, D])
        wslot = sb("wslot", [P, SLOT_SMALL, D])
        wsmall = sb("wsmall", [P, 4, 256])
        prow = sb("prow", [P, 4, P])
        pcol = sb("pcol", [P, 4, P])
        ada_bias = pcol[:, 2:4, :]
        lam_in = sb("lam_in", [P, DEPTH, 4, 64])
        lam_tmp = sb("lam_tmp", [P, DEPTH, 2, 64])
        lam = sb("lam", [P, DEPTH, 4])
        neg_lam = sb("neg_lam", [P, DEPTH])
        da_gain = sb("da_gain", [P, DEPTH])
        dt_bias = sb("dt_bias", [P, DEPTH, 8])
        a_neg = sb("a_neg", [P, DEPTH, 8])
        wg2 = sb("wg2", [16, DEPTH, 256])
        sinks = sb("sinks", [P, 16])
        a_log = sb("a_log", [P, DEPTH, 8])
        skip_all = sb("skip_all", [P, DEPTH, 8])
        skip = sb("skip", [P, DEPTH, 4])
        c_act = sb("c_act", [P, KT])
        mod = sb("mod", [P, DEPTH_2, ADA_TILES])
        mod_gain = sb("mod_gain", [P, DEPTH_2, 2, KT])
        pos_i = sb("pos_i", [P, S], I32)
        ang = sb("ang", [P, S])
        turns = sb("turns", [P, S])
        cos1 = sb("cos1", [P, S])
        sin1 = sb("sin1", [P, S])
        rs = sb("rs", [P, S])
        sq2 = sb("sq2", [P, 512])
        rs2 = sb("rs2", [P, 512])
        qkn = sb("qkn", [P, 512])
        qkc = sb("qkc", [P, 512])
        qk = sb("qk", [P, 512])
        v_sb = sb("v_sb", [P, TT, 256])
        sm = sb("sm", [P, 2, 384])
        pr = sb("pr", [P, 2, 384])
        pt = sb("pt", [P, 2, 384])
        mx = sb("mx", [P, 4])
        nmx = sb("nmx", [P, 4])
        sums = sb("sums", [P, 4])
        esink = sb("esink", [P, 4])
        rinv = sb("rinv", [P, 4])
        sink_now = sb("sink_now", [P, 2])
        y_sb = sb("y_sb", [P, 512])
        ysq = sb("ysq", [P, 512])
        conv = sb("conv", [P, 4, S])
        xbc = sb("xbc", [P, 4, S])
        z_sb = sb("z_sb", [P, 2, S])
        dts = sb("dts", [P, 8, 8])
        cum = sb("cum", [P, 8])
        xdt = sb("xdt", [P, TT, 4, 64])
        xe = sb("xe", [P, 4, 64])
        b_tok = sb("b_tok", [P, P])
        cbm = sb("cbm", [P, TT, P])
        dif = sb("dif", [P, TT, 512])
        mt = sb("mt", [P, TT, 512])
        ce = sb("ce", [P, 512])
        wend = sb("wend", [P, 4])
        wexp = sb("wexp", [P, 4])
        prev = sb("prev", [P, 256])
        silu_g = sb("silu_g", [P, 2, S])
        mid = sb("mid", [P, 2, S])
        lb = sb("lb", [P, 2, 384])
        attm = sb("attm", [P, 2, S])
        st_sb = sb("st_sb", [P, 384])
        ang2 = sb("ang2", [P, S])
        ada_prod = [x[:, :, :].rearrange("p a s -> p (a s)").rearrange("p (k c) -> p k c", k=KT) for x in (conv, xbc)]
        ada_rows = sb("ada_rows", [P, ADA_TILES, P])
        zero = sb("zero", [1, 512], BF16)
        epst = sb("epst", [P, 1])

        acc = ctx.enter_context(nc.psum_tensor("acc", [P, KT, S], F32))
        bank = ctx.enter_context(nc.psum_tensor("bank", [P, 4, 512], F32))

        names = sorted({k for _, at, _ in phases for k in at if not k.startswith(("slot", "extra"))})
        sem = {k: ctx.enter_context(nc.semaphore(k)) for k in names}
        slot_full = [ctx.enter_context(nc.semaphore(f"slot_full{n}")) for n in range(N_SLOTS)]
        slot_used = [ctx.enter_context(nc.semaphore(f"slot_used{n}")) for n in range(N_SLOTS)]
        loaded = ctx.enter_context(nc.semaphore("loaded"))
        x_loaded = ctx.enter_context(nc.semaphore("x_loaded"))
        p_loaded = ctx.enter_context(nc.semaphore("p_loaded"))
        consts_ready = ctx.enter_context(nc.semaphore("consts_ready"))
        params_turned = ctx.enter_context(nc.semaphore("params_turned"))
        params_ready = ctx.enter_context(nc.semaphore("params_ready"))
        x_turned = ctx.enter_context(nc.semaphore("x_turned"))
        rows_ready = ctx.enter_context(nc.semaphore("rows_ready"))
        small_ready = ctx.enter_context(nc.semaphore("small_ready"))
        small_exp = ctx.enter_context(nc.semaphore("small_exp"))
        cact_ready = ctx.enter_context(nc.semaphore("cact_ready"))
        rope_ready = ctx.enter_context(nc.semaphore("rope_ready"))
        reduced = ctx.enter_context(nc.semaphore("reduced"))
        stored = ctx.enter_context(nc.semaphore("stored"))
        def C(name, lo=0, hi=None):
            b, e = cols[name]
            return const[:, b + lo:(e if hi is None else b + hi)]

        def B(n, lo=0, hi=512):
            return bank[:, n, lo:hi]

        def per_head(ap, n):
            return ap.unsqueeze(2).broadcast_to([ap.shape[0], ap.shape[1], n])

        def per_tile(ap, n):
            return ap.unsqueeze(1).broadcast_to([ap.shape[0], n, ap.shape[1]])

        def gain_of(gain):
            if gain[0] == "attn":
                return pcol[:, 0, 8 * gain[1]:8 * gain[1] + 8]
            if gain[0] == "ffn":
                return pcol[:, 0, 16 + 8 * gain[1]:24 + 8 * gain[1]]
            return mod_gain[:, gain[1], gain[2], :]

        CONV_B, C_ROW, SSD_G = 96, 112, 120
        CONV_W, B_GATE, GLA_G, DA_SUB, DA_Q, DA_K, MOBA_G, SWA_G = 0, 64, 68, 70, 72, 74, 76, 78
        N_B = 80

        def qk_gains(kind, l):
            q, k = {"da": (DA_Q + l, DA_K + l), "moba": (MOBA_G, MOBA_G + 1), "swa": (SWA_G, SWA_G + 1)}[kind]
            return pcol[:, 1, q:q + 1], pcol[:, 1, k:k + 1]

        def rows(n, lo, hi):
            return prow[lo:hi, n, :]

        def over(ap, shape):
            return ap.unsqueeze(0).broadcast_to(shape)

        def twice(ap, rows_n):
            return ap.unsqueeze(1).broadcast_to([rows_n, 2, 64])

        tiles = "l (t p) -> (l t) p"
        loads = [
            (pos_i[:, :], a["positions"][0:1, :].broadcast_to([P, S])),
            (rows(0, 0, 16), a["attn_norm"].rearrange(tiles, p=P)),
            (rows(0, 16, 32), a["ffn_norm"].rearrange(tiles, p=P)),
            (rows(0, 32, 96), a["norm_gain_2"].rearrange("l n (t p) -> (l n t) p", p=P)),
            (rows(0, CONV_B, C_ROW), a["ssd_conv_b"].rearrange(tiles, p=P)),
            (rows(0, C_ROW, SSD_G), a["c_2"].rearrange(tiles, p=P)),
            (rows(0, SSD_G, P), a["ssd_norm"].rearrange(tiles, p=P)),
            (rows(1, CONV_W, B_GATE), a["ssd_conv_w"].rearrange("l w (t p) -> (l w t) p", p=P)),
            (rows(1, B_GATE, GLA_G), a["gla_b_gate"].rearrange(tiles, p=P)),
            (rows(1, GLA_G, DA_SUB), a["gla_norm"]),
            (rows(1, DA_SUB, DA_Q), a["da_sub_norm"]),
            (rows(1, DA_Q, DA_K).rearrange("r (u d) -> r u d", u=2), twice(a["da_q_norm"], 2)),
            (rows(1, DA_K, MOBA_G).rearrange("r (u d) -> r u d", u=2), twice(a["da_k_norm"], 2)),
            (rows(1, MOBA_G, SWA_G).rearrange("r (u d) -> r u d", u=2), twice(a["moba_qk_gain_2"][0], 2)),
            (rows(1, SWA_G, N_B).rearrange("r (u d) -> r u d", u=2), twice(a["swa_qk_gain_2"][0], 2)),
        ] + [
            (rows(2 + n, 0, 96), a["ada_b_2"][2 * n:2 * n + 2].rearrange(tiles, p=P)) for n in range(2)
        ] + [
            (lam_in[:, :, n, :], over(a[name], [P, DEPTH, 64]))
            for n, name in enumerate(("da_lambda_q1", "da_lambda_k1", "da_lambda_q2", "da_lambda_k2"))
        ] + [
            (skip_all[:, :, :], over(a["ssd_d"], [P, DEPTH, 8])),
            (dt_bias[:, :, :], over(a["ssd_dt_bias"], [P, DEPTH, 8])),
            (a_log[:, :, :], over(a["ssd_a_log"], [P, DEPTH, 8])),
            (wg2[:, :, :], a["gla_w_gate2"].rearrange("l r c -> r l c")),
            (sinks[:, :], a["swa_sinks_2"][0:1, :].broadcast_to([P, 16])),
        ]

        block = ctx.enter_context(nc.Block())

        @block.sync
        def _(sp):
            def unit(w, row_tiles, col, width=P):
                return w[0:row_tiles * P, bass.ds(col, width)].rearrange("(k p) c -> p k c", p=P)

            def mix_slot(n):
                return wslot[:, n, :].rearrange("p (k c) -> p k c", k=KT)

            def load(n, dst, src, uses):
                sp.wait_ge(slot_used[n], uses)
                sp.dma_start(dst, src).then_inc(slot_full[n], 16)

            for kind, at, ph in phases:
                u = [at.get(f"slot{n}", 0) for n in range(N_SLOTS)]
                if kind == "att":
                    att, l = ph["att"], ph["layer"]
                    if att == "da":
                        w, wo = a["w_in"][l], a["w_out"][l]
                        offs = (OFF_DA_Q, OFF_DA_K, OFF_DA_V)
                    elif att == "sb":
                        w, wo, offs = a["sb_w_in_2"][l // 3], a["sb_w_out_2"][l // 3], (0, D, 2 * D)
                    elif att == "moba":
                        w, wo, offs = a["moba_w_in_2"][l // 3], a["moba_w_out_2"][l // 3], (0, D, 2 * D)
                    else:
                        w, wo, offs = a["swa_w_in_2"][l // 3], a["swa_w_out_2"][l // 3], (0, D, D + P)
                    if att == "swa":
                        for kv in range(2):
                            with sp.Fori(0, 4) as i:
                                q_col = sp.snap((i + 4 * kv) * P)
                                row = sp.snap((i + 4 * kv) * P)
                                need = [sp.snap(i + 4 * kv + u[n] + 1) for n in range(4)]
                                load(0, mix_slot(0), unit(w, KT, q_col), need[0])
                                for n in (1, 2):
                                    kv_src = unit(w, KT, D + P * (n - 1) + 64 * kv, 64)
                                    sp.wait_ge(slot_used[n], need[n])
                                    for half in range(2):
                                        sp.dma_start(mix_slot(n)[:, :, 64 * half:64 * half + 64], kv_src)\
                                            .then_inc(slot_full[n], 16)
                                load(3, wslot[:, 3, :], wo[bass.ds(row, P), :], need[3])
                    else:
                        with sp.Fori(0, ph["n"]) as i:
                            col = [sp.snap(i * P + o) for o in offs]
                            row = sp.snap(i * P)
                            need = [sp.snap(i + u[n] + 1) for n in range(4)]
                            for n in range(3):
                                load(n, mix_slot(n), unit(w, KT, col[n]), need[n])
                            load(3, wslot[:, 3, :], wo[bass.ds(row, P), :], need[3])
                elif kind == "ssd":
                    l, g = ph["layer"], ph["g"]
                    w = a["w_in"][l]
                    for n, col in enumerate((OFF_X + 256 * g, OFF_X + 256 * g + P, OFF_B + P * g, OFF_C + P * g,
                                             OFF_Z + 256 * g, OFF_Z + 256 * g + P)):
                        load(n, mix_slot(n), unit(w, KT, col), u[n] + 1)
                    load(SLOT_SMALL, wsmall[:, 0, 0:32].rearrange("p (k c) -> p k c", k=KT),
                         unit(w, KT, OFF_DT + 4 * g, 4), u[SLOT_SMALL] + 1)
                    for n in range(2):
                        row = 512 + 256 * g + P * n
                        load(6 + n, wslot[:, 6 + n, :], a["w_out"][l][row:row + P, :], u[6 + n] + 1)
                elif kind == "gla":
                    l, g = ph["layer"], ph["g"]
                    w = a["w_in"][l]
                    load(SLOT_SMALL + 1, wsmall[:, 1, 0:P].rearrange("p (k c) -> p k c", k=KT),
                         unit(w, KT, OFF_LR, 16), u[SLOT_SMALL + 1] + 1)
                    for n, col in enumerate((OFF_GQ + P * g, OFF_GK + P * g, OFF_GV + 256 * g, OFF_GV + 256 * g + P,
                                             OFF_GG + 256 * g, OFF_GG + 256 * g + P)):
                        load(n, mix_slot(n), unit(w, KT, col), u[n] + 1)
                    for n in range(2):
                        row = 1024 + 256 * g + P * n
                        load(6 + n, wslot[:, 6 + n, :], a["w_out"][l][row:row + P, :], u[6 + n] + 1)
                elif kind == "ffn":
                    l, tail = ph["layer"], "" if ph["stack"] == 1 else "_2"
                    wg, wu, wd = (a[("ffn_" if tail else "") + n + tail][l] for n in
                                  (("w_gate", "w_up", "w_down") if tail else ("w_ffn_gate", "w_ffn_up", "w_ffn_down")))
                    ada = ph["ada"]
                    with sp.Fori(0, NF // 2) as i:
                        col = [sp.snap((2 * i + b) * P) for b in range(2)]
                        need = [sp.snap(i + u[SLOT_FF + n] + 1) for n in range(6)]
                        if ada is not None:
                            acol = [sp.snap((ADA_SLOTS * i + n) * P) for n in range(ADA_SLOTS)]
                            aneed = [sp.snap(i + u[SLOT_ADA + n] + 1) for n in range(ADA_SLOTS)]
                        for b in range(2):
                            s = SLOT_FF + 3 * b
                            load(s, mix_slot(s), unit(wg, KT, col[b]), need[3 * b])
                            load(s + 1, mix_slot(s + 1), unit(wu, KT, col[b]), need[3 * b + 1])
                            load(s + 2, wslot[:, s + 2, :], wd[bass.ds(col[b], P), :], need[3 * b + 2])
                            if ada is not None:
                                for n in range(2 * b, 2 * b + 2):
                                    s = SLOT_ADA + n
                                    load(s, mix_slot(s), unit(a["ada_w_2"][ada], KT, acol[n]), aneed[n])
                    if ada is not None:
                        for n in range(ADA_SLOTS):
                            s = SLOT_ADA + n
                            load(s, mix_slot(s), unit(a["ada_w_2"][ada], KT, (ADA_TILES - ADA_SLOTS + n) * P),
                                 NF // 2 + u[s] + 1)
                elif kind == "ple":
                    l = ph["layer"]
                    with sp.Fori(0, KT // 2) as i:
                        col = [sp.snap((2 * i + b) * P) for b in range(2)]
                        need = [sp.snap(i + u[SLOT_MIX + 4 + b] + 1) for b in range(2)]
                        sneed = [sp.snap(i + u[SLOT_SMALL + 2 + b] + 1) for b in range(2)]
                        for b in range(2):
                            load(4 + b, mix_slot(4 + b), unit(a["ple_w_gate"][l], KT, col[b]), need[b])
                            load(SLOT_SMALL + 2 + b, wsmall[:, 2 + b, :].rearrange("p (k c) -> p k c", k=2),
                                 unit(a["ple_w_proj"][l], 2, col[b]), sneed[b])
            sp.wait_ge(rows_ready, 1)
            sp.dma_start(out[0].rearrange("(t p) d -> p t d", p=P), x_rows[:, :, :]).then_inc(stored, 16)
            sp.wait_ge(stored, 16)

        @block.tensor
        def _(pe):
            for n in range(N_SLOTS):
                pe.sem_inc(slot_used[n], 1)

            def wk(n, k):
                return wslot[:, n, P * k:P * k + P]

            def feature_tile(n, dst, uses, at=None):
                pe.wait_ge(slot_full[n], uses)
                for k in range(KT):
                    if at is not None:
                        pe.wait_ge(sem["h_ready"], at + k + 1)
                    mm = pe.matmul(dst, wk(n, k), hT[:, k, :], start=(k == 0), stop=(k == KT - 1))
                mm.then_inc(slot_used[n], 1)
                return mm

            def token_tiles(n, dst, uses):
                pe.wait_ge(slot_full[n], uses)
                for t in range(TT):
                    for k in range(KT):
                        mm = pe.matmul(dst(t), hT[:, k, P * t:P * t + P], wk(n, k), start=(k == 0), stop=(k == KT - 1))
                mm.then_inc(slot_used[n], 1)

            def clear_acc():
                for m in range(4):
                    pe.matmul(acc[:, 2 * m:2 * m + 2, :].rearrange("p m s -> p (m s)"), zero[0:1, 0:P], zero[0:1, :],
                              start=True, stop=False, skip_group_check=True)

            def add_out(n, y, tiles=range(KT), free=True):
                for m in tiles:
                    mm = pe.matmul(acc[:, m, :], wk(n, m), y, start=False, stop=False, skip_group_check=True)
                if free:
                    mm.then_inc(slot_used[n], 1)

            pe.wait_ge(consts_ready, 1)
            pe.wait_ge(x_loaded, 32)
            ident = C("ident")
            for m in range(KT):
                for t in range(TT):
                    mm = pe.transpose(acc[:, m, P * t:P * t + P], x_rows[:, t, P * m:P * m + P], ident)
            mm.then_inc(x_turned, 1)
            pe.wait_ge(loaded, 16 * len(loads))
            for n, rows in enumerate((P, N_B, 96, 96)):
                mm = pe.transpose(B(0, P * n, P * n + rows), prow[0:rows, n, :], const[0:rows, cols["ident"][0]:cols["ident"][0] + rows])
            mm.then_inc(params_turned, 1)

            def attention(ph, at, first_h):
                att = ph["att"]
                n = ph["n"]
                g = lambda k: at.get(k, 0)
                normed = att != "sb"

                def full_kv(n, i):
                    return 16 * (g(f"slot{n}") + g(f"extra{n}")) + (32 if att == "swa" else 16) * (i + 1)

                def proj_qk(i, first=False):
                    if not first:
                        pe.wait_ge(sem["qk_n" if normed else "qk_ready"], g("qk_n" if normed else "qk_ready") + i)
                    h = g("h_ready") - 8 if first else None
                    feature_tile(0, B(0, 0, 256), 16 * (g("slot0") + i + 1), h)
                    pe.wait_ge(slot_full[1], full_kv(1, i))
                    for k in range(KT):
                        mm = pe.matmul(B(0, 256, 512), wk(1, k), hT[:, k, :], start=(k == 0), stop=(k == KT - 1))
                    mm.then_inc(slot_used[1], 1)
                    return mm

                def scores(i):
                    pe.wait_ge(sem["qk_ready"], g("qk_ready") + i + 1)
                    pe.wait_ge(consts_ready, 1)
                    for hh in range(2):
                        r = slice(64 * hh, 64 * hh + 64)
                        if att == "sb":
                            pe.matmul(bank[:, 2 + hh, 0:256], qk[r, 256:384], qk[r, 0:256], start=True, stop=True)
                            mm = pe.matmul(bank[:, 2 + hh, 256:384], qk[r, 384:512], qk[r, 128:256], start=True, stop=True)
                        else:
                            pe.matmul(bank[:, 2 + hh, 0:128], qk[r, 0:128], qk[r, 256:384], start=True, stop=True)
                            mm = pe.matmul(bank[:, 2 + hh, 128:384], qk[r, 128:256], qk[r, 256:512], start=True, stop=True)
                        mm.then_inc(sem["scores"], 1)

                def middle(i):
                    if att == "sb":
                        for hh in range(2):
                            pe.wait_ge(sem["sb_spm"], g("sb_spm") + 2 * i + hh + 1)
                            pe.matmul(bank[:, 2 + hh, 0:256], C("later"), sm[:, hh, 0:256], start=True, stop=False)
                            pe.matmul(bank[:, 2 + hh, 128:256], C("ones"), sm[:, hh, 256:384], start=False, stop=True)
                            pe.matmul(bank[:, 2 + hh, 256:384], C("later"), sm[:, hh, 256:384], start=True, stop=True)\
                                .then_inc(sem["sb_later"], 1)
                        return
                    heads = 1 if att == "da" else 2
                    for hh in range(heads):
                        pe.wait_ge(sem["p_ready"], g("p_ready") + heads * i + hh + 1)
                        for b in range(3):
                            mm = pe.transpose(bank[:, 2 + hh, P * b:P * b + P], pr[:, hh, P * b:P * b + P], ident)
                        mm.then_inc(sem["p_tr"], 1)

                def values(i):
                    heads = 1 if att == "da" else 2
                    width = P // heads
                    pe.wait_ge(sem["v_copied"], g("v_copied") + i + 1)
                    pe.wait_ge(consts_ready, 1)
                    for hh in range(heads):
                        c = slice(width * hh, width * hh + width)
                        pe.wait_ge(sem["pt_ready"], g("pt_ready") + heads * i + hh + 1)
                        pe.wait_ge(consts_ready, 1)
                        pe.matmul(bank[c, 1, 0:256], v_sb[:, 0, c], pt[:, hh, 0:256], start=True, stop=False)
                        mm = pe.matmul(bank[c, 1, 128:256], v_sb[:, 1, c], pt[:, hh, 256:384], start=False, stop=True)
                    mm.then_inc(sem["pv_done"], 1)

                def proj_v(i, first):
                    if not first:
                        pe.wait_ge(sem["v_copied"], g("v_copied") + i)
                    token_tiles(2, lambda t: B(1, 256 + P * t, 384 + P * t), full_kv(2, i))

                def whole(i, first, prior):
                    proj_qk(i, first)
                    if prior is not None:
                        middle(prior)
                    proj_v(i, first)
                    if prior is not None:
                        values(prior)
                    if normed:
                        pe.wait_ge(sem["qk_sq"], g("qk_sq") + i + 1)
                        pe.matmul(B(2), C("halves"), sq2[:, :], start=True, stop=True).then_inc(sem["qk_ss"], 1)
                    if prior is not None:
                        if att == "da":
                            pe.wait_ge(sem["y_sq"], g("y_sq") + prior + 1)
                            pe.matmul(B(3, 0, 256), C("ones"), ysq[:, 0:256], start=True, stop=True)\
                                .then_inc(sem["y_ss"], 1)
                        pe.wait_ge(slot_full[3], 16 * (g("slot3") + prior + 1))
                        pe.wait_ge(sem["y_ready"], g("y_ready") + prior + 1)
                        add_out(3, y_sb[:, 0:256], range(4), free=False)
                    if normed:
                        pe.wait_ge(sem["qk_n"], g("qk_n") + i + 1)
                        pe.matmul(B(3), C("turn_da" if att == "da" else "turn"), qkn[:, :], start=True, stop=True)\
                            .then_inc(sem["qk_rot"], 1)
                    if prior is not None:
                        add_out(3, y_sb[:, 0:256], range(4, 8))
                    scores(i)

                whole(0, True, None)
                with pe.Fori(0, n - 1) as j:
                    whole(j + 1, False, j)
                last = n - 1
                middle(last)
                values(last)
                if att == "da":
                    pe.wait_ge(sem["y_sq"], g("y_sq") + last + 1)
                    pe.matmul(B(3, 0, 256), C("ones"), ysq[:, 0:256], start=True, stop=True).then_inc(sem["y_ss"], 1)
                pe.wait_ge(slot_full[3], 16 * (g("slot3") + last + 1))
                pe.wait_ge(sem["y_ready"], g("y_ready") + last + 1)
                add_out(3, y_sb[:, 0:256])

            for kind, at, ph in phases:
                g = lambda k: at.get(k, 0)
                full = lambda n: 16 * (g(f"slot{n}") + g(f"extra{n}") + 1)
                if kind == "norm":
                    for k in range(KT):
                        if k % 2 == 0:
                            pe.wait_ge(sem["squares"], g("squares") + k // 2 + 1)
                        mm = pe.matmul(B(0, 0, 256), C("ones"), sqT[:, k, :], start=(k == 0), stop=(k == KT - 1))
                    mm.then_inc(sem["sumsq"], 1)
                    clear_acc()
                elif kind == "att":
                    attention(ph, at, True)
                elif kind == "ssd":
                    for n in range(2):
                        mm = feature_tile(n, B(0, 256 * n, 256 * n + 256), full(n))

                    for n in range(2):
                        feature_tile(2 + n, B(1, 256 * n, 256 * n + 256), full(2 + n))

                    pe.wait_ge(slot_full[SLOT_SMALL], full(SLOT_SMALL))
                    for t in range(TT):
                        for k in range(KT):
                            mm = pe.matmul(B(3, 4 * t, 4 * t + 4), hT[:, k, P * t:P * t + P], wsmall[:, 0, 4 * k:4 * k + 4],
                                           start=(k == 0), stop=(k == KT - 1))
                    mm.then_inc(slot_used[SLOT_SMALL], 1)

                    for n in range(2):
                        feature_tile(4 + n, B(2, 256 * n, 256 * n + 256), full(4 + n))

                    pe.wait_ge(sem["ssd_da"], g("ssd_da") + 1)
                    da = dts[:, 7, :]
                    pe.matmul(B(3, 16, 24), C("upto"), da, start=True, stop=True)
                    for t in range(TT):
                        for h in range(4):
                            i = 4 * t + h
                            mm = pe.matmul(B(t, P * h, P * h + P), da[:, i:i + 1].broadcast_to([P, P]), C("upto"),
                                           start=True, stop=True)
                    mm.then_inc(sem["ssd_cum"], 1)
                    pe.wait_ge(sem["ssd_act"], g("ssd_act") + 1)
                    for t in range(TT):
                        for j in range(2):
                            mm = pe.transpose(B(2, 256 * t + P * j, 256 * t + P * j + P), xbc[:, j, P * t:P * t + P], ident)
                    mm.then_inc(sem["ssd_xtok"], 1)
                    pe.wait_ge(sem["ssd_cumc"], g("ssd_cumc") + 1)
                    pe.transpose(B(3, 128, 256), xbc[:, 2, 0:P], ident)
                    for t in range(TT):
                        mm = pe.matmul(B(3, 256 + P * t, 384 + P * t), xbc[:, 2, P * t:P * t + P], xbc[:, 3, P * t:P * t + P],
                                       start=True, stop=True)
                    mm.then_inc(sem["ssd_cb"], 1)
                    pe.wait_ge(sem["ssd_xe"], g("ssd_xe") + 1)
                    pe.matmul(B(3, 256, 512), b_tok[:, :], xe[:, :, :].rearrange("p h d -> p (h d)"), start=True, stop=True)\
                        .then_inc(sem["ssd_st"], 1)
                    pe.wait_ge(sem["ssd_m"], g("ssd_m") + 1)
                    pe.wait_ge(sem["ssd_stc"], g("ssd_stc") + 1)
                    for h in range(4):
                        j, r = h // 2, slice(64 * (h % 2), 64 * (h % 2) + 64)
                        for t in range(TT):
                            mm = pe.matmul(bank[r, 2, 256 * j + P * t:256 * j + P * t + P], xdt[:, t, h, :],
                                           mt[:, t, P * h:P * h + P], start=True, stop=(t == 0))
                        mm = pe.matmul(bank[r, 2, 256 * j + P:256 * j + 256], prev[:, 64 * h:64 * h + 64],
                                       ce[:, P * h:P * h + P], start=False, stop=True)
                    mm.then_inc(sem["ssd_y"], 1)
                    pe.wait_ge(sem["ssd_sq"], g("ssd_sq") + 1)
                    for j in range(2):
                        mm = pe.matmul(B(3, 0, 256), C("ones"), ysq[:, 256 * j:256 * j + 256], start=(j == 0), stop=(j == 1))
                    mm.then_inc(sem["ssd_ss"], 1)
                    pe.wait_ge(sem["ssd_yn"], g("ssd_yn") + 1)
                    for j in range(2):
                        pe.wait_ge(slot_full[6 + j], full(6 + j))
                        add_out(6 + j, y_sb[:, 256 * j:256 * j + 256])
                elif kind == "gla":
                    gg = ph["g"]
                    pe.wait_ge(slot_full[SLOT_SMALL + 1], full(SLOT_SMALL + 1))
                    for k in range(KT):
                        mm = pe.matmul(bank[0:16, 3, 0:256], wsmall[:, 1, 16 * k:16 * k + 16], hT[:, k, :],
                                       start=(k == 0), stop=(k == KT - 1))
                    mm.then_inc(slot_used[SLOT_SMALL + 1], 1)

                    for n in range(2):
                        feature_tile(n, B(0, 256 * n, 256 * n + 256), full(n))

                    pe.wait_ge(sem["gla_lr"], g("gla_lr") + 1)
                    pe.matmul(B(3, 256, 512), wg2[0:16, ph["layer"], P * gg:P * gg + P], qkc[0:16, 0:256],
                              start=True, stop=True).then_inc(sem["gla_pgk"], 1)
                    for n in range(2):
                        token_tiles(2 + n, lambda t: B(1, 256 * t + P * n, 256 * t + P * n + P), full(2 + n))

                    for n in range(2):
                        feature_tile(4 + n, B(2, 256 * n, 256 * n + 256), full(4 + n))

                    pe.wait_ge(sem["gla_kee"], g("gla_kee") + 1)
                    pe.wait_ge(sem["gla_ev"], g("gla_ev") + 1)
                    for t in range(TT):
                        mm = pe.transpose(B(2, P * t, P * t + P), qkc[:, P * t:P * t + P], ident)
                    mm.then_inc(sem["gla_tr"], 1)
                    pe.wait_ge(sem["gla_dec"], g("gla_dec") + 1)
                    for c in range(4):
                        t, r = c // 2, slice(64 * (c % 2), 64 * (c % 2) + 64)
                        for hh in range(2):
                            d = slice(64 * hh, 64 * hh + 64)
                            mm = pe.matmul(bank[r, hh, P * t + r.start:P * t + r.stop], qk[d, 256 + 64 * c:320 + 64 * c],
                                           qk[d, 64 * c:64 * c + 64], start=True, stop=True)
                    mm.then_inc(sem["gla_att"], 1)
                    pe.wait_ge(sem["gla_kt"], g("gla_kt") + 1)
                    for c in range(3):
                        t, r = c // 2, slice(64 * (c % 2), 64 * (c % 2) + 64)
                        for hh in range(2):
                            d = slice(64 * hh, 64 * hh + 64)
                            dst = bank[d, 3, 0:P] if c == 1 else bank[d, 2, 256 + 64 * c:384 + 64 * c]
                            mm = pe.matmul(dst, qkn[r, P * t + d.start:P * t + d.stop], v_sb[r, t, P * hh:P * hh + P],
                                           start=True, stop=True)
                    mm.then_inc(sem["gla_states"], 1)
                    pe.wait_ge(sem["gla_attm"], g("gla_attm") + 1)
                    pe.wait_ge(sem["gla_st"], g("gla_st") + 1)
                    st = st_sb
                    for hh in range(2):
                        d = slice(64 * hh, 64 * hh + 64)
                        for t in range(TT):
                            pe.matmul(bank[:, hh, 256 + P * t:384 + P * t], v_sb[:, t, P * hh:P * hh + P], attm[:, hh, P * t:P * t + P],
                                      start=True, stop=False)
                            for c in ((1,) if t == 0 else (2, 3)):
                                mm = pe.matmul(bank[:, hh, 256 + 64 * c:320 + 64 * c], st[d, P * (c - 1):P * c],
                                               qk[d, 64 * c:64 * c + 64], start=False, stop=(c != 2))
                    mm.then_inc(sem["gla_o"], 1)
                    pe.wait_ge(sem["gla_sq"], g("gla_sq") + 1)
                    pe.matmul(B(2), C("ones"), ysq[:, :], start=True, stop=True).then_inc(sem["gla_ss"], 1)
                    pe.wait_ge(sem["gla_yn"], g("gla_yn") + 1)
                    for j in range(2):
                        pe.wait_ge(slot_full[6 + j], full(6 + j))
                        add_out(6 + j, y_sb[:, 256 * j:256 * j + 256])
                elif kind == "ffn":
                    ada = ph["ada"]

                    def up(f, b, i, first=False):
                        if not first:
                            pe.wait_ge(sem["mid_ready"], g("mid_ready") + f - 1)
                        s = SLOT_FF + 3 * b
                        feature_tile(s, B(b, 0, 256), 16 * (g(f"slot{s}") + i + 1), g("h_ready") - 8 if first else None)
                        feature_tile(s + 1, B(b, 256, 512), 16 * (g(f"slot{s + 1}") + i + 1))


                    def down(f, b, i):
                        s = SLOT_FF + 3 * b + 2
                        pe.wait_ge(slot_full[s], 16 * (g(f"slot{s}") + i + 1))
                        pe.wait_ge(sem["mid_ready"], g("mid_ready") + f + 1)
                        add_out(s, mid[:, b, :])

                    up(0, 0, 0, first=True)
                    with pe.Fori(0, NF // 2 - 1) as i:
                        s = SLOT_FF + 3
                        feature_tile(s, B(1, 0, 256), 16 * (g(f"slot{s}") + i + 1))
                        feature_tile(s + 1, B(1, 256, 512), 16 * (g(f"slot{s + 1}") + i + 1))

                        down(2 * i, 0, i)
                        up(2 * i + 2, 0, i + 1)
                        down(2 * i + 1, 1, i)
                    last = NF // 2 - 1
                    up(NF - 1, 1, last)
                    down(NF - 2, 0, last)
                    down(NF - 1, 1, last)
                    if ada is not None:
                        pe.wait_ge(sem["ada_rows"], g("ada_rows") + 1)
                        for m in range(ADA_TILES):
                            mm = pe.matmul(B(3, m, m + 1), ada_rows[:, m, :], C("ones", 0, 1), start=True, stop=True)
                        mm.then_inc(sem["ada_sums"], 1)

                elif kind == "ple":
                    l = ph["layer"]
                    pe.wait_ge(p_loaded, 16 * (l + 1))
                    for kk in range(2):
                        for t in range(TT):
                            mm = pe.transpose(B(2, 256 * kk + P * t, 256 * kk + P * t + P), x_rows[:, t, P * kk:P * kk + P], ident)
                    mm.then_inc(sem["ple_t"], 1)
                    pe.wait_ge(sem["x_ready"], g("x_ready"))
                    pe.wait_ge(sem["ple_tc"], g("ple_tc") + 1)

                    def ple_tile(i, b, reused):
                        if reused:
                            pe.wait_ge(sem["ple_d"], 2 * i + (g("ple_d") + b - 1))
                        s = SLOT_MIX + 4 + b
                        pe.wait_ge(slot_full[s], 16 * (g(f"slot{s}") + i + 1))
                        for k in range(KT):
                            mm = pe.matmul(B(2 * b, 0, 256), wk(s, k), xT[:, k, :], start=(k == 0),
                                           stop=(k == KT - 1))
                        mm.then_inc(slot_used[s], 1)
                        s = SLOT_SMALL + 2 + b
                        pe.wait_ge(slot_full[s], 16 * (g(f"slot{s}") + i + 1))
                        for k in range(2):
                            mm = pe.matmul(B(2 * b + 1, 0, 256), wsmall[:, 2 + b, P * k:P * k + P],
                                           qk[:, 256 * k:256 * k + 256], start=(k == 0), stop=(k == 1))
                        mm.then_inc(slot_used[s], 1)

                    for b in range(2):
                        ple_tile(0, b, False)
                    with pe.Fori(1, KT // 2) as i:
                        for b in range(2):
                            ple_tile(i, b, True)
                elif kind == "store":
                    pe.wait_ge(sem["x_ready"], g("x_ready"))
                    for t in range(TT):
                        for m in range(KT):
                            mm = pe.transpose(acc[:, 4 * t + m // 2, P * (m % 2):P * (m % 2) + P], xT[:, m, P * t:P * t + P], ident)
                    mm.then_inc(x_turned, 1)

        @block.scalar
        def _(act):
            act.dma_start(x_rows[:, :, :], a["x"][0].rearrange("(t p) d -> p t d", p=P)).then_inc(x_loaded, 16)
            act.dma_start(const[:, :], table_dram).then_inc(x_loaded, 16)
            for dst, src in loads:
                act.dma_start(dst, src).then_inc(loaded, 16)

            def copy(dst, src):
                return act.activation(dst, src, ACT.Copy)

            def inverse_root(dst, src, n):
                act.activation(dst, src, ACT.Ln, scale=1.0 / n, bias=epst[:, 0:1])
                act.drain()
                return act.activation(dst, dst, ACT.Exp, scale=-0.5)

            def log_one_plus_exp(tmp, src, scale=1.0):
                act.activation(tmp, src, ACT.Abs, scale=scale)
                act.drain()
                act.activation(tmp, tmp, ACT.Exp, scale=-1.0)
                act.drain()
                return act.activation(tmp, tmp, ACT.Ln, bias=1.0)

            def load_p(l):
                act.dma_start(x_rows[:, :, 0:256], a["p"][l, 0].rearrange("(t p) d -> p t d", p=P)).then_inc(p_loaded, 16)

            LN_EXP = "natural_log_exp_and_others"
            act.preload_act_table_set(LN_EXP)
            act.wait_ge(small_ready, 1)
            act.activation(lam[:, :, 2:4], lam[:, :, 0:2], ACT.Exp)
            act.activation(a_neg[:, :, :], a_log[:, :, :], ACT.Exp).then_inc(small_exp, 1)
            act.wait_ge(rope_ready, 1)
            act.activation(sin1[:, :], turns[:, :], ACT.Sin)
            act.activation(cos1[:, :], ang2[:, :], ACT.Sin).then_inc(rope_ready, 1)
            act.wait_ge(params_ready, 1)
            act.activation(c_act[:, :], pcol[:, 0, C_ROW:SSD_G], ACT.Silu).then_inc(cact_ready, 1)
            act.wait_ge(x_turned, 1)
            load_p(0)

            def attention(ph, at):
                att, n = ph["att"], ph["n"]
                g = lambda k: at.get(k, 0)
                heads = 1 if att == "da" else 2

                def whole(i, prior):
                    if i is not None:
                        act.wait_ge(slot_used[1], g("slot1") + i + 2)
                        if att == "sb":
                            copy(qk[:, :], B(0)).then_inc(sem["qk_ready"], 1)
                        else:
                            act.activation(sq2[:, :], B(0), ACT.Square).then_inc(sem["qk_sq"], 1)
                    if prior is not None:
                        for hh in range(heads):
                            if att == "sb":
                                act.wait_ge(sem["sb_la"], g("sb_la") + 2 * prior + hh + 1)
                                act.activation(pt[:, hh, :], pr[:, hh, :], ACT.Exp).then_inc(sem["sb_exp"], 1)
                            else:
                                act.wait_ge(sem["p_tr"], g("p_tr") + heads * prior + hh + 1)
                                copy(pt[:, hh, :], bank[:, 2 + hh, 0:384]).then_inc(sem["pt_ready"], 1)
                        act.wait_ge(sem["pv_done"], g("pv_done") + prior + 1)
                    if i is not None:
                        act.wait_ge(slot_used[2], g("slot2") + i + 2)
                        copy(v_sb[:, :, 0:P], B(1, 256, 512).rearrange("p (t d) -> p t d", t=TT)).then_inc(sem["v_copied"], 1)
                    if prior is not None:
                        if att == "da":
                            act.activation(ysq[:, 0:256], B(1, 0, 256), ACT.Square).then_inc(sem["y_sq"], 1)
                        else:
                            copy(y_sb[:, 0:256], B(1, 0, 256)).then_inc(sem["y_ready"], 1)
                    if i is not None and att != "sb":
                        act.wait_ge(sem["qk_ss"], g("qk_ss") + i + 1)
                        inverse_root(rs2[:, :], B(2), 64).then_inc(sem["qk_rs"], 1)
                    if prior is not None and att == "da":
                        act.wait_ge(sem["y_ss"], g("y_ss") + prior + 1)
                        inverse_root(rs[:, :], B(3, 0, 256), P).then_inc(sem["y_rs"], 1)
                    if i is None:
                        return
                    for hh in range(2):
                        if att == "sb":
                            act.wait_ge(sem["s_read"], g("s_read") + 2 * i + hh + 1)
                            log_one_plus_exp(pr[:, hh, :], lb[:, hh, :]).then_inc(sem["sb_log"], 1)
                        else:
                            act.wait_ge(sem["negmax"], g("negmax") + 2 * i + hh + 1)
                            act.activation(pr[:, hh, 0:128], sm[:, hh, 0:128], ACT.Exp, bias=nmx[:, 2 * hh:2 * hh + 1],
                                           accum_out=sums[:, 2 * hh:2 * hh + 1])
                            if att == "swa":
                                act.activation(esink[:, 2 * hh:2 * hh + 2], nmx[:, 2 * hh:2 * hh + 2], ACT.Exp,
                                               bias=sink_now[:, hh:hh + 1])
                            act.activation(pr[:, hh, 128:384], sm[:, hh, 128:384], ACT.Exp,
                                           bias=nmx[:, 2 * hh + 1:2 * hh + 2],
                                           accum_out=sums[:, 2 * hh + 1:2 * hh + 2]).then_inc(sem["exps"], 1)

                whole(0, None)
                with act.Fori(0, n - 1) as j:
                    whole(j + 1, j)
                whole(None, n - 1)

            for kind, at, ph in phases:
                g = lambda k: at.get(k, 0)
                if kind == "norm":
                    act.preload_act_table_set(LN_EXP)
                    for q in range(4):
                        act.wait_ge(sem["x_ready"], g("x_ready") - 3 + q)
                        act.activation(sqT[:, 2 * q:2 * q + 2, :], xT[:, 2 * q:2 * q + 2, :], ACT.Square)\
                           .then_inc(sem["squares"], 1)
                    act.wait_ge(sem["sumsq"], g("sumsq") + 1)
                    inverse_root(rs[:, :], B(0, 0, 256), D).then_inc(sem["rstd"], 1)
                elif kind == "att":
                    attention(ph, at)
                elif kind == "ssd":
                    act.wait_ge(sem["ssd_u"], g("ssd_u") + 1)
                    act.activation(dts[:, 1, :], dts[:, 0, :], ACT.Abs)
                    act.drain()
                    act.activation(dts[:, 2, :], dts[:, 1, :], ACT.Exp, scale=-1.0)
                    act.drain()
                    act.activation(dts[:, 3, :], dts[:, 2, :], ACT.Ln, bias=1.0).then_inc(sem["ssd_ln"], 1)
                    act.wait_ge(sem["ssd_conv"], g("ssd_conv") + 1)
                    act.activation(xbc[:, :, :], conv[:, :, :], ACT.Silu)
                    act.wait_ge(slot_used[5], g("slot5") + 2)
                    act.activation(z_sb[:, :, :], B(2).rearrange("p (j s) -> p j s", j=2), ACT.Silu).then_inc(sem["ssd_act"], 1)
                    act.preload_act_table_set(LN_EXP)
                    act.wait_ge(sem["ssd_dif"], g("ssd_dif") + 1)
                    act.activation(wexp[:, :], wend[:, :], ACT.Exp)
                    act.activation(dif[:, 0, :], dif[:, 0, :], ACT.Exp).then_inc(sem["ssd_dec"], 1)
                    act.wait_ge(sem["ssd_dif"], g("ssd_dif") + 2)
                    act.activation(dif[:, 1, :], dif[:, 1, :], ACT.Exp)
                    act.activation(ce[:, :], B(1), ACT.Exp).then_inc(sem["ssd_dec"], 1)
                    act.wait_ge(sem["ssd_yg"], g("ssd_yg") + 1)
                    act.activation(ysq[:, :], y_sb[:, :], ACT.Square).then_inc(sem["ssd_sq"], 1)
                    act.wait_ge(sem["ssd_ss"], g("ssd_ss") + 1)
                    inverse_root(rs[:, :], B(3, 0, 256), 256).then_inc(sem["ssd_rs"], 1)
                elif kind == "gla":
                    act.wait_ge(slot_used[SLOT_SMALL + 1], g(f"slot{SLOT_SMALL + 1}") + 2)
                    copy(qkc[0:16, 0:256], bank[0:16, 3, 0:256]).then_inc(sem["gla_lr"], 1)
                    act.wait_ge(sem["gla_u"], g("gla_u") + 1)
                    log_one_plus_exp(sm[:, 1, 0:256], sm[:, 0, 0:256]).then_inc(sem["gla_ls"], 1)
                    act.wait_ge(sem["gla_scan"], g("gla_scan") + 1)
                    act.activation(sq2[:, 0:256], rs2[:, 0:256], ACT.Exp, scale=1.0 / 16)
                    act.activation(sq2[:, 256:512], rs2[:, 0:256], ACT.Exp, scale=-1.0 / 16)
                    act.wait_ge(sem["gla_ked"], g("gla_ked") + 1)
                    act.activation(qkn[:, 256:512], rs2[:, 256:512], ACT.Exp, scale=1.0 / 16).then_inc(sem["gla_e"], 1)
                    act.wait_ge(slot_used[3], g("slot3") + 2)
                    copy(v_sb[:, :, :], B(1).rearrange("p (t d) -> p t d", t=TT))
                    act.wait_ge(slot_used[5], g("slot5") + 2)
                    act.activation(silu_g[:, :, :], B(2).rearrange("p (j s) -> p j s", j=2), ACT.Silu).then_inc(sem["gla_ev"], 1)
                    act.preload_act_table_set(LN_EXP)
                    act.wait_ge(sem["gla_o"], g("gla_o") + 1)
                    act.activation(ysq[:, :].rearrange("p (j s) -> p j s", j=2), bank[:, 0:2, 256:512], ACT.Square)\
                       .then_inc(sem["gla_sq"], 1)
                    act.wait_ge(sem["gla_ss"], g("gla_ss") + 1)
                    inverse_root(rs2[:, :], B(2), P).then_inc(sem["gla_rs"], 1)
                elif kind == "ffn":
                    act.preload_act_table(ACT.Silu)
                    with act.Fori(0, NF // 2) as i:
                        for b in range(2):
                            s = SLOT_FF + 3 * b + 1
                            act.wait_ge(slot_used[s], g(f"slot{s}") + i + 2)
                            act.activation(silu_g[:, b, :], B(b, 0, 256), ACT.Silu).then_inc(sem["silu_ready"], 1)
                elif kind == "ple":
                    act.wait_ge(sem["ple_t"], g("ple_t") + 1)
                    if ph["layer"] + 1 < DEPTH:
                        load_p(ph["layer"] + 1)
                    copy(qk[:, :], B(2)).then_inc(sem["ple_tc"], 1)
                    act.preload_act_table(ACT.Sigmoid)
                    with act.Fori(0, KT // 2) as i:
                        for b in range(2):
                            s = SLOT_MIX + 4 + b
                            act.wait_ge(slot_used[s], g(f"slot{s}") + i + 2)
                            act.activation(silu_g[:, b, :], B(2 * b, 0, 256), ACT.Sigmoid)\
                               .then_inc(sem["ple_s"], 1)

        @block.vector
        def _(dve):
            def stt(out, x, scalar, y, op0=ALU.mult, op1=ALU.mult):
                return dve.scalar_tensor_tensor(out=out, in0=x, scalar=scalar, in1=y, op0=op0, op1=op1)

            dve.memset(zero[:, :], 0.0)
            dve.memset(epst[:, :], EPS)
            dve.memset(attm[:, :, :], 0.0).then_inc(consts_ready, 1)
            dve.wait_ge(x_turned, 1)
            for q in range(4):
                dve.tensor_copy(xT[:, 2 * q:2 * q + 2, :], acc[:, 2 * q:2 * q + 2, :]).then_inc(sem["x_ready"], 1)
            dve.wait_ge(params_turned, 1)
            for n, r in enumerate((P, N_B, 96, 96)):
                last = dve.tensor_copy(pcol[:, n, 0:r], B(0, P * n, P * n + r))
            last.then_inc(params_ready, 1)
            dve.wait_ge(loaded, 16 * len(loads))
            dve.tensor_tensor(lam_tmp[:, :, :, :], lam_in[:, :, 0::2, :], lam_in[:, :, 1::2, :], ALU.mult)
            dve.drain()
            dve.tensor_reduce(lam[:, :, 0:2], lam_tmp[:, :, :, :], AX, ALU.add).then_inc(small_ready, 1)
            dve.wait_ge(small_exp, 1)
            for l in range(DEPTH):
                init = 0.8 - 0.6 * math.exp(-0.3 * l)
                stt(neg_lam[:, l:l + 1], lam[:, l, 3:4], init, lam[:, l, 2:3], ALU.subtract, ALU.subtract)
                dve.tensor_scalar(da_gain[:, l:l + 1], pcol[:, 1, DA_SUB + l:DA_SUB + l + 1], 1.0 - init, None, ALU.mult)
            dve.tensor_scalar(a_neg[:, :, :], a_neg[:, :, :], -1.0, None, ALU.mult)
            for half in range(2):
                r = slice(64 * half, 64 * half + 64)
                dve.tensor_copy(skip[r, :, :], skip_all[r, :, half::2])
            dve.tensor_copy(ang[:, :], pos_i[:, :])
            dve.drain()
            dve.tensor_scalar(ang[:, :], ang[:, :], C("inv"), None, ALU.mult)
            dve.drain()
            for quarter, dst in ((0.0, turns), (0.25, ang2)):
                whole = rs
                dve.tensor_scalar(whole[:, :], ang[:, :], 0.5 / math.pi, quarter, ALU.mult, ALU.add)
                dve.drain()
                dve.tensor_scalar(whole[:, :], whole[:, :], 12582912.0, None, ALU.add)
                dve.drain()
                dve.tensor_scalar(whole[:, :], whole[:, :], -12582912.0, None, ALU.add)
                dve.drain()
                stt(dst[:, :], whole[:, :], -TWO_PI_PARTS[0], ang[:, :], ALU.mult, ALU.add)
                for part in TWO_PI_PARTS[1:]:
                    dve.drain()
                    stt(dst[:, :], whole[:, :], -part, dst[:, :], ALU.mult, ALU.add)
                dve.drain()
                dve.tensor_scalar(dst[:, :], dst[:, :], 2 * math.pi * quarter, 3.1415925, ALU.add, ALU.min)
                dve.drain()
                last = dve.tensor_scalar(dst[:, :], dst[:, :], -3.1415925, None, ALU.max)
            last.then_inc(rope_ready, 1)
            dve.wait_ge(rope_ready, 2)

            def attention(ph, at):
                att, n, l = ph["att"], ph["n"], ph["layer"]
                g = lambda k: at.get(k, 0)
                if att != "sb":
                    gains = qk_gains(att, l)
                    cos, sin = (cos1[:, :], sin1[:, :]) if att == "da" else (C("cos2"), C("sin2"))
                    mask = C("window") if att == "swa" else C("causal")

                def end_softmax(i):
                    if att == "sb":
                        for hh in range(2):
                            dve.wait_ge(sem["sb_later"], g("sb_later") + 2 * i + hh + 1)
                            dve.tensor_tensor(pr[:, hh, :], lb[:, hh, :], bank[:, 2 + hh, 0:384], ALU.subtract)\
                               .then_inc(sem["sb_la"], 1)
                        for hh in range(2):
                            dve.wait_ge(sem["sb_exp"], g("sb_exp") + 2 * i + hh + 1)
                            dve.tensor_tensor(pt[:, hh, :], pt[:, hh, :], C("past"), ALU.mult).then_inc(sem["pt_ready"], 1)
                        return
                    dve.wait_ge(sem["exps"], g("exps") + 2 * i + 2)
                    if att == "swa":
                        dve.tensor_tensor(sums[:, :], sums[:, :], esink[:, :], ALU.add)
                        dve.drain()
                    dve.reciprocal(rinv[:, :], sums[:, :])
                    dve.drain()
                    if att == "da":
                        dve.tensor_scalar(rinv[:, 2:4], rinv[:, 2:4], neg_lam[:, l:l + 1], None, ALU.mult)
                    for hh in range(1 if att == "da" else 2):
                        dve.tensor_scalar(pr[:, hh, 0:128], pr[:, hh, 0:128], rinv[:, 2 * hh:2 * hh + 1], None, ALU.mult)
                        last = dve.tensor_scalar(pr[:, hh, 128:384], pr[:, hh, 128:384], rinv[:, 2 * hh + 1:2 * hh + 2],
                                                 None, ALU.mult)
                        if att != "da":
                            last.then_inc(sem["p_ready"], 1)
                    if att == "da":
                        dve.drain()
                        stt(pr[:, 0, 0:128], pr[:, 1, 0:128], rinv[:, 2:3], pr[:, 0, 0:128], ALU.mult, ALU.add)
                        stt(pr[:, 0, 128:384], pr[:, 1, 128:384], rinv[:, 3:4], pr[:, 0, 128:384], ALU.mult, ALU.add)\
                            .then_inc(sem["p_ready"], 1)

                def end_da(i):
                    dve.wait_ge(sem["y_rs"], g("y_rs") + i + 1)
                    stt(y_sb[:, 0:256], B(1, 0, 256), da_gain[:, l:l + 1], rs[:, :]).then_inc(sem["y_ready"], 1)

                def whole(i, prior):
                    if prior is not None:
                        end_softmax(prior)
                    if i is not None and att != "sb":
                        dve.wait_ge(sem["qk_rs"], g("qk_rs") + i + 1)
                        stt(qkn[:, 0:256], B(0, 0, 256), gains[0], rs2[:, 0:256])
                        stt(qkn[:, 256:512], B(0, 256, 512), gains[1], rs2[:, 256:512]).then_inc(sem["qk_n"], 1)
                    if prior is not None and att == "da":
                        end_da(prior)
                    if i is None:
                        return
                    if att == "sb":
                        for hh in range(2):
                            z = bank[:, 2 + hh, 0:384]
                            dve.wait_ge(sem["scores"], g("scores") + 2 * i + hh + 1)
                            dve.tensor_scalar(lb[:, hh, :], z, HEAD_SCALE, None, ALU.mult).then_inc(sem["s_read"], 1)
                        dve.drain()
                        for hh in range(2):
                            dve.tensor_scalar(sm[:, hh, :], lb[:, hh, :], 0.0, None, ALU.max)
                        dve.drain()
                        for hh in range(2):
                            dve.wait_ge(sem["sb_log"], g("sb_log") + 2 * i + hh + 1)
                            dve.tensor_tensor(sm[:, hh, :], sm[:, hh, :], pr[:, hh, :], ALU.add)
                            dve.drain()
                            dve.tensor_tensor(lb[:, hh, :], lb[:, hh, :], sm[:, hh, :], ALU.subtract)
                            dve.tensor_tensor(sm[:, hh, :], sm[:, hh, :], C("past"), ALU.mult).then_inc(sem["sb_spm"], 1)
                        return
                    dve.drain()
                    two = lambda ap: ap.rearrange("p (a s) -> p a s", a=2)
                    dve.tensor_tensor(two(qkc[:, :]), two(qkn[:, :]), per_tile(cos, 2), ALU.mult)
                    dve.wait_ge(sem["qk_rot"], g("qk_rot") + i + 1)
                    dve.tensor_tensor(two(qk[:, :]), two(B(3)), per_tile(sin, 2), ALU.mult)
                    dve.drain()
                    dve.tensor_tensor(qk[:, :], qk[:, :], qkc[:, :], ALU.add).then_inc(sem["qk_ready"], 1)
                    if att == "swa":
                        dve.tensor_copy(sink_now[:, :], sinks[:, bass.ds(2 * i, 2)])
                    for hh in range(2):
                        dve.wait_ge(sem["scores"], g("scores") + 2 * i + hh + 1)
                        stt(sm[:, hh, :], bank[:, 2 + hh, 0:384], HEAD_SCALE, mask, ALU.mult, ALU.add)
                        dve.drain()
                        dve.reduce_max(mx[:, 2 * hh:2 * hh + 1], sm[:, hh, 0:128], AX)
                        dve.reduce_max(mx[:, 2 * hh + 1:2 * hh + 2], sm[:, hh, 128:384], AX)
                        dve.drain()
                        if att == "swa":
                            dve.tensor_scalar(nmx[:, 2 * hh:2 * hh + 2], mx[:, 2 * hh:2 * hh + 2], sink_now[:, hh:hh + 1],
                                              -1.0, ALU.max, ALU.mult).then_inc(sem["negmax"], 1)
                        else:
                            dve.tensor_scalar(nmx[:, 2 * hh:2 * hh + 2], mx[:, 2 * hh:2 * hh + 2], -1.0, None,
                                              ALU.mult).then_inc(sem["negmax"], 1)

                whole(0, None)
                with dve.Fori(0, n - 1) as j:
                    whole(j + 1, j)
                whole(None, n - 1)

            for kind, at, ph in phases:
                g = lambda k: at.get(k, 0)
                if kind == "norm":
                    gain = ph["gain"]
                    w = gain_of(gain)
                    dve.wait_ge(sem["rstd"], g("rstd") + 1)
                    shifted = gain[0] == "two"
                    for k in range(KT):
                        ins = stt((sqT if shifted else hT)[:, k, :], xT[:, k, :], w[:, k:k + 1], rs[:, :])
                        if not shifted:
                            ins.then_inc(sem["h_ready"], 1)
                    if shifted:
                        dve.drain()
                        for k in range(KT):
                            c = 24 * gain[2] + k
                            dve.tensor_scalar(hT[:, k, :], sqT[:, k, :], mod[:, gain[1], c:c + 1], None, ALU.add)\
                               .then_inc(sem["h_ready"], 1)
                elif kind == "att":
                    attention(ph, at)
                elif kind == "ssd":
                    l, gr = ph["layer"], ph["g"]
                    tile_of = (2 * gr, 2 * gr + 1, 4 + gr, 6 + gr)
                    wcol = lambda w, j: pcol[:, 1, 32 * l + 8 * w + tile_of[j]:32 * l + 8 * w + tile_of[j] + 1]
                    for half in range(2):
                        dve.wait_ge(slot_used[1 + 2 * half], g(f"slot{1 + 2 * half}") + 2)
                        for w in range(3, -1, -1):
                            for j in (2 * half, 2 * half + 1):
                                src = B(half, 256 * (j % 2), 256 * (j % 2) + 256)
                                if w == 3:
                                    cb = CONV_B + 8 * l + tile_of[j]
                                    last = dve.tensor_scalar(conv[:, j, :], src, wcol(3, j), pcol[:, 0, cb:cb + 1], ALU.mult, ALU.add)
                                else:
                                    lag = 3 - w
                                    last = stt(conv[:, j, lag:S], src[:, 0:S - lag], wcol(w, j), conv[:, j, lag:S], ALU.mult, ALU.add)
                            if w:
                                dve.drain()
                    last.then_inc(sem["ssd_conv"], 1)
                    u, ab, e, ln, m, dt, lost, da = (dts[:, n, :] for n in range(8))
                    dve.wait_ge(slot_used[SLOT_SMALL], g(f"slot{SLOT_SMALL}") + 2)
                    halves4 = lambda ap: ap.rearrange("p (t h) -> p t h", t=TT)
                    dve.tensor_tensor(halves4(u), halves4(B(3, 0, 8)), per_tile(dt_bias[:, l, 4 * gr:4 * gr + 4], 2), ALU.add)\
                       .then_inc(sem["ssd_u"], 1)
                    dve.drain()
                    dve.tensor_scalar(m, u, 0.0, None, ALU.max)
                    dve.wait_ge(sem["ssd_ln"], g("ssd_ln") + 1)
                    dve.tensor_scalar(dt, e, 1.0, None, ALU.add)
                    dve.drain()
                    stt(lost, dt, 1.0, e, ALU.subtract, ALU.subtract)
                    dve.reciprocal(ab, dt)
                    dve.tensor_tensor(m, m, ln, ALU.add)
                    dve.drain()
                    dve.tensor_tensor(lost, lost, ab, ALU.mult)
                    dve.drain()
                    dve.tensor_tensor(dt, m, lost, ALU.subtract)
                    dve.drain()
                    dve.tensor_tensor(halves4(da), halves4(dt), per_tile(a_neg[:, l, 4 * gr:4 * gr + 4], 2), ALU.mult)\
                       .then_inc(sem["ssd_da"], 1)
                    dve.wait_ge(sem["ssd_cum"], g("ssd_cum") + 1)
                    dve.tensor_copy(cum[:, :], B(3, 16, 24)).then_inc(sem["ssd_cumc"], 1)
                    dve.drain()
                    dve.tensor_tensor(wend[:, :].unsqueeze(2), B(0).rearrange("p (h s) -> p h s", h=4)[:, :, P - 1:P],
                                      cum[:, 0:4].unsqueeze(2), ALU.subtract)
                    for t in range(TT):
                        for h in range(4):
                            last = dve.tensor_scalar(dif[:, t, P * h:P * h + P], B(t, P * h, P * h + P),
                                                     cum[:, 4 * t + h:4 * t + h + 1], 0.0, ALU.subtract, ALU.min)
                        last.then_inc(sem["ssd_dif"], 1)
                    dve.wait_ge(sem["ssd_xtok"], g("ssd_xtok") + 1)
                    for t in range(TT):
                        dve.tensor_tensor(xdt[:, t, :, :], B(2, 256 * t, 256 * t + 256).rearrange("p (h d) -> p h d", h=4),
                                          per_head(dt[:, 4 * t:4 * t + 4], 64), ALU.mult)
                    dve.wait_ge(sem["ssd_dec"], g("ssd_dec") + 1)
                    dve.drain()
                    dve.tensor_tensor(xe[:, :, :], xdt[:, 0, :, :], per_head(wexp[:, :], 64), ALU.mult)
                    dve.wait_ge(sem["ssd_cb"], g("ssd_cb") + 1)
                    dve.tensor_copy(b_tok[:, :], B(3, 128, 256))
                    dve.tensor_tensor(cbm[:, :, :], B(3, 256, 512).rearrange("p (t s) -> p t s", t=TT),
                                      per_tile(C("upto"), TT), ALU.mult).then_inc(sem["ssd_xe"], 1)
                    dve.drain()
                    four = lambda ap: ap.rearrange("p (h s) -> p h s", h=4)
                    dve.tensor_tensor(four(mt[:, 0, :]), four(dif[:, 0, :]), per_tile(cbm[:, 0, :], 4), ALU.mult)
                    dve.wait_ge(sem["ssd_dec"], g("ssd_dec") + 2)
                    dve.tensor_tensor(four(mt[:, 1, :]), four(dif[:, 1, :]), per_tile(cbm[:, 1, :], 4), ALU.mult)
                    dve.tensor_tensor(four(ce[:, :]), four(ce[:, :]), per_tile(xbc[:, 3, P:S], 4), ALU.mult)\
                       .then_inc(sem["ssd_m"], 1)
                    dve.wait_ge(sem["ssd_st"], g("ssd_st") + 1)
                    dve.tensor_copy(prev[:, :], B(3, 256, 512)).then_inc(sem["ssd_stc"], 1)
                    dve.wait_ge(sem["ssd_y"], g("ssd_y") + 1)
                    for j in range(2):
                        c = 2 * gr + j
                        stt(y_sb[:, 256 * j:256 * j + 256], xbc[:, j, :], skip[:, l, c:c + 1], B(2, 256 * j, 256 * j + 256),
                            ALU.mult, ALU.add)
                    dve.drain()
                    dve.tensor_tensor(y_sb[:, :], y_sb[:, :], z_sb[:, :, :].rearrange("p j s -> p (j s)"), ALU.mult)\
                       .then_inc(sem["ssd_yg"], 1)
                    dve.wait_ge(sem["ssd_rs"], g("ssd_rs") + 1)
                    for j in range(2):
                        c = SSD_G + 4 * l + 2 * gr + j
                        y = y_sb[:, 256 * j:256 * j + 256]
                        last = stt(y, y, pcol[:, 0, c:c + 1], rs[:, :])
                    last.then_inc(sem["ssd_yn"], 1)
                elif kind == "gla":
                    l, gr = ph["layer"], ph["g"]
                    u, m, ls, bc = sm[:, 0, 0:256], pr[:, 0, 0:256], pr[:, 1, 0:256], rs2[:, 0:256]
                    dve.wait_ge(sem["gla_pgk"], g("gla_pgk") + 1)
                    c = B_GATE + 2 * l + gr
                    dve.tensor_scalar(u, B(3, 256, 512), pcol[:, 1, c:c + 1], None, ALU.add).then_inc(sem["gla_u"], 1)
                    dve.drain()
                    dve.tensor_scalar(m, u, 0.0, None, ALU.min)
                    dve.drain()
                    dve.wait_ge(sem["gla_ls"], g("gla_ls") + 1)
                    dve.tensor_tensor(ls, m, sm[:, 1, 0:256], ALU.subtract)
                    dve.drain()
                    dve.tensor_tensor_scan(bc, C("keep"), ls, 0.0, ALU.mult, ALU.add).then_inc(sem["gla_scan"], 1)
                    dve.drain()
                    chunks = lambda ap: ap.rearrange("p (c s) -> p c s", c=4)
                    dve.tensor_tensor(chunks(rs2[:, 256:512]), chunks(bc)[:, :, 63:64].broadcast_to([P, 4, 64]), chunks(bc),
                                      ALU.subtract).then_inc(sem["gla_ked"], 1)
                    dve.wait_ge(sem["gla_e"], g("gla_e") + 1)
                    dve.wait_ge(slot_used[1], g("slot1") + 2)
                    stt(qk[:, 0:256], B(0, 0, 256), HEAD_SCALE, sq2[:, 0:256])
                    dve.tensor_tensor(qk[:, 256:512], B(0, 256, 512), sq2[:, 256:512], ALU.mult).then_inc(sem["gla_dec"], 1)
                    dve.tensor_tensor(qkc[:, 0:256], B(0, 256, 512), qkn[:, 256:512], ALU.mult).then_inc(sem["gla_kee"], 1)
                    dve.wait_ge(sem["gla_tr"], g("gla_tr") + 1)
                    dve.tensor_copy(qkn[:, 0:256], B(2, 0, 256)).then_inc(sem["gla_kt"], 1)
                    dve.wait_ge(sem["gla_att"], g("gla_att") + 1)
                    for r in (0, 64):
                        view = lambda ap: ap[r:r + 64].rearrange("p h (t s) -> p h t s", t=TT)[:, :, :, r:r + 64]
                        tri = C("tri64")[r:r + 64].unsqueeze(1).unsqueeze(1).broadcast_to([64, 2, TT, 64])
                        last = dve.tensor_tensor(view(attm[:, :, :]), view(bank[:, 0:2, 0:256]), tri, ALU.mult)
                    last.then_inc(sem["gla_attm"], 1)
                    dve.wait_ge(sem["gla_states"], g("gla_states") + 1)
                    dve.tensor_copy(st_sb[:, 0:128], B(2, 256, 384))
                    dve.drain()
                    stt(st_sb[:, 128:256], st_sb[:, 0:128], sq2[:, 127:128], B(3, 0, 128), ALU.mult, ALU.add)
                    dve.drain()
                    stt(st_sb[:, 256:384], st_sb[:, 128:256], sq2[:, 191:192], B(2, 384, 512), ALU.mult, ALU.add)\
                        .then_inc(sem["gla_st"], 1)
                    dve.wait_ge(sem["gla_rs"], g("gla_rs") + 1)
                    two = lambda ap: ap.rearrange("p (a s) -> p a s", a=2)
                    stt(two(y_sb[:, :]), bank[:, 0:2, 256:512], pcol[:, 1, GLA_G + l:GLA_G + l + 1], two(rs2[:, :]))
                    dve.drain()
                    dve.tensor_tensor(two(y_sb[:, :]), two(y_sb[:, :]), silu_g[:, :, :], ALU.mult).then_inc(sem["gla_yn"], 1)
                elif kind == "add":
                    s = ph["last_slot"]
                    dve.wait_ge(slot_used[s], g(f"slot{s}") + 1)
                    for q in range(4):
                        if ph["gate"] is None:
                            last = dve.tensor_tensor(xT[:, 2 * q:2 * q + 2, :], xT[:, 2 * q:2 * q + 2, :],
                                                     acc[:, 2 * q:2 * q + 2, :], ALU.add)
                        else:
                            l, part = ph["gate"]
                            for m in (2 * q, 2 * q + 1):
                                last = stt(xT[:, m, :], acc[:, m, :], mod[:, l, 8 * part + m:8 * part + m + 1], xT[:, m, :],
                                           ALU.mult, ALU.add)
                        last.then_inc(sem["x_ready"], 1)
                elif kind == "ffn":
                    ada = ph["ada"]

                    def ada_tile(i, n):
                        s = SLOT_ADA + n
                        dve.wait_ge(slot_full[s], 16 * (g(f"slot{s}") + i + 1))
                        prod = ada_prod[n % 2]
                        dve.tensor_tensor(prod, wslot[:, s, :].rearrange("p (k c) -> p k c", k=KT),
                                          per_head(c_act[:, :], P), ALU.mult).then_inc(slot_used[s], 1)
                        dve.drain()
                        return dve.tensor_reduce(ada_rows[:, bass.ds(ADA_SLOTS * i + n, 1), :].rearrange("p o c -> p (o c)"),
                                                 prod.rearrange("p k c -> p c k"), AX, ALU.add)

                    with dve.Fori(0, NF // 2) as i:
                        for b in range(2):
                            dve.wait_ge(sem["silu_ready"], 2 * i + (g("silu_ready") + b + 1))
                            dve.tensor_tensor(mid[:, b, :], silu_g[:, b, :], B(b, 256, 512), ALU.mult).then_inc(sem["mid_ready"], 1)
                            if ada is not None:
                                ada_tile(i, 2 * b)
                                ada_tile(i, 2 * b + 1)
                    if ada is not None:
                        for n in range(ADA_SLOTS):
                            last = ada_tile(NF // 2, n)
                        last.then_inc(sem["ada_rows"], 1)
                    if ph["ada"] is not None:
                        l = ph["ada"]
                        dve.wait_ge(sem["ada_sums"], g("ada_sums") + 1)
                        dve.tensor_tensor(mod[:, l, :], B(3, 0, ADA_TILES), ada_bias[:, l // 2, 48 * (l % 2):48 * (l % 2) + 48], ALU.add)
                        dve.drain()
                        for n in range(2):
                            c = 32 + 8 * (2 * l + n)
                            stt(mod_gain[:, l, n, :], mod[:, l, 8 + 24 * n:16 + 24 * n], 1.0, pcol[:, 0, c:c + 8], ALU.add, ALU.mult)
                elif kind == "ple":
                    with dve.Fori(0, KT // 2) as i:
                        for b in range(2):
                            s = SLOT_SMALL + 2 + b
                            dve.wait_ge(slot_used[s], g(f"slot{s}") + i + 2)
                            dve.wait_ge(sem["ple_s"], 2 * i + (g("ple_s") + b + 1))
                            dve.tensor_tensor(sqT[:, bass.ds(2 * i + b, 1), :], silu_g[:, b:b + 1, :], bank[:, 2 * b + 1:2 * b + 2, 0:256],
                                              ALU.mult).then_inc(sem["ple_d"], 1)
                    dve.drain()
                    for q in range(4):
                        dve.tensor_tensor(xT[:, 2 * q:2 * q + 2, :], xT[:, 2 * q:2 * q + 2, :], sqT[:, 2 * q:2 * q + 2, :],
                                          ALU.add).then_inc(sem["x_ready"], 1)
                elif kind == "store":
                    dve.wait_ge(x_turned, 2)
                    for t in range(TT):
                        last = dve.tensor_copy(x_rows[:, t, :], acc[:, 4 * t:4 * t + 4, :].rearrange("p m s -> p (m s)"))
                    last.then_inc(rows_ready, 1)


_INS = """x p positions attn_norm w_in da_q_norm da_k_norm da_lambda_q1 da_lambda_k1 da_lambda_q2 da_lambda_k2
da_sub_norm ssd_conv_w ssd_conv_b ssd_dt_bias ssd_a_log ssd_d ssd_norm gla_w_gate2 gla_b_gate gla_norm w_out ffn_norm
w_ffn_gate w_ffn_up w_ffn_down ple_w_proj ple_w_gate c_2 ada_w_2 ada_b_2 norm_gain_2 ffn_w_gate_2 ffn_w_up_2
ffn_w_down_2 sb_w_in_2 sb_w_out_2 moba_w_in_2 moba_qk_gain_2 moba_w_out_2 swa_w_in_2 swa_qk_gain_2 swa_sinks_2
swa_w_out_2""".split()


def kernel(**inputs):
    import numpy as _np
    import concourse.bacc as _bacc
    from concourse import mybir as _mybir
    from concourse.bass_utils import run_bass_kernel_spmd as _run

    nc = _bacc.Bacc("TRN2", target_bir_lowering=False, num_devices=1)
    arrays, aps = {}, {}
    for name in _INS:
        v = _np.ascontiguousarray(inputs[name])
        arrays[f"in_{name}_dram"] = v
        aps[name] = nc.dram_tensor(f"in_{name}_dram", v.shape, _mybir.dt.from_np(v.dtype), kind="ExternalInput").ap()
    table, cols = constants()
    table_dram = nc.inline_tensor(table, "table").ap()
    out = nc.dram_tensor("out_0_dram", (1, S, D), _mybir.dt.float32, kind="ExternalOutput").ap()
    two_stacks(nc, aps, table_dram, cols, out)
    r = _run(nc, [arrays], core_ids=[0])
    return r.results[0]["out_0_dram"]
```

```python
import math
from contextlib import ExitStack

import numpy as np
import concourse.bass as bass
from concourse import mybir

F32 = mybir.dt.float32
F32R = mybir.dt.float32r
BF16 = mybir.dt.bfloat16
I32 = mybir.dt.int32
ALU = mybir.AluOpType
ACT = mybir.ActivationFunctionType
AX = mybir.AxisListType.X

P = 128
D = 1024
KT = D // P
S = 256
TT = S // P
FF = 2816
NF = FF // P
DEPTH = 2
DEPTH_2 = 4
EPS = 1e-6
BIG = 1.0e30
OFF_DA_Q, OFF_DA_K, OFF_DA_V = 0, 512, 1024
OFF_Z, OFF_X, OFF_B, OFF_C, OFF_DT = 1536, 2048, 2560, 2816, 3072
OFF_GQ, OFF_GK, OFF_GV, OFF_GG, OFF_LR = 3080, 3336, 3592, 4104, 4616
HEAD_SCALE = 64 ** -0.5
ADA_TILES = 6 * KT
TWO_PI_PARTS = (6.28125, 0.0019340515136718750, 1.2556659146e-06)


def constants():
    p = np.arange(P)
    q = np.arange(P)
    ident = np.eye(P)
    ones = np.ones((P, P))
    halves = (p[:, None] // 64 == q[None, :] // 64) * 1.0
    later = (p[:, None] > q[None, :]) * 1.0
    upto = (p[:, None] <= q[None, :]) * 1.0

    def turn(half, width):
        m = np.zeros((P, P))
        for b in range(0, P, 64):
            for d in range(half):
                m[b + d + half, b + d] = -1.0
                m[b + d, b + d + half] = 1.0
        return m

    causal = np.where(q[None, :] <= p[:, None], 0.0, -BIG)
    causal_neg = np.concatenate([causal, np.zeros((P, P)), causal], 1)
    window = np.where(q[None, :] > p[:, None], 0.0, -BIG)
    window_neg = np.concatenate([causal, window, causal], 1)
    past = (p[:, None] < q[None, :]) * 1.0
    past01 = np.concatenate([past, np.ones((P, P)), past], 1)
    keep = np.tile((np.arange(S) % 64 != 0) * 1.0, (P, 1))
    tri64 = (p[:, None] % 64 <= np.arange(64)[None, :]) * 1.0
    inv2 = (1.0 / (np.float32(10000.0) ** (np.arange(0, 64, 2, dtype=np.float32) / np.float32(64)))).astype(np.float32)
    ang = (np.arange(S, dtype=np.float32)[None, :] * inv2[p % 32][:, None]).astype(np.float32)
    cos2, sin2 = np.cos(ang.astype(np.float64)), np.sin(ang.astype(np.float64))
    inv1 = (np.float32(500000.0) ** (-np.arange(0, 16, 2, dtype=np.float32) / np.float32(16))).astype(np.float32)
    inv = np.where(p % 64 < 16, inv1[p % 8], 0.0)[:, None]
    parts = dict(ident=ident, ones=ones, halves=halves, later=later, upto=upto, turn_da=turn(8, 16),
                 turn=turn(32, 64), causal=causal_neg, window=window_neg, past=past01, keep=keep,
                 tri64=tri64, cos2=cos2, sin2=sin2, inv=inv)
    at, cols = {}, 0
    for name, a in parts.items():
        at[name] = (cols, cols + a.shape[1])
        cols += a.shape[1]
    return np.concatenate([a.astype(np.float32) for a in parts.values()], 1), at


ATT_STEP = dict(v_copied=1, pv_done=1, y_ready=1, scores=2, qk_ready=1)
NORMED = dict(qk_sq=1, qk_ss=1, qk_rs=1, qk_n=1, qk_rot=1, negmax=2, exps=2)
KINDS = {
    "da": dict(ATT_STEP, **NORMED, p_ready=1, p_tr=1, pt_ready=1, y_sq=1, y_ss=1, y_rs=1),
    "moba": dict(ATT_STEP, **NORMED, p_ready=2, p_tr=2, pt_ready=2),
    "swa": dict(ATT_STEP, **NORMED, p_ready=2, p_tr=2, pt_ready=2),
    "sb": dict(ATT_STEP, s_read=2, sb_log=2, sb_spm=2, sb_later=2, sb_la=2, sb_exp=2, pt_ready=2),
}
SSD = dict.fromkeys("""ssd_conv ssd_u ssd_ln ssd_da ssd_act ssd_cum ssd_cumc ssd_xtok ssd_cb ssd_xe ssd_st
                       ssd_m ssd_stc ssd_y ssd_yg ssd_sq ssd_ss ssd_rs ssd_yn""".split(), 1) | dict(ssd_dif=2, ssd_dec=2)
GLA = dict.fromkeys("""gla_lr gla_pgk gla_u gla_ls gla_scan gla_ked gla_e gla_ev gla_dec gla_kee gla_tr gla_kt gla_att
                       gla_attm gla_states gla_st gla_o gla_sq gla_ss gla_rs gla_yn""".split(), 1)
ADA_SLOTS = 4
ADA_BLOCK = ADA_SLOTS * P
ADA_BLOCKS = 6 * D // ADA_BLOCK
SLOT_MIX, SLOT_ADA, SLOT_FF, SLOT_SMALL = 0, 4, 8, 11
N_SLOTS = 15
PART_DOWN = 4


def split_index(what, f):
    if what == "down":
        return 3 * f + (4 if f < NF - 1 else 2) if isinstance(f, int) else 3 * f + 4
    if isinstance(f, int) and f == 0:
        return 0 if what == "gate" else 1
    return 3 * f - (1 if what == "gate" else 0)


def schedule():
    phases, at = [], {}

    def phase(kind, counts, **more):
        phases.append((kind, dict(at), more))
        for k, v in counts.items():
            at[k] = at.get(k, 0) + v

    def slots(base, uses):
        return {f"slot{base + n}": u for n, u in enumerate(uses)}

    def norm(split=False, **more):
        counts = dict(squares=4, sumsq=1, rstd=1, h_ready=KT)
        if split:
            counts.update(h_high=KT, h_parts=KT, w_high=2, **slots(SLOT_FF, [1, 1]))
        phase("norm", counts, split=split, **more)

    def attention(kind, n, **more):
        counts = {k: v * n for k, v in KINDS[kind].items()}
        if kind == "swa":
            counts.update(extra1=n, extra2=n)
        phase("att", dict(counts, **slots(SLOT_MIX, [n] * 4)), att=kind, n=n, **more)

    def add(**more):
        phase("add", dict(x_ready=4), **more)

    def ffn(ada=None, **more):
        counts = dict(silu_ready=NF, mid=NF, mid_high=NF, mid_ready=NF, up_done=NF, down_done=NF,
                      w_high=3 * NF - 2, **slots(SLOT_FF, [NF - 1, NF - 1, NF]))
        if ada is not None:
            counts.update(ada_sums=ADA_BLOCKS, **slots(SLOT_ADA, [ADA_BLOCKS] * ADA_SLOTS))
        phase("ffn", counts, ada=ada, **more)

    phase("setup", dict(x_ready=4))
    for l in range(DEPTH):
        norm(gain=("attn", l))
        attention("da", 4, layer=l)
        for g in range(2):
            phase("ssd", dict(SSD, **slots(SLOT_MIX, [1] * 8), **slots(SLOT_SMALL, [1])), layer=l, g=g)
        for g in range(2):
            phase("gla", dict(GLA, **slots(SLOT_MIX, [1] * 8), **slots(SLOT_SMALL + 1, [1])), layer=l, g=g)
        add(gate=None, last=("slot7", 1))
        norm(gain=("ffn", l), split=True, layer=l, stack=1)
        ffn(ada=l, layer=l, stack=1)
        add(gate=None, last=("down_done", 0))
        phase("ple", dict(ple_t=1, ple_tc=1, ple_s=KT, ple_d=KT, x_ready=4,
                          **slots(SLOT_SMALL + 2, [4] * 2), **slots(SLOT_MIX + 4, [4] * 2)), layer=l)
    for l in range(DEPTH_2):
        norm(gain=("two", l, 0))
        attention(("sb", "moba", "swa")[l % 3], 8, layer=l)
        add(gate=(l, 2), last=("slot3", 1))
        norm(gain=("two", l, 1), split=True, layer=l, stack=2)
        ffn(ada=l + 2 if l + 2 < DEPTH_2 else None, layer=l, stack=2)
        add(gate=(l, 5), last=("down_done", 0))
    phase("store", dict())
    return phases


def two_stacks(nc, a, table_dram, cols, out):
    phases = schedule()
    ctx = ExitStack()
    with ctx:
        ctx.enter_context(nc.allow_non_contiguous_dma(reason="small parameters"))

        def sb(name, shape, dt=F32):
            return ctx.enter_context(nc.sbuf_tensor(name, shape, dt))

        const = sb("const", [P, table_dram.shape[1]])
        xT = sb("xT", [P, KT, S])
        hT = sb("hT", [P, KT, S])
        sqT = sb("sqT", [P, KT, S])
        x_rows = sb("x_rows", [P, TT, D])
        p_rows = sb("p_rows", [P, TT, 256])
        wslot = sb("wslot", [P, SLOT_SMALL, D])
        wsmall = sb("wsmall", [P, 4, 256])
        pcol = sb("pcol", [P, 4, P])
        ada_bias = pcol[:, 2:4, :]
        lam_in = sb("lam_in", [P, DEPTH, 4, 64])
        lam_tmp = sb("lam_tmp", [P, DEPTH, 2, 64])
        lam = sb("lam", [P, DEPTH, 4])
        neg_lam = sb("neg_lam", [P, DEPTH])
        da_gain = sb("da_gain", [P, DEPTH])
        dt_bias = sb("dt_bias", [P, DEPTH, 8])
        a_neg = sb("a_neg", [P, DEPTH, 8])
        wg2 = sb("wg2", [16, DEPTH, 256])
        sinks = sb("sinks", [P, 16])
        a_log = sb("a_log", [P, DEPTH, 8])
        skip_all = sb("skip_all", [P, DEPTH, 8])
        skip = sb("skip", [P, DEPTH, 4])
        c_act = sb("c_act", [P, KT])
        mod = sb("mod", [P, DEPTH_2, ADA_TILES])
        mod_gain = sb("mod_gain", [P, DEPTH_2, 2, KT])
        pos_i = sb("pos_i", [P, S], I32)
        cos1 = sb("cos1", [P, S])
        sin1 = sb("sin1", [P, S])
        rs = sb("rs", [P, S])
        head_work = sb("head_work", [P, 5, 512])
        sq2, rs2, qkn, qkc, qk = (head_work[:, n, :] for n in range(5))
        lb = head_work[:, 0:2, 0:384]
        ang, turns = qk[:, 0:256], qk[:, 256:512]
        ang2 = qkc[:, 0:256]
        ce, xdt = qk, qkc.rearrange("p (t h d) -> p t h d", t=TT, h=4)
        prow = sq2[:, :].rearrange("p (n c) -> p n c", n=4)
        v_sb = sb("v_sb", [P, TT, 256])
        sm = sb("sm", [P, 2, 384])
        pr = sb("pr", [P, 2, 384])
        pt = sb("pt", [P, 2, 384])
        mx = sb("mx", [P, 4])
        nmx = sb("nmx", [P, 4])
        sums = sb("sums", [P, 4])
        esink = sb("esink", [P, 4])
        rinv = sb("rinv", [P, 4])
        sink_now = sb("sink_now", [P, 2])
        y_sb = sb("y_sb", [P, 512])
        ysq = sb("ysq", [P, 512])
        conv, xbc = (x_rows[:, n, :].rearrange("p (j s) -> p j s", j=4) for n in range(2))
        z_sb = sb("z_sb", [P, 2, S])
        dts = sb("dts", [P, 8, 8])
        cum = sb("cum", [P, 8])
        xe = sb("xe", [P, 4, 64])
        b_tok = sb("b_tok", [P, P])
        cbm = sb("cbm", [P, TT, P])
        dif, mt = (sqT[:, 4 * n:4 * n + 4, :].rearrange("p (t a) s -> p t (a s)", t=TT) for n in range(2))
        wend = sb("wend", [P, 4])
        wexp = sb("wexp", [P, 4])
        prev = sb("prev", [P, 256])
        silu_g = sb("silu_g", [P, 2, S])
        mid = sb("mid", [P, 2, S])
        mid_hi = sb("mid_hi", [P, 2, S], F32R)
        mid_lo = sb("mid_lo", [P, 2, S], F32R)
        h_hi = sb("h_hi", [P, KT, S], F32R)
        h_lo = sb("h_lo", [P, KT, S], F32R)
        w_hi = sb("w_hi", [P, PART_DOWN + 1, D], F32R)
        w_lo = sb("w_lo", [P, PART_DOWN + 1, D], F32R)
        attm = sb("attm", [P, 2, S])
        st_sb = pt[:, 0, :]
        ada_part, ada_rows = qkc, qkn
        zero = sb("zero", [1, 512], BF16)
        epst = sb("epst", [P, 1])

        acc = ctx.enter_context(nc.psum_tensor("acc", [P, KT, S], F32))
        bank = ctx.enter_context(nc.psum_tensor("bank", [P, 4, 512], F32))

        names = sorted({k for _, at, _ in phases for k in at if not k.startswith(("slot", "extra"))})
        sem = {k: ctx.enter_context(nc.semaphore(k)) for k in names}
        slot_full = [ctx.enter_context(nc.semaphore(f"slot_full{n}")) for n in range(N_SLOTS)]
        slot_used = [ctx.enter_context(nc.semaphore(f"slot_used{n}")) for n in range(N_SLOTS)]
        loaded = ctx.enter_context(nc.semaphore("loaded"))
        x_loaded = ctx.enter_context(nc.semaphore("x_loaded"))
        p_loaded = ctx.enter_context(nc.semaphore("p_loaded"))
        consts_ready = ctx.enter_context(nc.semaphore("consts_ready"))
        params_turned = ctx.enter_context(nc.semaphore("params_turned"))
        params_ready = ctx.enter_context(nc.semaphore("params_ready"))
        x_turned = ctx.enter_context(nc.semaphore("x_turned"))
        rows_ready = ctx.enter_context(nc.semaphore("rows_ready"))
        small_ready = ctx.enter_context(nc.semaphore("small_ready"))
        small_exp = ctx.enter_context(nc.semaphore("small_exp"))
        cact_ready = ctx.enter_context(nc.semaphore("cact_ready"))
        rope_ready = ctx.enter_context(nc.semaphore("rope_ready"))
        reduced = ctx.enter_context(nc.semaphore("reduced"))
        stored = ctx.enter_context(nc.semaphore("stored"))
        def C(name, lo=0, hi=None):
            b, e = cols[name]
            return const[:, b + lo:(e if hi is None else b + hi)]

        def B(n, lo=0, hi=512):
            return bank[:, n, lo:hi]

        def per_head(ap, n):
            return ap.unsqueeze(2).broadcast_to([ap.shape[0], ap.shape[1], n])

        def per_tile(ap, n):
            return ap.unsqueeze(1).broadcast_to([ap.shape[0], n, ap.shape[1]])

        def gain_of(gain):
            if gain[0] == "attn":
                return pcol[:, 0, 8 * gain[1]:8 * gain[1] + 8]
            if gain[0] == "ffn":
                return pcol[:, 0, 16 + 8 * gain[1]:24 + 8 * gain[1]]
            return mod_gain[:, gain[1], gain[2], :]

        CONV_B, C_ROW, SSD_G = 96, 112, 120
        CONV_W, B_GATE, GLA_G, DA_SUB, DA_Q, DA_K, MOBA_G, SWA_G = 0, 64, 68, 70, 72, 74, 76, 78
        N_B = 80

        def qk_gains(kind, l):
            q, k = {"da": (DA_Q + l, DA_K + l), "moba": (MOBA_G, MOBA_G + 1), "swa": (SWA_G, SWA_G + 1)}[kind]
            return pcol[:, 1, q:q + 1], pcol[:, 1, k:k + 1]

        def rows(n, lo, hi):
            return prow[lo:hi, n, :]

        def over(ap, shape):
            return ap.unsqueeze(0).broadcast_to(shape)

        def twice(ap, rows_n):
            return ap.unsqueeze(1).broadcast_to([rows_n, 2, 64])

        tiles = "l (t p) -> (l t) p"
        loads = [
            (pos_i[:, :], a["positions"][0:1, :].broadcast_to([P, S])),
            (rows(0, 0, 16), a["attn_norm"].rearrange(tiles, p=P)),
            (rows(0, 16, 32), a["ffn_norm"].rearrange(tiles, p=P)),
            (rows(0, 32, 96), a["norm_gain_2"].rearrange("l n (t p) -> (l n t) p", p=P)),
            (rows(0, CONV_B, C_ROW), a["ssd_conv_b"].rearrange(tiles, p=P)),
            (rows(0, C_ROW, SSD_G), a["c_2"].rearrange(tiles, p=P)),
            (rows(0, SSD_G, P), a["ssd_norm"].rearrange(tiles, p=P)),
            (rows(1, CONV_W, B_GATE), a["ssd_conv_w"].rearrange("l w (t p) -> (l w t) p", p=P)),
            (rows(1, B_GATE, GLA_G), a["gla_b_gate"].rearrange(tiles, p=P)),
            (rows(1, GLA_G, DA_SUB), a["gla_norm"]),
            (rows(1, DA_SUB, DA_Q), a["da_sub_norm"]),
            (rows(1, DA_Q, DA_K).rearrange("r (u d) -> r u d", u=2), twice(a["da_q_norm"], 2)),
            (rows(1, DA_K, MOBA_G).rearrange("r (u d) -> r u d", u=2), twice(a["da_k_norm"], 2)),
            (rows(1, MOBA_G, SWA_G).rearrange("r (u d) -> r u d", u=2), twice(a["moba_qk_gain_2"][0], 2)),
            (rows(1, SWA_G, N_B).rearrange("r (u d) -> r u d", u=2), twice(a["swa_qk_gain_2"][0], 2)),
        ] + [
            (rows(2 + n, 0, 96), a["ada_b_2"][2 * n:2 * n + 2].rearrange(tiles, p=P)) for n in range(2)
        ] + [
            (lam_in[:, :, n, :], over(a[name], [P, DEPTH, 64]))
            for n, name in enumerate(("da_lambda_q1", "da_lambda_k1", "da_lambda_q2", "da_lambda_k2"))
        ] + [
            (skip_all[:, :, :], over(a["ssd_d"], [P, DEPTH, 8])),
            (dt_bias[:, :, :], over(a["ssd_dt_bias"], [P, DEPTH, 8])),
            (a_log[:, :, :], over(a["ssd_a_log"], [P, DEPTH, 8])),
            (wg2[:, :, :], a["gla_w_gate2"].rearrange("l r c -> r l c")),
            (sinks[:, :], a["swa_sinks_2"][0:1, :].broadcast_to([P, 16])),
        ]

        block = ctx.enter_context(nc.Block())

        @block.sync
        def _(sp):
            def unit(w, row_tiles, col, width=P):
                return w[0:row_tiles * P, bass.ds(col, width)].rearrange("(k p) c -> p k c", p=P)

            def mix_slot(n):
                return wslot[:, n, :].rearrange("p (k c) -> p k c", k=KT)

            def load(n, dst, src, uses):
                sp.wait_ge(slot_used[n], uses)
                sp.dma_start(dst, src).then_inc(slot_full[n], 16)

            def ffn_weights(ph):
                names = ("w_ffn_gate", "w_ffn_up", "w_ffn_down") if ph["stack"] == 1 else \
                    ("ffn_w_gate_2", "ffn_w_up_2", "ffn_w_down_2")
                return [a[n][ph["layer"]] for n in names]

            for kind, at, ph in phases:
                u = [at.get(f"slot{n}", 0) for n in range(N_SLOTS)]
                if kind == "norm" and ph["split"]:
                    for n, w in enumerate(ffn_weights(ph)[:2]):
                        load(SLOT_FF + n, mix_slot(SLOT_FF + n), unit(w, KT, 0), u[SLOT_FF + n] + 1)
                if kind == "att":
                    att, l = ph["att"], ph["layer"]
                    if att == "da":
                        w, wo = a["w_in"][l], a["w_out"][l]
                        offs = (OFF_DA_Q, OFF_DA_K, OFF_DA_V)
                    elif att == "sb":
                        w, wo, offs = a["sb_w_in_2"][l // 3], a["sb_w_out_2"][l // 3], (0, D, 2 * D)
                    elif att == "moba":
                        w, wo, offs = a["moba_w_in_2"][l // 3], a["moba_w_out_2"][l // 3], (0, D, 2 * D)
                    else:
                        w, wo, offs = a["swa_w_in_2"][l // 3], a["swa_w_out_2"][l // 3], (0, D, D + P)
                    if att == "swa":
                        for kv in range(2):
                            with sp.Fori(0, 4) as i:
                                q_col = sp.snap((i + 4 * kv) * P)
                                row = sp.snap((i + 4 * kv) * P)
                                need = [sp.snap(i + 4 * kv + u[n] + 1) for n in range(4)]
                                load(0, mix_slot(0), unit(w, KT, q_col), need[0])
                                for n in (1, 2):
                                    kv_src = unit(w, KT, D + P * (n - 1) + 64 * kv, 64)
                                    sp.wait_ge(slot_used[n], need[n])
                                    for half in range(2):
                                        sp.dma_start(mix_slot(n)[:, :, 64 * half:64 * half + 64], kv_src)\
                                            .then_inc(slot_full[n], 16)
                                load(3, wslot[:, 3, :], wo[bass.ds(row, P), :], need[3])
                    else:
                        for n in range(3):
                            load(n, mix_slot(n), unit(w, KT, offs[n]), u[n] + 1)
                        with sp.Fori(0, ph["n"] - 1) as i:
                            col = [sp.snap(i * P + (o + P)) for o in offs]
                            row = sp.snap(i * P)
                            need = [sp.snap(i + u[n] + 2) for n in range(3)] + [sp.snap(i + u[3] + 1)]
                            for n in range(3):
                                load(n, mix_slot(n), unit(w, KT, col[n]), need[n])
                            load(3, wslot[:, 3, :], wo[bass.ds(row, P), :], need[3])
                        last = ph["n"] - 1
                        load(3, wslot[:, 3, :], wo[P * last:P * last + P, :], last + u[3] + 1)
                elif kind == "ssd":
                    l, g = ph["layer"], ph["g"]
                    w = a["w_in"][l]
                    for n, col in enumerate((OFF_X + 256 * g, OFF_X + 256 * g + P, OFF_B + P * g, OFF_C + P * g,
                                             OFF_Z + 256 * g, OFF_Z + 256 * g + P)):
                        load(n, mix_slot(n), unit(w, KT, col), u[n] + 1)
                    load(SLOT_SMALL, wsmall[:, 0, 0:32].rearrange("p (k c) -> p k c", k=KT),
                         unit(w, KT, OFF_DT + 4 * g, 4), u[SLOT_SMALL] + 1)
                    for n in range(2):
                        row = 512 + 256 * g + P * n
                        load(6 + n, wslot[:, 6 + n, :], a["w_out"][l][row:row + P, :], u[6 + n] + 1)
                elif kind == "gla":
                    l, g = ph["layer"], ph["g"]
                    w = a["w_in"][l]
                    load(SLOT_SMALL + 1, wsmall[:, 1, 0:P].rearrange("p (k c) -> p k c", k=KT),
                         unit(w, KT, OFF_LR, 16), u[SLOT_SMALL + 1] + 1)
                    for n, col in enumerate((OFF_GQ + P * g, OFF_GK + P * g, OFF_GV + 256 * g, OFF_GV + 256 * g + P,
                                             OFF_GG + 256 * g, OFF_GG + 256 * g + P)):
                        load(n, mix_slot(n), unit(w, KT, col), u[n] + 1)
                    for n in range(2):
                        row = 1024 + 256 * g + P * n
                        load(6 + n, wslot[:, 6 + n, :], a["w_out"][l][row:row + P, :], u[6 + n] + 1)
                elif kind == "ffn":
                    wg, wu, wd = ffn_weights(ph)
                    ada = ph["ada"]
                    g_s, u_s, d_s = SLOT_FF, SLOT_FF + 1, SLOT_FF + 2

                    def ada_unit(n, col, need):
                        src = a["ada_w_2"][ada][2 * P * n:2 * P * n + 2 * P, bass.ds(col, ADA_BLOCK)]
                        load(SLOT_ADA + n, wslot[:, SLOT_ADA + n, :].rearrange("p (j c) -> p j c", j=2),
                             src.rearrange("(j p) c -> p j c", p=P), need)

                    def two_steps(cols, rows, need, acol, aneed):
                        for b in range(2):
                            if cols[b] is not None:
                                load(g_s, mix_slot(g_s), unit(wg, KT, cols[b]), need[b])
                                load(u_s, mix_slot(u_s), unit(wu, KT, cols[b]), need[2 + b])
                            load(d_s, wslot[:, d_s, :], wd[bass.ds(rows[b], P), :], need[4 + b])
                            if ada is not None:
                                for n in range(2 * b, 2 * b + 2):
                                    ada_unit(n, acol, aneed[n])

                    base = [u[g_s], u[g_s], u[u_s], u[u_s], u[d_s], u[d_s]]
                    with sp.Fori(0, NF // 2 - 1) as i:
                        cols = [sp.snap((2 * i + b) * P + P) for b in range(2)]
                        rows = [sp.snap((2 * i + b) * P) for b in range(2)]
                        need = [sp.snap(2 * i + (base[n] + n % 2 + 1)) for n in range(6)]
                        acol = aneed = None
                        if ada is not None:
                            acol = sp.snap(i * ADA_BLOCK)
                            aneed = [sp.snap(i + u[SLOT_ADA + n] + 1) for n in range(ADA_SLOTS)]
                        two_steps(cols, rows, need, acol, aneed)
                    i = NF // 2 - 1
                    two_steps([(NF - 1) * P, None], [(NF - 2) * P, (NF - 1) * P],
                              [2 * i + base[n] + n % 2 + 1 for n in range(6)],
                              i * ADA_BLOCK, [i + u[SLOT_ADA + n] + 1 for n in range(ADA_SLOTS)])
                    if ada is not None:
                        for n in range(ADA_SLOTS):
                            ada_unit(n, (ADA_BLOCKS - 1) * ADA_BLOCK, ADA_BLOCKS - 1 + u[SLOT_ADA + n] + 1)
                elif kind == "ple":
                    l = ph["layer"]
                    with sp.Fori(0, KT // 2) as i:
                        col = [sp.snap((2 * i + b) * P) for b in range(2)]
                        need = [sp.snap(i + u[SLOT_MIX + 4 + b] + 1) for b in range(2)]
                        sneed = [sp.snap(i + u[SLOT_SMALL + 2 + b] + 1) for b in range(2)]
                        for b in range(2):
                            load(4 + b, mix_slot(4 + b), unit(a["ple_w_gate"][l], KT, col[b]), need[b])
                            load(SLOT_SMALL + 2 + b, wsmall[:, 2 + b, :].rearrange("p (k c) -> p k c", k=2),
                                 unit(a["ple_w_proj"][l], 2, col[b]), sneed[b])
            sp.wait_ge(rows_ready, 1)
            sp.dma_start(out[0].rearrange("(t p) d -> p t d", p=P), x_rows[:, :, :]).then_inc(stored, 16)
            sp.wait_ge(stored, 16)

        @block.tensor
        def _(pe):
            for n in range(N_SLOTS):
                pe.sem_inc(slot_used[n], 1)

            def wk(n, k):
                return wslot[:, n, P * k:P * k + P]

            def feature_tile(n, dst, uses, at=None):
                pe.wait_ge(slot_full[n], uses)
                for k in range(KT):
                    if at is not None:
                        pe.wait_ge(sem["h_ready"], at + k + 1)
                    mm = pe.matmul(dst, wk(n, k), hT[:, k, :], start=(k == 0), stop=(k == KT - 1))
                mm.then_inc(slot_used[n], 1)
                return mm

            def token_tiles(n, dst, uses):
                pe.wait_ge(slot_full[n], uses)
                for t in range(TT):
                    for k in range(KT):
                        mm = pe.matmul(dst(t), hT[:, k, P * t:P * t + P], wk(n, k), start=(k == 0), stop=(k == KT - 1))
                mm.then_inc(slot_used[n], 1)

            def clear_acc():
                for m in range(4):
                    pe.matmul(acc[:, 2 * m:2 * m + 2, :].rearrange("p m s -> p (m s)"), zero[0:1, 0:P], zero[0:1, :],
                              start=True, stop=False, skip_group_check=True)

            def add_out(n, y, tiles=range(KT), free=True):
                for m in tiles:
                    mm = pe.matmul(acc[:, m, :], wk(n, m), y, start=False, stop=False, skip_group_check=True)
                if free:
                    mm.then_inc(slot_used[n], 1)

            pe.wait_ge(consts_ready, 1)
            pe.wait_ge(x_loaded, 32)
            ident = C("ident")
            for m in range(KT):
                for t in range(TT):
                    mm = pe.transpose(acc[:, m, P * t:P * t + P], x_rows[:, t, P * m:P * m + P], ident)
            mm.then_inc(x_turned, 1)
            pe.wait_ge(loaded, 16 * len(loads))
            for n, rows in enumerate((P, N_B, 96, 96)):
                mm = pe.transpose(B(0, P * n, P * n + rows), prow[0:rows, n, :], const[0:rows, cols["ident"][0]:cols["ident"][0] + rows])
            mm.then_inc(params_turned, 1)

            def attention(ph, at, first_h):
                att = ph["att"]
                n = ph["n"]
                g = lambda k: at.get(k, 0)
                normed = att != "sb"

                def full_kv(n, i):
                    return 16 * (g(f"slot{n}") + g(f"extra{n}")) + (32 if att == "swa" else 16) * (i + 1)

                def proj_qk(i, first=False):
                    if not first:
                        pe.wait_ge(sem["qk_n" if normed else "qk_ready"], g("qk_n" if normed else "qk_ready") + i)
                    h = g("h_ready") - 8 if first else None
                    feature_tile(0, B(0, 0, 256), 16 * (g("slot0") + i + 1), h)
                    pe.wait_ge(slot_full[1], full_kv(1, i))
                    for k in range(KT):
                        mm = pe.matmul(B(0, 256, 512), wk(1, k), hT[:, k, :], start=(k == 0), stop=(k == KT - 1))
                    mm.then_inc(slot_used[1], 1)
                    return mm

                def scores(i):
                    pe.wait_ge(sem["qk_ready"], g("qk_ready") + i + 1)
                    pe.wait_ge(consts_ready, 1)
                    for hh in range(2):
                        r = slice(64 * hh, 64 * hh + 64)
                        if att == "sb":
                            pe.matmul(bank[:, 2 + hh, 0:256], qk[r, 256:384], qk[r, 0:256], start=True, stop=True)
                            mm = pe.matmul(bank[:, 2 + hh, 256:384], qk[r, 384:512], qk[r, 128:256], start=True, stop=True)
                        else:
                            pe.matmul(bank[:, 2 + hh, 0:128], qk[r, 0:128], qk[r, 256:384], start=True, stop=True)
                            mm = pe.matmul(bank[:, 2 + hh, 128:384], qk[r, 128:256], qk[r, 256:512], start=True, stop=True)
                        mm.then_inc(sem["scores"], 1)

                def middle(i):
                    if att == "sb":
                        for hh in range(2):
                            pe.wait_ge(sem["sb_spm"], g("sb_spm") + 2 * i + hh + 1)
                            pe.matmul(bank[:, 2 + hh, 0:256], C("later"), sm[:, hh, 0:256], start=True, stop=False)
                            pe.matmul(bank[:, 2 + hh, 128:256], C("ones"), sm[:, hh, 256:384], start=False, stop=True)
                            pe.matmul(bank[:, 2 + hh, 256:384], C("later"), sm[:, hh, 256:384], start=True, stop=True)\
                                .then_inc(sem["sb_later"], 1)
                        return
                    heads = 1 if att == "da" else 2
                    for hh in range(heads):
                        pe.wait_ge(sem["p_ready"], g("p_ready") + heads * i + hh + 1)
                        for b in range(3):
                            mm = pe.transpose(bank[:, 2 + hh, P * b:P * b + P], pr[:, hh, P * b:P * b + P], ident)
                        mm.then_inc(sem["p_tr"], 1)

                def values(i):
                    heads = 1 if att == "da" else 2
                    width = P // heads
                    pe.wait_ge(sem["v_copied"], g("v_copied") + i + 1)
                    pe.wait_ge(consts_ready, 1)
                    for hh in range(heads):
                        c = slice(width * hh, width * hh + width)
                        pe.wait_ge(sem["pt_ready"], g("pt_ready") + heads * i + hh + 1)
                        pe.wait_ge(consts_ready, 1)
                        pe.matmul(bank[c, 1, 0:256], v_sb[:, 0, c], pt[:, hh, 0:256], start=True, stop=False)
                        mm = pe.matmul(bank[c, 1, 128:256], v_sb[:, 1, c], pt[:, hh, 256:384], start=False, stop=True)
                    mm.then_inc(sem["pv_done"], 1)

                def proj_v(i, first):
                    if not first:
                        pe.wait_ge(sem["v_copied"], g("v_copied") + i)
                    token_tiles(2, lambda t: B(1, 256 + P * t, 384 + P * t), full_kv(2, i))

                def whole(i, first, prior):
                    proj_qk(i, first)
                    if prior is not None:
                        middle(prior)
                    proj_v(i, first)
                    if prior is not None:
                        values(prior)
                    if normed:
                        pe.wait_ge(sem["qk_sq"], g("qk_sq") + i + 1)
                        pe.matmul(B(2), C("halves"), sq2[:, :], start=True, stop=True).then_inc(sem["qk_ss"], 1)
                    if prior is not None:
                        if att == "da":
                            pe.wait_ge(sem["y_sq"], g("y_sq") + prior + 1)
                            pe.matmul(B(3, 0, 256), C("ones"), ysq[:, 0:256], start=True, stop=True)\
                                .then_inc(sem["y_ss"], 1)
                        pe.wait_ge(slot_full[3], 16 * (g("slot3") + prior + 1))
                        pe.wait_ge(sem["y_ready"], g("y_ready") + prior + 1)
                        add_out(3, y_sb[:, 0:256], range(4), free=False)
                    if normed:
                        pe.wait_ge(sem["qk_n"], g("qk_n") + i + 1)
                        pe.matmul(B(3), C("turn_da" if att == "da" else "turn"), qkn[:, :], start=True, stop=True)\
                            .then_inc(sem["qk_rot"], 1)
                    if prior is not None:
                        add_out(3, y_sb[:, 0:256], range(4, 8))
                    scores(i)

                whole(0, True, None)
                with pe.Fori(0, n - 1) as j:
                    whole(j + 1, False, j)
                last = n - 1
                middle(last)
                values(last)
                if att == "da":
                    pe.wait_ge(sem["y_sq"], g("y_sq") + last + 1)
                    pe.matmul(B(3, 0, 256), C("ones"), ysq[:, 0:256], start=True, stop=True).then_inc(sem["y_ss"], 1)
                pe.wait_ge(slot_full[3], 16 * (g("slot3") + last + 1))
                pe.wait_ge(sem["y_ready"], g("y_ready") + last + 1)
                add_out(3, y_sb[:, 0:256])

            for kind, at, ph in phases:
                g = lambda k: at.get(k, 0)
                full = lambda n: 16 * (g(f"slot{n}") + g(f"extra{n}") + 1)
                if kind == "norm":
                    for k in range(KT):
                        if k % 2 == 0:
                            pe.wait_ge(sem["squares"], g("squares") + k // 2 + 1)
                        mm = pe.matmul(B(0, 0, 256), C("ones"), sqT[:, k, :], start=(k == 0), stop=(k == KT - 1))
                    mm.then_inc(sem["sumsq"], 1)
                    clear_acc()
                elif kind == "att":
                    attention(ph, at, True)
                elif kind == "ssd":
                    for n in range(2):
                        mm = feature_tile(n, B(0, 256 * n, 256 * n + 256), full(n))

                    for n in range(2):
                        feature_tile(2 + n, B(1, 256 * n, 256 * n + 256), full(2 + n))

                    pe.wait_ge(slot_full[SLOT_SMALL], full(SLOT_SMALL))
                    for t in range(TT):
                        for k in range(KT):
                            mm = pe.matmul(B(3, 4 * t, 4 * t + 4), hT[:, k, P * t:P * t + P], wsmall[:, 0, 4 * k:4 * k + 4],
                                           start=(k == 0), stop=(k == KT - 1))
                    mm.then_inc(slot_used[SLOT_SMALL], 1)

                    for n in range(2):
                        feature_tile(4 + n, B(2, 256 * n, 256 * n + 256), full(4 + n))

                    pe.wait_ge(sem["ssd_da"], g("ssd_da") + 1)
                    da = dts[:, 7, :]
                    pe.matmul(B(3, 16, 24), C("upto"), da, start=True, stop=True)
                    for t in range(TT):
                        for h in range(4):
                            i = 4 * t + h
                            mm = pe.matmul(B(t, P * h, P * h + P), da[:, i:i + 1].broadcast_to([P, P]), C("upto"),
                                           start=True, stop=True)
                    mm.then_inc(sem["ssd_cum"], 1)
                    pe.wait_ge(sem["ssd_act"], g("ssd_act") + 1)
                    for t in range(TT):
                        for j in range(2):
                            mm = pe.transpose(B(2, 256 * t + P * j, 256 * t + P * j + P), xbc[:, j, P * t:P * t + P], ident)
                    mm.then_inc(sem["ssd_xtok"], 1)
                    pe.wait_ge(sem["ssd_cumc"], g("ssd_cumc") + 1)
                    pe.transpose(B(3, 128, 256), xbc[:, 2, 0:P], ident)
                    for t in range(TT):
                        mm = pe.matmul(B(3, 256 + P * t, 384 + P * t), xbc[:, 2, P * t:P * t + P], xbc[:, 3, P * t:P * t + P],
                                       start=True, stop=True)
                    mm.then_inc(sem["ssd_cb"], 1)
                    pe.wait_ge(sem["ssd_xe"], g("ssd_xe") + 1)
                    pe.matmul(B(3, 256, 512), b_tok[:, :], xe[:, :, :].rearrange("p h d -> p (h d)"), start=True, stop=True)\
                        .then_inc(sem["ssd_st"], 1)
                    pe.wait_ge(sem["ssd_m"], g("ssd_m") + 1)
                    pe.wait_ge(sem["ssd_stc"], g("ssd_stc") + 1)
                    for h in range(4):
                        j, r = h // 2, slice(64 * (h % 2), 64 * (h % 2) + 64)
                        for t in range(TT):
                            mm = pe.matmul(bank[r, 2, 256 * j + P * t:256 * j + P * t + P], xdt[:, t, h, :],
                                           mt[:, t, P * h:P * h + P], start=True, stop=(t == 0))
                        mm = pe.matmul(bank[r, 2, 256 * j + P:256 * j + 256], prev[:, 64 * h:64 * h + 64],
                                       ce[:, P * h:P * h + P], start=False, stop=True)
                    mm.then_inc(sem["ssd_y"], 1)
                    pe.wait_ge(sem["ssd_sq"], g("ssd_sq") + 1)
                    for j in range(2):
                        mm = pe.matmul(B(3, 0, 256), C("ones"), ysq[:, 256 * j:256 * j + 256], start=(j == 0), stop=(j == 1))
                    mm.then_inc(sem["ssd_ss"], 1)
                    pe.wait_ge(sem["ssd_yn"], g("ssd_yn") + 1)
                    for j in range(2):
                        pe.wait_ge(slot_full[6 + j], full(6 + j))
                        add_out(6 + j, y_sb[:, 256 * j:256 * j + 256])
                elif kind == "gla":
                    gg = ph["g"]
                    pe.wait_ge(slot_full[SLOT_SMALL + 1], full(SLOT_SMALL + 1))
                    for k in range(KT):
                        mm = pe.matmul(bank[0:16, 3, 0:256], wsmall[:, 1, 16 * k:16 * k + 16], hT[:, k, :],
                                       start=(k == 0), stop=(k == KT - 1))
                    mm.then_inc(slot_used[SLOT_SMALL + 1], 1)

                    for n in range(2):
                        feature_tile(n, B(0, 256 * n, 256 * n + 256), full(n))

                    pe.wait_ge(sem["gla_lr"], g("gla_lr") + 1)
                    pe.matmul(B(3, 256, 512), wg2[0:16, ph["layer"], P * gg:P * gg + P], qkc[0:16, 0:256],
                              start=True, stop=True).then_inc(sem["gla_pgk"], 1)
                    for n in range(2):
                        token_tiles(2 + n, lambda t: B(1, 256 * t + P * n, 256 * t + P * n + P), full(2 + n))

                    for n in range(2):
                        feature_tile(4 + n, B(2, 256 * n, 256 * n + 256), full(4 + n))

                    pe.wait_ge(sem["gla_kee"], g("gla_kee") + 1)
                    pe.wait_ge(sem["gla_ev"], g("gla_ev") + 1)
                    for t in range(TT):
                        mm = pe.transpose(B(2, P * t, P * t + P), qkc[:, P * t:P * t + P], ident)
                    mm.then_inc(sem["gla_tr"], 1)
                    pe.wait_ge(sem["gla_dec"], g("gla_dec") + 1)
                    for c in range(4):
                        t, r = c // 2, slice(64 * (c % 2), 64 * (c % 2) + 64)
                        for hh in range(2):
                            d = slice(64 * hh, 64 * hh + 64)
                            mm = pe.matmul(bank[r, hh, P * t + r.start:P * t + r.stop], qk[d, 256 + 64 * c:320 + 64 * c],
                                           qk[d, 64 * c:64 * c + 64], start=True, stop=True)
                    mm.then_inc(sem["gla_att"], 1)
                    pe.wait_ge(sem["gla_kt"], g("gla_kt") + 1)
                    for c in range(3):
                        t, r = c // 2, slice(64 * (c % 2), 64 * (c % 2) + 64)
                        for hh in range(2):
                            d = slice(64 * hh, 64 * hh + 64)
                            dst = bank[d, 3, 0:P] if c == 1 else bank[d, 2, 256 + 64 * c:384 + 64 * c]
                            mm = pe.matmul(dst, qkn[r, P * t + d.start:P * t + d.stop], v_sb[r, t, P * hh:P * hh + P],
                                           start=True, stop=True)
                    mm.then_inc(sem["gla_states"], 1)
                    pe.wait_ge(sem["gla_attm"], g("gla_attm") + 1)
                    pe.wait_ge(sem["gla_st"], g("gla_st") + 1)
                    st = st_sb
                    for hh in range(2):
                        d = slice(64 * hh, 64 * hh + 64)
                        for t in range(TT):
                            pe.matmul(bank[:, hh, 256 + P * t:384 + P * t], v_sb[:, t, P * hh:P * hh + P], attm[:, hh, P * t:P * t + P],
                                      start=True, stop=False)
                            for c in ((1,) if t == 0 else (2, 3)):
                                mm = pe.matmul(bank[:, hh, 256 + 64 * c:320 + 64 * c], st[d, P * (c - 1):P * c],
                                               qk[d, 64 * c:64 * c + 64], start=False, stop=(c != 2))
                    mm.then_inc(sem["gla_o"], 1)
                    pe.wait_ge(sem["gla_sq"], g("gla_sq") + 1)
                    pe.matmul(B(2), C("ones"), ysq[:, :], start=True, stop=True).then_inc(sem["gla_ss"], 1)
                    pe.wait_ge(sem["gla_yn"], g("gla_yn") + 1)
                    for j in range(2):
                        pe.wait_ge(slot_full[6 + j], full(6 + j))
                        add_out(6 + j, y_sb[:, 256 * j:256 * j + 256])
                elif kind == "ffn":
                    ada = ph["ada"]

                    def three(dst, w, cols, hi, lo, start, stop):
                        pe.matmul(dst, w_hi[:, w, cols], hi, start=start, stop=False, skip_group_check=True)
                        pe.matmul(dst, w_hi[:, w, cols], lo, start=False, stop=False, skip_group_check=True)
                        return pe.matmul(dst, w_lo[:, w, cols], hi, start=False, stop=stop, skip_group_check=True)

                    def up(f, b, first=False):
                        for n in range(2):
                            s = SLOT_FF + n
                            pe.wait_ge(slot_used[s], g(f"slot{s}") + f + 1)
                            for k in range(KT):
                                if first and n == 0:
                                    pe.wait_ge(sem["h_parts"], g("h_parts") - KT + k + 1)
                                mm = three(B(b, 256 * n, 256 * n + 256), 2 * b + n, slice(P * k, P * k + P),
                                           h_hi[:, k, :], h_lo[:, k, :], k == 0, k == KT - 1)
                        mm.then_inc(sem["up_done"], 1)

                    def down(f, b):
                        s = SLOT_FF + 2
                        pe.wait_ge(slot_used[s], g(f"slot{s}") + f + 2)
                        pe.wait_ge(sem["mid_ready"], g("mid_ready") + f + 1)
                        for m in range(KT):
                            mm = three(acc[:, m, :], PART_DOWN, slice(P * m, P * m + P), mid_hi[:, b, :], mid_lo[:, b, :],
                                       False, False)
                        mm.then_inc(sem["down_done"], 1)

                    def ada_sum(block):
                        s = SLOT_ADA + ADA_SLOTS - 1
                        pe.wait_ge(slot_used[s], g(f"slot{s}") + block + 2)
                        pe.wait_ge(consts_ready, 1)
                        for m in range(ADA_SLOTS):
                            mm = pe.matmul(B(3, m, m + 1), ada_rows[:, P * m:P * m + P], C("ones", 0, 1), start=True, stop=True)
                        mm.then_inc(sem["ada_sums"], 1)

                    def two_chunks(i, block):
                        up(2 * i + 1, 1)
                        if block is not None and ada is not None:
                            ada_sum(block)
                        down(2 * i, 0)
                        up(2 * i + 2, 0)
                        down(2 * i + 1, 1)

                    up(0, 0, first=True)
                    two_chunks(0, None)
                    with pe.Fori(1, NF // 2 - 1) as i:
                        two_chunks(i, i - 1)
                    up(NF - 1, 1)
                    if ada is not None:
                        ada_sum(NF // 2 - 2)
                    down(NF - 2, 0)
                    down(NF - 1, 1)
                    if ada is not None:
                        for block in range(NF // 2 - 1, ADA_BLOCKS):
                            ada_sum(block)

                elif kind == "ple":
                    l = ph["layer"]
                    pe.wait_ge(p_loaded, 16 * (l + 1))
                    for kk in range(2):
                        for t in range(TT):
                            mm = pe.transpose(B(2, 256 * kk + P * t, 256 * kk + P * t + P), p_rows[:, t, P * kk:P * kk + P], ident)
                    mm.then_inc(sem["ple_t"], 1)
                    pe.wait_ge(sem["x_ready"], g("x_ready"))
                    pe.wait_ge(sem["ple_tc"], g("ple_tc") + 1)

                    def ple_tile(i, b, reused):
                        if reused:
                            pe.wait_ge(sem["ple_d"], 2 * i + (g("ple_d") + b - 1))
                        s = SLOT_MIX + 4 + b
                        pe.wait_ge(slot_full[s], 16 * (g(f"slot{s}") + i + 1))
                        for k in range(KT):
                            mm = pe.matmul(B(2 * b, 0, 256), wk(s, k), xT[:, k, :], start=(k == 0),
                                           stop=(k == KT - 1))
                        mm.then_inc(slot_used[s], 1)
                        s = SLOT_SMALL + 2 + b
                        pe.wait_ge(slot_full[s], 16 * (g(f"slot{s}") + i + 1))
                        for k in range(2):
                            mm = pe.matmul(B(2 * b + 1, 0, 256), wsmall[:, 2 + b, P * k:P * k + P],
                                           qk[:, 256 * k:256 * k + 256], start=(k == 0), stop=(k == 1))
                        mm.then_inc(slot_used[s], 1)

                    for b in range(2):
                        ple_tile(0, b, False)
                    with pe.Fori(1, KT // 2) as i:
                        for b in range(2):
                            ple_tile(i, b, True)
                elif kind == "store":
                    pe.wait_ge(sem["x_ready"], g("x_ready"))
                    for t in range(TT):
                        for m in range(KT):
                            mm = pe.transpose(acc[:, 4 * t + m // 2, P * (m % 2):P * (m % 2) + P], xT[:, m, P * t:P * t + P], ident)
                    mm.then_inc(x_turned, 1)

        @block.scalar
        def _(act):
            act.dma_start(x_rows[:, :, :], a["x"][0].rearrange("(t p) d -> p t d", p=P)).then_inc(x_loaded, 16)
            act.dma_start(const[:, :], table_dram).then_inc(x_loaded, 16)
            for dst, src in loads:
                act.dma_start(dst, src).then_inc(loaded, 16)

            def copy(dst, src):
                return act.activation(dst, src, ACT.Copy)

            def inverse_root(dst, src, n):
                act.activation(dst, src, ACT.Ln, scale=1.0 / n, bias=epst[:, 0:1])
                act.drain()
                return act.activation(dst, dst, ACT.Exp, scale=-0.5)

            def log_one_plus_exp(tmp, src, scale=1.0):
                act.activation(tmp, src, ACT.Abs, scale=scale)
                act.drain()
                act.activation(tmp, tmp, ACT.Exp, scale=-1.0)
                act.drain()
                return act.activation(tmp, tmp, ACT.Ln, bias=1.0)

            def load_p(l):
                act.dma_start(p_rows[:, :, :], a["p"][l, 0].rearrange("(t p) d -> p t d", p=P)).then_inc(p_loaded, 16)

            LN_EXP = "natural_log_exp_and_others"
            act.preload_act_table_set(LN_EXP)
            act.wait_ge(small_ready, 1)
            act.activation(lam[:, :, 2:4], lam[:, :, 0:2], ACT.Exp)
            act.activation(a_neg[:, :, :], a_log[:, :, :], ACT.Exp).then_inc(small_exp, 1)
            act.wait_ge(rope_ready, 1)
            act.activation(sin1[:, :], turns[:, :], ACT.Sin)
            act.activation(cos1[:, :], ang2[:, :], ACT.Sin).then_inc(rope_ready, 1)
            act.wait_ge(params_ready, 1)
            act.activation(c_act[:, :], pcol[:, 0, C_ROW:SSD_G], ACT.Silu).then_inc(cact_ready, 1)
            act.wait_ge(x_turned, 1)
            load_p(0)

            def attention(ph, at):
                att, n = ph["att"], ph["n"]
                g = lambda k: at.get(k, 0)
                heads = 1 if att == "da" else 2

                def whole(i, prior):
                    if i is not None:
                        act.wait_ge(slot_used[1], g("slot1") + i + 2)
                        if att == "sb":
                            copy(qk[:, :], B(0)).then_inc(sem["qk_ready"], 1)
                        else:
                            act.activation(sq2[:, :], B(0), ACT.Square).then_inc(sem["qk_sq"], 1)
                    if prior is not None:
                        for hh in range(heads):
                            if att == "sb":
                                act.wait_ge(sem["sb_la"], g("sb_la") + 2 * prior + hh + 1)
                                act.activation(pt[:, hh, :], pr[:, hh, :], ACT.Exp).then_inc(sem["sb_exp"], 1)
                            else:
                                act.wait_ge(sem["p_tr"], g("p_tr") + heads * prior + hh + 1)
                                copy(pt[:, hh, :], bank[:, 2 + hh, 0:384]).then_inc(sem["pt_ready"], 1)
                        act.wait_ge(sem["pv_done"], g("pv_done") + prior + 1)
                    if i is not None:
                        act.wait_ge(slot_used[2], g("slot2") + i + 2)
                        copy(v_sb[:, :, 0:P], B(1, 256, 512).rearrange("p (t d) -> p t d", t=TT)).then_inc(sem["v_copied"], 1)
                    if prior is not None:
                        if att == "da":
                            act.activation(ysq[:, 0:256], B(1, 0, 256), ACT.Square).then_inc(sem["y_sq"], 1)
                        else:
                            copy(y_sb[:, 0:256], B(1, 0, 256)).then_inc(sem["y_ready"], 1)
                    if i is not None and att != "sb":
                        act.wait_ge(sem["qk_ss"], g("qk_ss") + i + 1)
                        inverse_root(rs2[:, :], B(2), 64).then_inc(sem["qk_rs"], 1)
                    if prior is not None and att == "da":
                        act.wait_ge(sem["y_ss"], g("y_ss") + prior + 1)
                        inverse_root(rs[:, :], B(3, 0, 256), P).then_inc(sem["y_rs"], 1)
                    if i is None:
                        return
                    for hh in range(2):
                        if att == "sb":
                            act.wait_ge(sem["s_read"], g("s_read") + 2 * i + hh + 1)
                            log_one_plus_exp(pr[:, hh, :], lb[:, hh, :]).then_inc(sem["sb_log"], 1)
                        else:
                            act.wait_ge(sem["negmax"], g("negmax") + 2 * i + hh + 1)
                            act.activation(pr[:, hh, 0:128], sm[:, hh, 0:128], ACT.Exp, bias=nmx[:, 2 * hh:2 * hh + 1],
                                           accum_out=sums[:, 2 * hh:2 * hh + 1])
                            if att == "swa":
                                act.activation(esink[:, 2 * hh:2 * hh + 2], nmx[:, 2 * hh:2 * hh + 2], ACT.Exp,
                                               bias=sink_now[:, hh:hh + 1])
                            act.activation(pr[:, hh, 128:384], sm[:, hh, 128:384], ACT.Exp,
                                           bias=nmx[:, 2 * hh + 1:2 * hh + 2],
                                           accum_out=sums[:, 2 * hh + 1:2 * hh + 2]).then_inc(sem["exps"], 1)

                whole(0, None)
                with act.Fori(0, n - 1) as j:
                    whole(j + 1, j)
                whole(None, n - 1)

            def high(n, part, loads):
                act.wait_ge(slot_full[n], loads)
                copy(w_hi[:, part, :], wslot[:, n, :]).then_inc(sem["w_high"], 1)

            for kind, at, ph in phases:
                g = lambda k: at.get(k, 0)
                if kind == "norm":
                    act.preload_act_table_set(LN_EXP)
                    if ph["split"]:
                        for n in range(2):
                            high(SLOT_FF + n, n, 16 * (g(f"slot{SLOT_FF + n}") + 1))
                    for q in range(4):
                        act.wait_ge(sem["x_ready"], g("x_ready") - 3 + q)
                        act.activation(sqT[:, 2 * q:2 * q + 2, :], xT[:, 2 * q:2 * q + 2, :], ACT.Square)\
                           .then_inc(sem["squares"], 1)
                    act.wait_ge(sem["sumsq"], g("sumsq") + 1)
                    inverse_root(rs[:, :], B(0, 0, 256), D).then_inc(sem["rstd"], 1)
                    if ph["split"]:
                        for k in range(KT):
                            act.wait_ge(sem["h_ready"], g("h_ready") + k + 1)
                            copy(h_hi[:, k, :], hT[:, k, :]).then_inc(sem["h_high"], 1)
                elif kind == "att":
                    attention(ph, at)
                elif kind == "ssd":
                    act.wait_ge(sem["ssd_u"], g("ssd_u") + 1)
                    act.activation(dts[:, 1, :], dts[:, 0, :], ACT.Abs)
                    act.drain()
                    act.activation(dts[:, 2, :], dts[:, 1, :], ACT.Exp, scale=-1.0)
                    act.drain()
                    act.activation(dts[:, 3, :], dts[:, 2, :], ACT.Ln, bias=1.0).then_inc(sem["ssd_ln"], 1)
                    act.wait_ge(sem["ssd_conv"], g("ssd_conv") + 1)
                    act.activation(xbc[:, :, :], conv[:, :, :], ACT.Silu)
                    act.wait_ge(slot_used[5], g("slot5") + 2)
                    act.activation(z_sb[:, :, :], B(2).rearrange("p (j s) -> p j s", j=2), ACT.Silu).then_inc(sem["ssd_act"], 1)
                    act.preload_act_table_set(LN_EXP)
                    act.wait_ge(sem["ssd_dif"], g("ssd_dif") + 1)
                    act.activation(wexp[:, :], wend[:, :], ACT.Exp)
                    act.activation(dif[:, 0, :], dif[:, 0, :], ACT.Exp).then_inc(sem["ssd_dec"], 1)
                    act.wait_ge(sem["ssd_dif"], g("ssd_dif") + 2)
                    act.activation(dif[:, 1, :], dif[:, 1, :], ACT.Exp)
                    act.activation(ce[:, :], B(1), ACT.Exp).then_inc(sem["ssd_dec"], 1)
                    act.wait_ge(sem["ssd_yg"], g("ssd_yg") + 1)
                    act.activation(ysq[:, :], y_sb[:, :], ACT.Square).then_inc(sem["ssd_sq"], 1)
                    act.wait_ge(sem["ssd_ss"], g("ssd_ss") + 1)
                    inverse_root(rs[:, :], B(3, 0, 256), 256).then_inc(sem["ssd_rs"], 1)
                elif kind == "gla":
                    act.wait_ge(slot_used[SLOT_SMALL + 1], g(f"slot{SLOT_SMALL + 1}") + 2)
                    copy(qkc[0:16, 0:256], bank[0:16, 3, 0:256]).then_inc(sem["gla_lr"], 1)
                    act.wait_ge(sem["gla_u"], g("gla_u") + 1)
                    log_one_plus_exp(sm[:, 1, 0:256], sm[:, 0, 0:256]).then_inc(sem["gla_ls"], 1)
                    act.wait_ge(sem["gla_scan"], g("gla_scan") + 1)
                    act.activation(sq2[:, 0:256], rs2[:, 0:256], ACT.Exp, scale=1.0 / 16)
                    act.activation(sq2[:, 256:512], rs2[:, 0:256], ACT.Exp, scale=-1.0 / 16)
                    act.wait_ge(sem["gla_ked"], g("gla_ked") + 1)
                    act.activation(qkn[:, 256:512], rs2[:, 256:512], ACT.Exp, scale=1.0 / 16).then_inc(sem["gla_e"], 1)
                    act.wait_ge(slot_used[3], g("slot3") + 2)
                    copy(v_sb[:, :, :], B(1).rearrange("p (t d) -> p t d", t=TT))
                    act.wait_ge(slot_used[5], g("slot5") + 2)
                    act.activation(silu_g[:, :, :], B(2).rearrange("p (j s) -> p j s", j=2), ACT.Silu).then_inc(sem["gla_ev"], 1)
                    act.preload_act_table_set(LN_EXP)
                    act.wait_ge(sem["gla_o"], g("gla_o") + 1)
                    act.activation(ysq[:, :].rearrange("p (j s) -> p j s", j=2), bank[:, 0:2, 256:512], ACT.Square)\
                       .then_inc(sem["gla_sq"], 1)
                    act.wait_ge(sem["gla_ss"], g("gla_ss") + 1)
                    inverse_root(rs2[:, :], B(2), P).then_inc(sem["gla_rs"], 1)
                elif kind == "ffn":
                    act.preload_act_table(ACT.Silu)

                    def step(f, b, more=True, first=False):
                        if more:
                            for n in range(2):
                                s = SLOT_FF + n
                                high(s, 2 * (1 - b) + n, 16 * (g(f"slot{s}") + f + 1))
                        act.wait_ge(sem["up_done"], g("up_done") + f + 1)
                        act.activation(silu_g[:, b, :], B(b, 0, 256), ACT.Silu).then_inc(sem["silu_ready"], 1)
                        if not first:
                            act.wait_ge(sem["down_done"], g("down_done") + f)
                        high(SLOT_FF + 2, PART_DOWN, 16 * (g(f"slot{SLOT_FF + 2}") + f + 1))
                        act.wait_ge(sem["mid"], g("mid") + f + 1)
                        copy(mid_hi[:, b, :], mid[:, b, :]).then_inc(sem["mid_high"], 1)

                    step(0, 0, first=True)
                    step(1, 1)
                    with act.Fori(1, NF // 2 - 1) as i:
                        for b in range(2):
                            step(2 * i + b, b)
                    step(NF - 2, 0)
                    step(NF - 1, 1, more=False)
                elif kind == "ple":
                    act.wait_ge(sem["ple_t"], g("ple_t") + 1)
                    if ph["layer"] + 1 < DEPTH:
                        load_p(ph["layer"] + 1)
                    copy(qk[:, :], B(2)).then_inc(sem["ple_tc"], 1)
                    act.preload_act_table(ACT.Sigmoid)
                    with act.Fori(0, KT // 2) as i:
                        for b in range(2):
                            s = SLOT_MIX + 4 + b
                            act.wait_ge(slot_used[s], g(f"slot{s}") + i + 2)
                            act.activation(silu_g[:, b, :], B(2 * b, 0, 256), ACT.Sigmoid)\
                               .then_inc(sem["ple_s"], 1)

        @block.vector
        def _(dve):
            def stt(out, x, scalar, y, op0=ALU.mult, op1=ALU.mult):
                return dve.scalar_tensor_tensor(out=out, in0=x, scalar=scalar, in1=y, op0=op0, op1=op1)

            dve.memset(zero[:, :], 0.0)
            dve.memset(epst[:, :], EPS)
            dve.memset(attm[:, :, :], 0.0).then_inc(consts_ready, 1)
            dve.wait_ge(x_turned, 1)
            for q in range(4):
                dve.tensor_copy(xT[:, 2 * q:2 * q + 2, :], acc[:, 2 * q:2 * q + 2, :]).then_inc(sem["x_ready"], 1)
            dve.wait_ge(params_turned, 1)
            for n, r in enumerate((P, N_B, 96, 96)):
                last = dve.tensor_copy(pcol[:, n, 0:r], B(0, P * n, P * n + r))
            last.then_inc(params_ready, 1)
            dve.wait_ge(loaded, 16 * len(loads))
            dve.tensor_tensor(lam_tmp[:, :, :, :], lam_in[:, :, 0::2, :], lam_in[:, :, 1::2, :], ALU.mult)
            dve.drain()
            dve.tensor_reduce(lam[:, :, 0:2], lam_tmp[:, :, :, :], AX, ALU.add).then_inc(small_ready, 1)
            dve.wait_ge(small_exp, 1)
            for l in range(DEPTH):
                init = 0.8 - 0.6 * math.exp(-0.3 * l)
                stt(neg_lam[:, l:l + 1], lam[:, l, 3:4], init, lam[:, l, 2:3], ALU.subtract, ALU.subtract)
                dve.tensor_scalar(da_gain[:, l:l + 1], pcol[:, 1, DA_SUB + l:DA_SUB + l + 1], 1.0 - init, None, ALU.mult)
            dve.tensor_scalar(a_neg[:, :, :], a_neg[:, :, :], -1.0, None, ALU.mult)
            for half in range(2):
                r = slice(64 * half, 64 * half + 64)
                dve.tensor_copy(skip[r, :, :], skip_all[r, :, half::2])
            dve.tensor_copy(ang[:, :], pos_i[:, :])
            dve.drain()
            dve.tensor_scalar(ang[:, :], ang[:, :], C("inv"), None, ALU.mult)
            dve.drain()
            for quarter, dst in ((0.0, turns), (0.25, ang2)):
                whole = rs
                dve.tensor_scalar(whole[:, :], ang[:, :], 0.5 / math.pi, quarter, ALU.mult, ALU.add)
                dve.drain()
                dve.tensor_scalar(whole[:, :], whole[:, :], 12582912.0, None, ALU.add)
                dve.drain()
                dve.tensor_scalar(whole[:, :], whole[:, :], -12582912.0, None, ALU.add)
                dve.drain()
                stt(dst[:, :], whole[:, :], -TWO_PI_PARTS[0], ang[:, :], ALU.mult, ALU.add)
                for part in TWO_PI_PARTS[1:]:
                    dve.drain()
                    stt(dst[:, :], whole[:, :], -part, dst[:, :], ALU.mult, ALU.add)
                dve.drain()
                dve.tensor_scalar(dst[:, :], dst[:, :], 2 * math.pi * quarter, 3.1415925, ALU.add, ALU.min)
                dve.drain()
                last = dve.tensor_scalar(dst[:, :], dst[:, :], -3.1415925, None, ALU.max)
            last.then_inc(rope_ready, 1)
            dve.wait_ge(rope_ready, 2)

            def attention(ph, at):
                att, n, l = ph["att"], ph["n"], ph["layer"]
                g = lambda k: at.get(k, 0)
                if att != "sb":
                    gains = qk_gains(att, l)
                    cos, sin = (cos1[:, :], sin1[:, :]) if att == "da" else (C("cos2"), C("sin2"))
                    mask = C("window") if att == "swa" else C("causal")

                def end_softmax(i):
                    if att == "sb":
                        for hh in range(2):
                            dve.wait_ge(sem["sb_later"], g("sb_later") + 2 * i + hh + 1)
                            dve.tensor_tensor(pr[:, hh, :], lb[:, hh, :], bank[:, 2 + hh, 0:384], ALU.subtract)\
                               .then_inc(sem["sb_la"], 1)
                        for hh in range(2):
                            dve.wait_ge(sem["sb_exp"], g("sb_exp") + 2 * i + hh + 1)
                            dve.tensor_tensor(pt[:, hh, :], pt[:, hh, :], C("past"), ALU.mult).then_inc(sem["pt_ready"], 1)
                        return
                    dve.wait_ge(sem["exps"], g("exps") + 2 * i + 2)
                    if att == "swa":
                        dve.tensor_tensor(sums[:, :], sums[:, :], esink[:, :], ALU.add)
                        dve.drain()
                    dve.reciprocal(rinv[:, :], sums[:, :])
                    dve.drain()
                    if att == "da":
                        dve.tensor_scalar(rinv[:, 2:4], rinv[:, 2:4], neg_lam[:, l:l + 1], None, ALU.mult)
                    for hh in range(1 if att == "da" else 2):
                        dve.tensor_scalar(pr[:, hh, 0:128], pr[:, hh, 0:128], rinv[:, 2 * hh:2 * hh + 1], None, ALU.mult)
                        last = dve.tensor_scalar(pr[:, hh, 128:384], pr[:, hh, 128:384], rinv[:, 2 * hh + 1:2 * hh + 2],
                                                 None, ALU.mult)
                        if att != "da":
                            last.then_inc(sem["p_ready"], 1)
                    if att == "da":
                        dve.drain()
                        stt(pr[:, 0, 0:128], pr[:, 1, 0:128], rinv[:, 2:3], pr[:, 0, 0:128], ALU.mult, ALU.add)
                        stt(pr[:, 0, 128:384], pr[:, 1, 128:384], rinv[:, 3:4], pr[:, 0, 128:384], ALU.mult, ALU.add)\
                            .then_inc(sem["p_ready"], 1)

                def end_da(i):
                    dve.wait_ge(sem["y_rs"], g("y_rs") + i + 1)
                    stt(y_sb[:, 0:256], B(1, 0, 256), da_gain[:, l:l + 1], rs[:, :]).then_inc(sem["y_ready"], 1)

                def whole(i, prior):
                    if prior is not None:
                        end_softmax(prior)
                    if i is not None and att != "sb":
                        dve.wait_ge(sem["qk_rs"], g("qk_rs") + i + 1)
                        stt(qkn[:, 0:256], B(0, 0, 256), gains[0], rs2[:, 0:256])
                        stt(qkn[:, 256:512], B(0, 256, 512), gains[1], rs2[:, 256:512]).then_inc(sem["qk_n"], 1)
                    if prior is not None and att == "da":
                        end_da(prior)
                    if i is None:
                        return
                    if att == "sb":
                        for hh in range(2):
                            z = bank[:, 2 + hh, 0:384]
                            dve.wait_ge(sem["scores"], g("scores") + 2 * i + hh + 1)
                            dve.tensor_scalar(lb[:, hh, :], z, HEAD_SCALE, None, ALU.mult).then_inc(sem["s_read"], 1)
                        dve.drain()
                        for hh in range(2):
                            dve.tensor_scalar(sm[:, hh, :], lb[:, hh, :], 0.0, None, ALU.max)
                        dve.drain()
                        for hh in range(2):
                            dve.wait_ge(sem["sb_log"], g("sb_log") + 2 * i + hh + 1)
                            dve.tensor_tensor(sm[:, hh, :], sm[:, hh, :], pr[:, hh, :], ALU.add)
                            dve.drain()
                            dve.tensor_tensor(lb[:, hh, :], lb[:, hh, :], sm[:, hh, :], ALU.subtract)
                            dve.tensor_tensor(sm[:, hh, :], sm[:, hh, :], C("past"), ALU.mult).then_inc(sem["sb_spm"], 1)
                        return
                    dve.drain()
                    two = lambda ap: ap.rearrange("p (a s) -> p a s", a=2)
                    dve.tensor_tensor(two(qkc[:, :]), two(qkn[:, :]), per_tile(cos, 2), ALU.mult)
                    dve.wait_ge(sem["qk_rot"], g("qk_rot") + i + 1)
                    dve.tensor_tensor(two(qk[:, :]), two(B(3)), per_tile(sin, 2), ALU.mult)
                    dve.drain()
                    dve.tensor_tensor(qk[:, :], qk[:, :], qkc[:, :], ALU.add).then_inc(sem["qk_ready"], 1)
                    if att == "swa":
                        dve.tensor_copy(sink_now[:, :], sinks[:, bass.ds(2 * i, 2)])
                    for hh in range(2):
                        dve.wait_ge(sem["scores"], g("scores") + 2 * i + hh + 1)
                        stt(sm[:, hh, :], bank[:, 2 + hh, 0:384], HEAD_SCALE, mask, ALU.mult, ALU.add)
                        dve.drain()
                        dve.reduce_max(mx[:, 2 * hh:2 * hh + 1], sm[:, hh, 0:128], AX)
                        dve.reduce_max(mx[:, 2 * hh + 1:2 * hh + 2], sm[:, hh, 128:384], AX)
                        dve.drain()
                        if att == "swa":
                            dve.tensor_scalar(nmx[:, 2 * hh:2 * hh + 2], mx[:, 2 * hh:2 * hh + 2], sink_now[:, hh:hh + 1],
                                              -1.0, ALU.max, ALU.mult).then_inc(sem["negmax"], 1)
                        else:
                            dve.tensor_scalar(nmx[:, 2 * hh:2 * hh + 2], mx[:, 2 * hh:2 * hh + 2], -1.0, None,
                                              ALU.mult).then_inc(sem["negmax"], 1)

                whole(0, None)
                with dve.Fori(0, n - 1) as j:
                    whole(j + 1, j)
                whole(None, n - 1)

            def low(n, part, count):
                dve.wait_ge(sem["w_high"], count)
                dve.tensor_tensor(w_lo[:, part, :], wslot[:, n, :], w_hi[:, part, :], ALU.subtract).then_inc(slot_used[n], 1)

            for kind, at, ph in phases:
                g = lambda k: at.get(k, 0)
                if kind == "norm":
                    gain = ph["gain"]
                    w = gain_of(gain)
                    if ph["split"]:
                        for n in range(2):
                            low(SLOT_FF + n, n, g("w_high") + n + 1)
                    dve.wait_ge(sem["rstd"], g("rstd") + 1)
                    shifted = gain[0] == "two"

                    def h_low(k):
                        dve.wait_ge(sem["h_high"], g("h_high") + k + 1)
                        dve.tensor_tensor(h_lo[:, k, :], hT[:, k, :], h_hi[:, k, :], ALU.subtract).then_inc(sem["h_parts"], 1)

                    if shifted:
                        for k in range(KT):
                            stt(sqT[:, k, :], xT[:, k, :], w[:, k:k + 1], rs[:, :])
                        dve.drain()
                    for k in range(KT + 2):
                        if k < KT and shifted:
                            c = 24 * gain[2] + k
                            dve.tensor_scalar(hT[:, k, :], sqT[:, k, :], mod[:, gain[1], c:c + 1], None, ALU.add)\
                               .then_inc(sem["h_ready"], 1)
                        elif k < KT:
                            stt(hT[:, k, :], xT[:, k, :], w[:, k:k + 1], rs[:, :]).then_inc(sem["h_ready"], 1)
                        if k >= 2 and ph["split"]:
                            h_low(k - 2)
                elif kind == "att":
                    attention(ph, at)
                elif kind == "ssd":
                    l, gr = ph["layer"], ph["g"]
                    tile_of = (2 * gr, 2 * gr + 1, 4 + gr, 6 + gr)
                    wcol = lambda w, j: pcol[:, 1, 32 * l + 8 * w + tile_of[j]:32 * l + 8 * w + tile_of[j] + 1]
                    for half in range(2):
                        dve.wait_ge(slot_used[1 + 2 * half], g(f"slot{1 + 2 * half}") + 2)
                        for w in range(3, -1, -1):
                            for j in (2 * half, 2 * half + 1):
                                src = B(half, 256 * (j % 2), 256 * (j % 2) + 256)
                                if w == 3:
                                    cb = CONV_B + 8 * l + tile_of[j]
                                    last = dve.tensor_scalar(conv[:, j, :], src, wcol(3, j), pcol[:, 0, cb:cb + 1], ALU.mult, ALU.add)
                                else:
                                    lag = 3 - w
                                    last = stt(conv[:, j, lag:S], src[:, 0:S - lag], wcol(w, j), conv[:, j, lag:S], ALU.mult, ALU.add)
                            if w:
                                dve.drain()
                    last.then_inc(sem["ssd_conv"], 1)
                    u, ab, e, ln, m, dt, lost, da = (dts[:, n, :] for n in range(8))
                    dve.wait_ge(slot_used[SLOT_SMALL], g(f"slot{SLOT_SMALL}") + 2)
                    halves4 = lambda ap: ap.rearrange("p (t h) -> p t h", t=TT)
                    dve.tensor_tensor(halves4(u), halves4(B(3, 0, 8)), per_tile(dt_bias[:, l, 4 * gr:4 * gr + 4], 2), ALU.add)\
                       .then_inc(sem["ssd_u"], 1)
                    dve.drain()
                    dve.tensor_scalar(m, u, 0.0, None, ALU.max)
                    dve.wait_ge(sem["ssd_ln"], g("ssd_ln") + 1)
                    dve.tensor_scalar(dt, e, 1.0, None, ALU.add)
                    dve.drain()
                    stt(lost, dt, 1.0, e, ALU.subtract, ALU.subtract)
                    dve.reciprocal(ab, dt)
                    dve.tensor_tensor(m, m, ln, ALU.add)
                    dve.drain()
                    dve.tensor_tensor(lost, lost, ab, ALU.mult)
                    dve.drain()
                    dve.tensor_tensor(dt, m, lost, ALU.subtract)
                    dve.drain()
                    dve.tensor_tensor(halves4(da), halves4(dt), per_tile(a_neg[:, l, 4 * gr:4 * gr + 4], 2), ALU.mult)\
                       .then_inc(sem["ssd_da"], 1)
                    dve.wait_ge(sem["ssd_cum"], g("ssd_cum") + 1)
                    dve.tensor_copy(cum[:, :], B(3, 16, 24)).then_inc(sem["ssd_cumc"], 1)
                    dve.drain()
                    dve.tensor_tensor(wend[:, :].unsqueeze(2), B(0).rearrange("p (h s) -> p h s", h=4)[:, :, P - 1:P],
                                      cum[:, 0:4].unsqueeze(2), ALU.subtract)
                    for t in range(TT):
                        for h in range(4):
                            last = dve.tensor_scalar(dif[:, t, P * h:P * h + P], B(t, P * h, P * h + P),
                                                     cum[:, 4 * t + h:4 * t + h + 1], 0.0, ALU.subtract, ALU.min)
                        last.then_inc(sem["ssd_dif"], 1)
                    dve.wait_ge(sem["ssd_xtok"], g("ssd_xtok") + 1)
                    for t in range(TT):
                        dve.tensor_tensor(xdt[:, t, :, :], B(2, 256 * t, 256 * t + 256).rearrange("p (h d) -> p h d", h=4),
                                          per_head(dt[:, 4 * t:4 * t + 4], 64), ALU.mult)
                    dve.wait_ge(sem["ssd_dec"], g("ssd_dec") + 1)
                    dve.drain()
                    dve.tensor_tensor(xe[:, :, :], xdt[:, 0, :, :], per_head(wexp[:, :], 64), ALU.mult)
                    dve.wait_ge(sem["ssd_cb"], g("ssd_cb") + 1)
                    dve.tensor_copy(b_tok[:, :], B(3, 128, 256))
                    dve.tensor_tensor(cbm[:, :, :], B(3, 256, 512).rearrange("p (t s) -> p t s", t=TT),
                                      per_tile(C("upto"), TT), ALU.mult).then_inc(sem["ssd_xe"], 1)
                    dve.drain()
                    four = lambda ap: ap.rearrange("p (h s) -> p h s", h=4)
                    dve.tensor_tensor(four(mt[:, 0, :]), four(dif[:, 0, :]), per_tile(cbm[:, 0, :], 4), ALU.mult)
                    dve.wait_ge(sem["ssd_dec"], g("ssd_dec") + 2)
                    dve.tensor_tensor(four(mt[:, 1, :]), four(dif[:, 1, :]), per_tile(cbm[:, 1, :], 4), ALU.mult)
                    dve.tensor_tensor(four(ce[:, :]), four(ce[:, :]), per_tile(xbc[:, 3, P:S], 4), ALU.mult)\
                       .then_inc(sem["ssd_m"], 1)
                    dve.wait_ge(sem["ssd_st"], g("ssd_st") + 1)
                    dve.tensor_copy(prev[:, :], B(3, 256, 512)).then_inc(sem["ssd_stc"], 1)
                    dve.wait_ge(sem["ssd_y"], g("ssd_y") + 1)
                    for j in range(2):
                        c = 2 * gr + j
                        stt(y_sb[:, 256 * j:256 * j + 256], xbc[:, j, :], skip[:, l, c:c + 1], B(2, 256 * j, 256 * j + 256),
                            ALU.mult, ALU.add)
                    dve.drain()
                    dve.tensor_tensor(y_sb[:, :], y_sb[:, :], z_sb[:, :, :].rearrange("p j s -> p (j s)"), ALU.mult)\
                       .then_inc(sem["ssd_yg"], 1)
                    dve.wait_ge(sem["ssd_rs"], g("ssd_rs") + 1)
                    for j in range(2):
                        c = SSD_G + 4 * l + 2 * gr + j
                        y = y_sb[:, 256 * j:256 * j + 256]
                        last = stt(y, y, pcol[:, 0, c:c + 1], rs[:, :])
                    last.then_inc(sem["ssd_yn"], 1)
                elif kind == "gla":
                    l, gr = ph["layer"], ph["g"]
                    u, m, ls, bc = sm[:, 0, 0:256], pr[:, 0, 0:256], pr[:, 1, 0:256], rs2[:, 0:256]
                    dve.wait_ge(sem["gla_pgk"], g("gla_pgk") + 1)
                    c = B_GATE + 2 * l + gr
                    dve.tensor_scalar(u, B(3, 256, 512), pcol[:, 1, c:c + 1], None, ALU.add).then_inc(sem["gla_u"], 1)
                    dve.drain()
                    dve.tensor_scalar(m, u, 0.0, None, ALU.min)
                    dve.drain()
                    dve.wait_ge(sem["gla_ls"], g("gla_ls") + 1)
                    dve.tensor_tensor(ls, m, sm[:, 1, 0:256], ALU.subtract)
                    dve.drain()
                    dve.tensor_tensor_scan(bc, C("keep"), ls, 0.0, ALU.mult, ALU.add).then_inc(sem["gla_scan"], 1)
                    dve.drain()
                    chunks = lambda ap: ap.rearrange("p (c s) -> p c s", c=4)
                    dve.tensor_tensor(chunks(rs2[:, 256:512]), chunks(bc)[:, :, 63:64].broadcast_to([P, 4, 64]), chunks(bc),
                                      ALU.subtract).then_inc(sem["gla_ked"], 1)
                    dve.wait_ge(sem["gla_e"], g("gla_e") + 1)
                    dve.wait_ge(slot_used[1], g("slot1") + 2)
                    stt(qk[:, 0:256], B(0, 0, 256), HEAD_SCALE, sq2[:, 0:256])
                    dve.tensor_tensor(qk[:, 256:512], B(0, 256, 512), sq2[:, 256:512], ALU.mult).then_inc(sem["gla_dec"], 1)
                    dve.tensor_tensor(qkc[:, 0:256], B(0, 256, 512), qkn[:, 256:512], ALU.mult).then_inc(sem["gla_kee"], 1)
                    dve.wait_ge(sem["gla_tr"], g("gla_tr") + 1)
                    dve.tensor_copy(qkn[:, 0:256], B(2, 0, 256)).then_inc(sem["gla_kt"], 1)
                    dve.wait_ge(sem["gla_att"], g("gla_att") + 1)
                    for r in (0, 64):
                        view = lambda ap: ap[r:r + 64].rearrange("p h (t s) -> p h t s", t=TT)[:, :, :, r:r + 64]
                        tri = C("tri64")[r:r + 64].unsqueeze(1).unsqueeze(1).broadcast_to([64, 2, TT, 64])
                        last = dve.tensor_tensor(view(attm[:, :, :]), view(bank[:, 0:2, 0:256]), tri, ALU.mult)
                    last.then_inc(sem["gla_attm"], 1)
                    dve.wait_ge(sem["gla_states"], g("gla_states") + 1)
                    dve.tensor_copy(st_sb[:, 0:128], B(2, 256, 384))
                    dve.drain()
                    stt(st_sb[:, 128:256], st_sb[:, 0:128], sq2[:, 127:128], B(3, 0, 128), ALU.mult, ALU.add)
                    dve.drain()
                    stt(st_sb[:, 256:384], st_sb[:, 128:256], sq2[:, 191:192], B(2, 384, 512), ALU.mult, ALU.add)\
                        .then_inc(sem["gla_st"], 1)
                    dve.wait_ge(sem["gla_rs"], g("gla_rs") + 1)
                    two = lambda ap: ap.rearrange("p (a s) -> p a s", a=2)
                    stt(two(y_sb[:, :]), bank[:, 0:2, 256:512], pcol[:, 1, GLA_G + l:GLA_G + l + 1], two(rs2[:, :]))
                    dve.drain()
                    dve.tensor_tensor(two(y_sb[:, :]), two(y_sb[:, :]), silu_g[:, :, :], ALU.mult).then_inc(sem["gla_yn"], 1)
                elif kind == "add":
                    last, freed = ph["last"]
                    done = slot_used[int(last[4:])] if last.startswith("slot") else sem[last]
                    dve.wait_ge(done, g(last) + freed)
                    for q in range(4):
                        if ph["gate"] is None:
                            last = dve.tensor_tensor(xT[:, 2 * q:2 * q + 2, :], xT[:, 2 * q:2 * q + 2, :],
                                                     acc[:, 2 * q:2 * q + 2, :], ALU.add)
                        else:
                            l, part = ph["gate"]
                            for m in (2 * q, 2 * q + 1):
                                last = stt(xT[:, m, :], acc[:, m, :], mod[:, l, 8 * part + m:8 * part + m + 1], xT[:, m, :],
                                           ALU.mult, ALU.add)
                        last.then_inc(sem["x_ready"], 1)
                elif kind == "ffn":
                    ada = ph["ada"]

                    def ada_unit(i, n, waits):
                        s = SLOT_ADA + n
                        for j in range(2):
                            k = 2 * n + j
                            dve.drain()
                            if j == 0:
                                dve.wait_ge(slot_full[s], 16 * (g(f"slot{s}") + i + 1))
                            w, c = wslot[:, s, ADA_BLOCK * j:ADA_BLOCK * j + ADA_BLOCK], c_act[:, k:k + 1]
                            if k == 0:
                                last = dve.tensor_scalar(ada_part[:, :], w, c, None, ALU.mult)
                            else:
                                if k == KT - 1 and waits:
                                    ada_store(i - 1)
                                last = stt((ada_rows if k == KT - 1 else ada_part)[:, :], w, c, ada_part[:, :], ALU.mult, ALU.add)
                        last.then_inc(slot_used[s], 1)

                    def ada_store(block):
                        dve.wait_ge(sem["ada_sums"], g("ada_sums") + block + 1)
                        c = ADA_SLOTS * block
                        dve.tensor_tensor(mod[:, ada, bass.ds(c, ADA_SLOTS)], B(3, 0, ADA_SLOTS),
                                          ada_bias[:, ada // 2, bass.ds(48 * (ada % 2) + c, ADA_SLOTS)], ALU.add)

                    def step(f, b, i, more=True, waits=True):
                        count = g("w_high") - 1
                        if more:
                            for n, what in enumerate(("gate", "up")):
                                low(SLOT_FF + n, 2 * (1 - b) + n, count + split_index(what, f + 1))
                        dve.wait_ge(sem["silu_ready"], g("silu_ready") + f + 1)
                        dve.tensor_tensor(mid[:, b, :], silu_g[:, b, :], B(b, 256, 512), ALU.mult).then_inc(sem["mid"], 1)
                        low(SLOT_FF + 2, PART_DOWN, count + split_index("down", f))
                        dve.wait_ge(sem["mid_high"], g("mid_high") + f + 1)
                        dve.tensor_tensor(mid_lo[:, b, :], mid[:, b, :], mid_hi[:, b, :], ALU.subtract).then_inc(sem["mid_ready"], 1)
                        if ada is not None:
                            for n in range(2 * b, 2 * b + 2):
                                ada_unit(i, n, waits)

                    for b in range(2):
                        step(b, b, 0, waits=False)
                    with dve.Fori(1, NF // 2 - 1) as i:
                        for b in range(2):
                            step(2 * i + b, b, i)
                    step(NF - 2, 0, NF // 2 - 1)
                    step(NF - 1, 1, NF // 2 - 1, more=False)
                    if ada is not None:
                        for n in range(ADA_SLOTS):
                            ada_unit(ADA_BLOCKS - 1, n, True)
                        ada_store(ADA_BLOCKS - 1)
                        dve.drain()
                        for n in range(2):
                            c = 32 + 8 * (2 * ada + n)
                            stt(mod_gain[:, ada, n, :], mod[:, ada, 8 + 24 * n:16 + 24 * n], 1.0, pcol[:, 0, c:c + 8], ALU.add, ALU.mult)
                elif kind == "ple":
                    with dve.Fori(0, KT // 2) as i:
                        for b in range(2):
                            s = SLOT_SMALL + 2 + b
                            dve.wait_ge(slot_used[s], g(f"slot{s}") + i + 2)
                            dve.wait_ge(sem["ple_s"], 2 * i + (g("ple_s") + b + 1))
                            dve.tensor_tensor(sqT[:, bass.ds(2 * i + b, 1), :], silu_g[:, b:b + 1, :], bank[:, 2 * b + 1:2 * b + 2, 0:256],
                                              ALU.mult).then_inc(sem["ple_d"], 1)
                    dve.drain()
                    for q in range(4):
                        dve.tensor_tensor(xT[:, 2 * q:2 * q + 2, :], xT[:, 2 * q:2 * q + 2, :], sqT[:, 2 * q:2 * q + 2, :],
                                          ALU.add).then_inc(sem["x_ready"], 1)
                elif kind == "store":
                    dve.wait_ge(x_turned, 2)
                    for t in range(TT):
                        last = dve.tensor_copy(x_rows[:, t, :], acc[:, 4 * t:4 * t + 4, :].rearrange("p m s -> p (m s)"))
                    last.then_inc(rows_ready, 1)


_INS = """x p positions attn_norm w_in da_q_norm da_k_norm da_lambda_q1 da_lambda_k1 da_lambda_q2 da_lambda_k2
da_sub_norm ssd_conv_w ssd_conv_b ssd_dt_bias ssd_a_log ssd_d ssd_norm gla_w_gate2 gla_b_gate gla_norm w_out ffn_norm
w_ffn_gate w_ffn_up w_ffn_down ple_w_proj ple_w_gate c_2 ada_w_2 ada_b_2 norm_gain_2 ffn_w_gate_2 ffn_w_up_2
ffn_w_down_2 sb_w_in_2 sb_w_out_2 moba_w_in_2 moba_qk_gain_2 moba_w_out_2 swa_w_in_2 swa_qk_gain_2 swa_sinks_2
swa_w_out_2""".split()


def kernel(**inputs):
    import numpy as _np
    import concourse.bacc as _bacc
    from concourse import mybir as _mybir
    from concourse.bass_utils import run_bass_kernel_spmd as _run

    nc = _bacc.Bacc("TRN2", target_bir_lowering=False, num_devices=1)
    arrays, aps = {}, {}
    for name in _INS:
        v = _np.ascontiguousarray(inputs[name])
        arrays[f"in_{name}_dram"] = v
        aps[name] = nc.dram_tensor(f"in_{name}_dram", v.shape, _mybir.dt.from_np(v.dtype), kind="ExternalInput").ap()
    table, cols = constants()
    table_dram = nc.inline_tensor(table, "table").ap()
    out = nc.dram_tensor("out_0_dram", (1, S, D), _mybir.dt.float32, kind="ExternalOutput").ap()
    two_stacks(nc, aps, table_dram, cols, out)
    r = _run(nc, [arrays], core_ids=[0])
    return r.results[0]["out_0_dram"]
```

```python
import math
from contextlib import ExitStack

import numpy as np
import concourse.bass as bass
from concourse import mybir

F32 = mybir.dt.float32
F32R = mybir.dt.float32r
BF16 = mybir.dt.bfloat16
I32 = mybir.dt.int32
ALU = mybir.AluOpType
ACT = mybir.ActivationFunctionType
AX = mybir.AxisListType.X

P = 128
D = 1024
KT = D // P
S = 256
TT = S // P
FF = 2816
NF = FF // P
DEPTH = 2
DEPTH_2 = 4
EPS = 1e-6
BIG = 1.0e30
OFF_DA_Q, OFF_DA_K, OFF_DA_V = 0, 512, 1024
OFF_Z, OFF_X, OFF_B, OFF_C, OFF_DT = 1536, 2048, 2560, 2816, 3072
OFF_GQ, OFF_GK, OFF_GV, OFF_GG, OFF_LR = 3080, 3336, 3592, 4104, 4616
HEAD_SCALE = 64 ** -0.5
ADA_TILES = 6 * KT
TWO_PI_PARTS = (6.28125, 0.0019340515136718750, 1.2556659146e-06)


def constants():
    p = np.arange(P)
    q = np.arange(P)
    ident = np.eye(P)
    ones = np.ones((P, P))
    halves = (p[:, None] // 64 == q[None, :] // 64) * 1.0
    later = (p[:, None] > q[None, :]) * 1.0
    upto = (p[:, None] <= q[None, :]) * 1.0

    def turn(half, width):
        m = np.zeros((P, P))
        for b in range(0, P, 64):
            for d in range(half):
                m[b + d + half, b + d] = -1.0
                m[b + d, b + d + half] = 1.0
        return m

    causal = np.where(q[None, :] <= p[:, None], 0.0, -BIG)
    causal_neg = np.concatenate([causal, np.zeros((P, P)), causal], 1)
    window = np.where(q[None, :] > p[:, None], 0.0, -BIG)
    window_neg = np.concatenate([causal, window, causal], 1)
    past = (p[:, None] < q[None, :]) * 1.0
    past01 = np.concatenate([past, np.ones((P, P)), past], 1)
    keep = np.tile((np.arange(S) % 64 != 0) * 1.0, (P, 1))
    tri64 = (p[:, None] % 64 <= np.arange(64)[None, :]) * 1.0
    inv2 = (1.0 / (np.float32(10000.0) ** (np.arange(0, 64, 2, dtype=np.float32) / np.float32(64)))).astype(np.float32)
    ang = (np.arange(S, dtype=np.float32)[None, :] * inv2[p % 32][:, None]).astype(np.float32)
    cos2, sin2 = np.cos(ang.astype(np.float64)), np.sin(ang.astype(np.float64))
    inv1 = (np.float32(500000.0) ** (-np.arange(0, 16, 2, dtype=np.float32) / np.float32(16))).astype(np.float32)
    inv = np.where(p % 64 < 16, inv1[p % 8], 0.0)[:, None]
    parts = dict(ident=ident, ones=ones, halves=halves, later=later, upto=upto, turn_da=turn(8, 16),
                 turn=turn(32, 64), causal=causal_neg, window=window_neg, past=past01, keep=keep,
                 tri64=tri64, cos2=cos2, sin2=sin2, inv=inv)
    at, cols = {}, 0
    for name, a in parts.items():
        at[name] = (cols, cols + a.shape[1])
        cols += a.shape[1]
    return np.concatenate([a.astype(np.float32) for a in parts.values()], 1), at


ATT_STEP = dict(v_copied=1, pv_done=1, y_ready=1, scores=2, qk_ready=1, y_high=1)
NORMED = dict(qk_sq=1, qk_ss=1, qk_rs=1, qk_n=1, qk_rot=1, negmax=2, exps=2)
KINDS = {
    "da": dict(ATT_STEP, **NORMED, p_ready=1, p_tr=1, pt_ready=1, y_sq=1, y_ss=1, y_rs=1, y_whole=1),
    "moba": dict(ATT_STEP, **NORMED, p_ready=2, p_tr=2, pt_ready=2),
    "swa": dict(ATT_STEP, **NORMED, p_ready=2, p_tr=2, pt_ready=2),
    "sb": dict(ATT_STEP, s_read=2, sb_log=2, sb_spm=2, sb_later=2, sb_la=2, sb_exp=2, pt_ready=2),
}
SSD = dict.fromkeys("""ssd_z ssd_conv ssd_u ssd_ln ssd_da ssd_act ssd_cum ssd_cumc ssd_xtok ssd_cb ssd_xe ssd_st
                       ssd_m ssd_stc ssd_y ssd_yg ssd_sq ssd_ss ssd_rs ssd_yn""".split(), 1) | dict(ssd_dif=2, ssd_dec=2)
GLA = dict.fromkeys("""gla_lr gla_pgk gla_u gla_ls gla_scan gla_ked gla_e gla_ev gla_dec gla_kee gla_tr gla_kt gla_att
                       gla_attm gla_states gla_st gla_o gla_sq gla_ss gla_rs gla_yn""".split(), 1)
ADA_SLOTS = 4
ADA_BLOCK = ADA_SLOTS * P
ADA_BLOCKS = 6 * D // ADA_BLOCK
SLOT_MIX, SLOT_PLE, SLOT_ADA, SLOT_FF, SLOT_SMALL = 0, 2, 4, 8, 11
N_SLOTS = 15
PART_DOWN = 4
PART_LAST = 2


def split_index(what, f):
    if what == "down":
        return 3 * f + (4 if f < NF - 1 else 2) if isinstance(f, int) else 3 * f + 4
    if isinstance(f, int) and f == 0:
        return 0 if what == "gate" else 1
    return 3 * f - (1 if what == "gate" else 0)


def segments(att, n):
    if att != "swa":
        return [(0, 1, None, True, True, True), (1, n - 1, None, True, True, True), (n - 1, n, None, True, False, False)]
    half = n // 2
    return [(0, 1, 0, True, False, True), (1, half - 1, 0, False, False, True), (half - 1, half, 0, False, True, True),
            (half, half + 1, 1, True, False, True), (half + 1, n - 1, 1, False, False, True),
            (n - 1, n, 1, False, False, False)]


def schedule():
    phases, at = [], {}

    def phase(kind, counts, **more):
        phases.append((kind, dict(at), more))
        for k, v in counts.items():
            at[k] = at.get(k, 0) + v

    def slots(base, uses):
        return {f"slot{base + n}": u for n, u in enumerate(uses)}

    def split(uses):
        return {f"{k}{n}": u for n, u in enumerate(uses) for k in ("slot", "high", "unit_done")}

    def norm(split="", **more):
        counts = dict(squares=4, sumsq=1, rstd=1)
        if split != "ffn" or more["stack"] == 1:
            counts.update(h_ready=KT)
        if more["gain"][0] == "two":
            counts.update(h_scaled=KT)
        if split:
            counts.update(h_high=KT, h_parts=KT)
        if split == "ffn":
            counts.update(w_high=2, **slots(SLOT_FF, [1, 1]))
        phase("norm", counts, split=split, **more)

    def attention(kind, n, **more):
        counts = {k: v * n for k, v in KINDS[kind].items()}
        counts.update(split([n] * 4))
        if kind == "swa":
            counts.update(extra1=2, extra2=2, slot1=2, high1=2, unit_done1=2, slot2=2, v_copied=2)
        counts.update(high2=0, unit_done2=0)
        phase("att", counts, att=kind, n=n, **more)

    def add(**more):
        phase("add", dict(x_ready=4, tiles_done=3), **more)

    def ffn(ada=None, **more):
        counts = dict(silu_ready=NF, mid=NF, mid_high=NF, mid_ready=NF, up_done=NF, down_done=NF,
                      w_high=3 * NF - 2, **slots(SLOT_FF, [NF - 1, NF - 1, NF]))
        if ada is not None:
            counts.update(ada_sums=ADA_BLOCKS, ada_stored=ADA_BLOCKS, **slots(SLOT_ADA, [ADA_BLOCKS] * ADA_SLOTS))
        start = dict(at)
        phase("ffn", counts, ada=ada, **more)
        return start

    phase("setup", dict(x_ready=4))
    for l in range(DEPTH):
        norm(gain=("attn", l), split="att", att="da", layer=l)
        if l == 0:
            phase("setup_2", {})
        attention("da", 4, layer=l)
        for g in range(2):
            phase("ssd", dict(SSD, **slots(SLOT_MIX, [1] * 8), **slots(SLOT_SMALL, [1])), layer=l, g=g)
        for g in range(2):
            phase("gla", dict(GLA, **slots(SLOT_MIX, [1] * 8), **slots(SLOT_SMALL + 1, [1])), layer=l, g=g)
        add(gate=None, last=("slot7", 1))
        norm(gain=("ffn", l), split="ffn", layer=l, stack=1)
        ada_at = ffn(ada=l, layer=l, stack=1)
        add(gate=None, last=("down_done", 0))
        phase("ada_units", {}, ada=l, start=ada_at)
        phase("ple", dict(ple_t=1, ple_tc=1, ple_s=KT, ple_d=KT, x_ready=4,
                          **slots(SLOT_SMALL + 2, [4] * 2), **slots(SLOT_PLE, [4] * 2)), layer=l, start=ada_at)
        phase("ada_end", {}, ada=l, start=ada_at)
    ada_at = None
    for l in range(DEPTH_2):
        kind = ("sb", "moba", "swa")[l % 3]
        norm(gain=("two", l, 0), split="att", att=kind, layer=l)
        if ada_at:
            phase("ada_units", {}, ada=l + 1, start=ada_at)
        attention(kind, 8, layer=l)
        if ada_at:
            phase("ada_end", {}, ada=l + 1, start=ada_at)
        add(gate=(l, 2), last=("unit_done3", 0))
        norm(gain=("two", l, 1), split="ffn", layer=l, stack=2)
        ada = l + 2 if l + 2 < DEPTH_2 else None
        ada_at = ffn(ada=ada, layer=l, stack=2)
        if ada is None:
            ada_at = None
        add(gate=(l, 5), last=("down_done", 0))
    phase("store", dict())
    return phases


def two_stacks(nc, a, table_dram, cols, out):
    phases = schedule()
    ctx = ExitStack()
    with ctx:
        ctx.enter_context(nc.allow_non_contiguous_dma(reason="small parameters"))

        def sb(name, shape, dt=F32):
            return ctx.enter_context(nc.sbuf_tensor(name, shape, dt))

        const = sb("const", [P, table_dram.shape[1]])
        xT = sb("xT", [P, KT, S])
        hT = sb("hT", [P, KT, S])
        sqT = sb("sqT", [P, KT, S])
        x_rows = sb("x_rows", [P, TT, D])
        p_rows = sb("p_rows", [P, TT, 256])
        wslot = sb("wslot", [P, SLOT_SMALL, D])
        wsmall = sb("wsmall", [P, 4, 256])
        pcol = sb("pcol", [P, 4, P])
        ada_bias = pcol[:, 2:4, :]
        lam_in = sb("lam_in", [P, DEPTH, 4, 64])
        lam_tmp = sb("lam_tmp", [P, DEPTH, 2, 64])
        lam = sb("lam", [P, DEPTH, 4])
        neg_lam = sb("neg_lam", [P, DEPTH])
        da_gain = sb("da_gain", [P, DEPTH])
        dt_bias = sb("dt_bias", [P, DEPTH, 8])
        a_neg = sb("a_neg", [P, DEPTH, 8])
        wg2 = sb("wg2", [16, DEPTH, 256])
        sinks = sb("sinks", [P, 16])
        a_log = sb("a_log", [P, DEPTH, 8])
        skip_all = sb("skip_all", [P, DEPTH, 8])
        skip = sb("skip", [P, DEPTH, 4])
        c_act = sb("c_act", [P, KT])
        mod = sb("mod", [P, DEPTH_2, ADA_TILES])
        mod_gain = sb("mod_gain", [P, DEPTH_2, 2, KT])
        pos_i = sb("pos_i", [P, S], I32)
        cos1 = sb("cos1", [P, S])
        sin1 = sb("sin1", [P, S])
        rs = sb("rs", [P, S])
        head_work = sb("head_work", [P, 5, 512])
        sq2, rs2, qkn, qkc, qk = (head_work[:, n, :] for n in range(5))
        lb = head_work[:, 0:2, 0:384]
        ang, turns = qk[:, 0:256], qk[:, 256:512]
        ang2 = qkc[:, 0:256]
        ce, xdt = qk, qkc.rearrange("p (t h d) -> p t h d", t=TT, h=4)
        prow = sq2[:, :].rearrange("p (n c) -> p n c", n=4)
        v_sb = sb("v_sb", [P, TT, 256])
        sm = sb("sm", [P, 2, 384])
        pr = sb("pr", [P, 2, 384])
        pt = sb("pt", [P, 2, 384])
        mx = sb("mx", [P, 4])
        nmx = sb("nmx", [P, 4])
        sums = sb("sums", [P, 4])
        esink = sb("esink", [P, 4])
        rinv = sb("rinv", [P, 4])
        sink_now = sb("sink_now", [P, 2])
        y_sb = sb("y_sb", [P, 512])
        y_hi = sb("y_hi", [P, 512], F32R)
        y_lo = sb("y_lo", [P, 512], F32R)
        ysq = sb("ysq", [P, 512])
        ada_part, ada_rows = qkc, ysq
        conv, xbc = (x_rows[:, n, :].rearrange("p (j s) -> p j s", j=4) for n in range(2))
        z_sb = sb("z_sb", [P, 2, S])
        dts = sb("dts", [P, 8, 8])
        cum = sb("cum", [P, 8])
        xe = sb("xe", [P, 4, 64])
        b_tok = sb("b_tok", [P, P])
        cbm = sb("cbm", [P, TT, P])
        dif, mt = (sqT[:, 4 * n:4 * n + 4, :].rearrange("p (t a) s -> p t (a s)", t=TT) for n in range(2))
        wend = sb("wend", [P, 4])
        wexp = sb("wexp", [P, 4])
        prev = sb("prev", [P, 256])
        silu_g = sb("silu_g", [P, 2, S])
        mid = sb("mid", [P, 2, S])
        mid_hi = sb("mid_hi", [P, 2, S], F32R)
        mid_lo = sb("mid_lo", [P, 2, S], F32R)
        h_hi = sb("h_hi", [P, KT, S], F32R)
        h_lo = sb("h_lo", [P, KT, S], F32R)
        w_hi = sb("w_hi", [P, PART_DOWN + 1, D], F32R)
        w_lo = sb("w_lo", [P, PART_DOWN + 1, D], F32R)
        attm = sb("attm", [P, 2, S])
        st_sb = pt[:, 0, :]
        zero = sb("zero", [1, 512], BF16)
        epst = sb("epst", [P, 1])

        acc = ctx.enter_context(nc.psum_tensor("acc", [P, KT, S], F32))
        bank = ctx.enter_context(nc.psum_tensor("bank", [P, 4, 512], F32))

        names = sorted({k for _, at, _ in phases for k in at if not k.startswith(("slot", "extra", "high", "unit_done"))})
        sem = {k: ctx.enter_context(nc.semaphore(k)) for k in names}
        slot_full = [ctx.enter_context(nc.semaphore(f"slot_full{n}")) for n in range(N_SLOTS)]
        slot_used = [ctx.enter_context(nc.semaphore(f"slot_used{n}")) for n in range(N_SLOTS)]
        slot_high = [ctx.enter_context(nc.semaphore(f"slot_high{n}")) for n in range(SLOT_FF)]
        unit_done = [ctx.enter_context(nc.semaphore(f"unit_done{n}")) for n in range(SLOT_FF)]
        loaded = ctx.enter_context(nc.semaphore("loaded"))
        x_loaded = ctx.enter_context(nc.semaphore("x_loaded"))
        p_loaded = ctx.enter_context(nc.semaphore("p_loaded"))
        consts_ready = ctx.enter_context(nc.semaphore("consts_ready"))
        params_turned = ctx.enter_context(nc.semaphore("params_turned"))
        params_ready = ctx.enter_context(nc.semaphore("params_ready"))
        x_turned = ctx.enter_context(nc.semaphore("x_turned"))
        rows_ready = ctx.enter_context(nc.semaphore("rows_ready"))
        small_ready = ctx.enter_context(nc.semaphore("small_ready"))
        small_exp = ctx.enter_context(nc.semaphore("small_exp"))
        cact_ready = ctx.enter_context(nc.semaphore("cact_ready"))
        rope_ready = ctx.enter_context(nc.semaphore("rope_ready"))
        reduced = ctx.enter_context(nc.semaphore("reduced"))
        stored = ctx.enter_context(nc.semaphore("stored"))
        def C(name, lo=0, hi=None):
            b, e = cols[name]
            return const[:, b + lo:(e if hi is None else b + hi)]

        def B(n, lo=0, hi=512):
            return bank[:, n, lo:hi]

        def per_head(ap, n):
            return ap.unsqueeze(2).broadcast_to([ap.shape[0], ap.shape[1], n])

        def per_tile(ap, n):
            return ap.unsqueeze(1).broadcast_to([ap.shape[0], n, ap.shape[1]])

        def gain_of(gain):
            if gain[0] == "attn":
                return pcol[:, 0, 8 * gain[1]:8 * gain[1] + 8]
            if gain[0] == "ffn":
                return pcol[:, 0, 16 + 8 * gain[1]:24 + 8 * gain[1]]
            return mod_gain[:, gain[1], gain[2], :]

        CONV_B, C_ROW, SSD_G = 96, 112, 120
        CONV_W, B_GATE, GLA_G, DA_SUB, DA_Q, DA_K, MOBA_G, SWA_G = 0, 64, 68, 70, 72, 74, 76, 78
        N_B = 80

        def qk_gains(kind, l):
            q, k = {"da": (DA_Q + l, DA_K + l), "moba": (MOBA_G, MOBA_G + 1), "swa": (SWA_G, SWA_G + 1)}[kind]
            return pcol[:, 1, q:q + 1], pcol[:, 1, k:k + 1]

        def rows(n, lo, hi):
            return prow[lo:hi, n, :]

        def over(ap, shape):
            return ap.unsqueeze(0).broadcast_to(shape)

        def twice(ap, rows_n):
            return ap.unsqueeze(1).broadcast_to([rows_n, 2, 64])

        tiles = "l (t p) -> (l t) p"
        loads = [
            (pos_i[:, :], a["positions"][0:1, :].broadcast_to([P, S])),
            (rows(0, 0, 16), a["attn_norm"].rearrange(tiles, p=P)),
            (rows(0, 16, 32), a["ffn_norm"].rearrange(tiles, p=P)),
            (rows(0, 32, 96), a["norm_gain_2"].rearrange("l n (t p) -> (l n t) p", p=P)),
            (rows(0, CONV_B, C_ROW), a["ssd_conv_b"].rearrange(tiles, p=P)),
            (rows(0, C_ROW, SSD_G), a["c_2"].rearrange(tiles, p=P)),
            (rows(0, SSD_G, P), a["ssd_norm"].rearrange(tiles, p=P)),
            (rows(1, CONV_W, B_GATE), a["ssd_conv_w"].rearrange("l w (t p) -> (l w t) p", p=P)),
            (rows(1, B_GATE, GLA_G), a["gla_b_gate"].rearrange(tiles, p=P)),
            (rows(1, GLA_G, DA_SUB), a["gla_norm"]),
            (rows(1, DA_SUB, DA_Q), a["da_sub_norm"]),
            (rows(1, DA_Q, DA_K).rearrange("r (u d) -> r u d", u=2), twice(a["da_q_norm"], 2)),
            (rows(1, DA_K, MOBA_G).rearrange("r (u d) -> r u d", u=2), twice(a["da_k_norm"], 2)),
            (rows(1, MOBA_G, SWA_G).rearrange("r (u d) -> r u d", u=2), twice(a["moba_qk_gain_2"][0], 2)),
            (rows(1, SWA_G, N_B).rearrange("r (u d) -> r u d", u=2), twice(a["swa_qk_gain_2"][0], 2)),
        ] + [
            (rows(2 + n, 0, 96), a["ada_b_2"][2 * n:2 * n + 2].rearrange(tiles, p=P)) for n in range(2)
        ] + [
            (lam_in[:, :, n, :], over(a[name], [P, DEPTH, 64]))
            for n, name in enumerate(("da_lambda_q1", "da_lambda_k1", "da_lambda_q2", "da_lambda_k2"))
        ] + [
            (skip_all[:, :, :], over(a["ssd_d"], [P, DEPTH, 8])),
            (dt_bias[:, :, :], over(a["ssd_dt_bias"], [P, DEPTH, 8])),
            (a_log[:, :, :], over(a["ssd_a_log"], [P, DEPTH, 8])),
            (wg2[:, :, :], a["gla_w_gate2"].rearrange("l r c -> r l c")),
            (sinks[:, :], a["swa_sinks_2"][0:1, :].broadcast_to([P, 16])),
        ]

        block = ctx.enter_context(nc.Block())

        @block.sync
        def _(sp):
            def unit(w, row_tiles, col, width=P):
                return w[0:row_tiles * P, bass.ds(col, width)].rearrange("(k p) c -> p k c", p=P)

            def mix_slot(n):
                return wslot[:, n, :].rearrange("p (k c) -> p k c", k=KT)

            def load(n, dst, src, uses):
                sp.wait_ge(slot_used[n], uses)
                sp.dma_start(dst, src).then_inc(slot_full[n], 16)

            def ada_unit(ada, n, col, need):
                src = a["ada_w_2"][ada][2 * P * n:2 * P * n + 2 * P, bass.ds(col, ADA_BLOCK)]
                load(SLOT_ADA + n, wslot[:, SLOT_ADA + n, :].rearrange("p (j c) -> p j c", j=2),
                     src.rearrange("(j p) c -> p j c", p=P), need)

            def att_weights(kind, l):
                if kind == "da":
                    return a["w_in"][l], a["w_out"][l], (OFF_DA_Q, OFF_DA_K, OFF_DA_V)
                return a[kind + "_w_in_2"][l // 3], a[kind + "_w_out_2"][l // 3], (0, D, D + P if kind == "swa" else 2 * D)

            def kv_load(w, n, kv, need):
                src = unit(w, KT, D + P * (n - 1) + 64 * kv, 64)
                sp.wait_ge(slot_used[n], need)
                for half in range(2):
                    sp.dma_start(mix_slot(n)[:, :, 64 * half:64 * half + 64], src).then_inc(slot_full[n], 16)

            def ffn_weights(ph):
                names = ("w_ffn_gate", "w_ffn_up", "w_ffn_down") if ph["stack"] == 1 else \
                    ("ffn_w_gate_2", "ffn_w_up_2", "ffn_w_down_2")
                return [a[n][ph["layer"]] for n in names]

            for kind, at, ph in phases:
                u = [at.get(f"slot{n}", 0) for n in range(N_SLOTS)]
                if kind == "norm" and ph["split"] == "ffn":
                    for n, w in enumerate(ffn_weights(ph)[:2]):
                        load(SLOT_FF + n, mix_slot(SLOT_FF + n), unit(w, KT, 0), u[SLOT_FF + n] + 1)
                if kind == "norm" and ph["split"] == "att":
                    w, _, offs = att_weights(ph["att"], ph["layer"])
                    for n in range(3):
                        if ph["att"] == "swa" and n:
                            kv_load(w, n, 0, u[n] + 1)
                        else:
                            load(n, mix_slot(n), unit(w, KT, offs[n]), u[n] + 1)
                elif kind == "att":
                    w, wo, offs = att_weights(ph["att"], ph["layer"])
                    grouped = ph["att"] == "swa"
                    fresh = (0,) if grouped else range(3)
                    for lo, hi, kv, _, new_kv, more in segments(ph["att"], ph["n"]):
                        if not more:
                            load(3, wslot[:, 3, :], wo[P * lo:P * lo + P, :], lo + u[3] + 1)
                        elif hi - lo == 1:
                            for n in range(3) if new_kv else (0,):
                                if grouped and n:
                                    kv_load(w, n, kv + 1, u[n] + kv + 2)
                                else:
                                    load(n, mix_slot(n), unit(w, KT, offs[n] + P * hi), lo + u[n] + 2)
                            load(3, wslot[:, 3, :], wo[P * lo:P * lo + P, :], lo + u[3] + 1)
                        else:
                            with sp.Fori(0, hi - lo) as j:
                                col = [sp.snap(j * P + (offs[n] + P * (lo + 1))) for n in fresh]
                                row = sp.snap(j * P + P * lo)
                                need = [sp.snap(j + (lo + u[n] + 2)) for n in fresh] + [sp.snap(j + (lo + u[3] + 1))]
                                for n in fresh:
                                    load(n, mix_slot(n), unit(w, KT, col[n]), need[n])
                                load(3, wslot[:, 3, :], wo[bass.ds(row, P), :], need[-1])
                elif kind == "ssd":
                    l, g = ph["layer"], ph["g"]
                    w = a["w_in"][l]
                    for n, col in enumerate((OFF_X + 256 * g, OFF_X + 256 * g + P, OFF_B + P * g, OFF_C + P * g,
                                             OFF_Z + 256 * g, OFF_Z + 256 * g + P)):
                        load(n, mix_slot(n), unit(w, KT, col), u[n] + 1)
                    load(SLOT_SMALL, wsmall[:, 0, 0:32].rearrange("p (k c) -> p k c", k=KT),
                         unit(w, KT, OFF_DT + 4 * g, 4), u[SLOT_SMALL] + 1)
                    for n in range(2):
                        row = 512 + 256 * g + P * n
                        load(6 + n, wslot[:, 6 + n, :], a["w_out"][l][row:row + P, :], u[6 + n] + 1)
                elif kind == "gla":
                    l, g = ph["layer"], ph["g"]
                    w = a["w_in"][l]
                    load(SLOT_SMALL + 1, wsmall[:, 1, 0:P].rearrange("p (k c) -> p k c", k=KT),
                         unit(w, KT, OFF_LR, 16), u[SLOT_SMALL + 1] + 1)
                    for n, col in enumerate((OFF_GQ + P * g, OFF_GK + P * g, OFF_GV + 256 * g, OFF_GV + 256 * g + P,
                                             OFF_GG + 256 * g, OFF_GG + 256 * g + P)):
                        load(n, mix_slot(n), unit(w, KT, col), u[n] + 1)
                    for n in range(2):
                        row = 1024 + 256 * g + P * n
                        load(6 + n, wslot[:, 6 + n, :], a["w_out"][l][row:row + P, :], u[6 + n] + 1)
                elif kind == "ffn":
                    wg, wu, wd = ffn_weights(ph)
                    ada = ph["ada"]
                    g_s, u_s, d_s = SLOT_FF, SLOT_FF + 1, SLOT_FF + 2

                    def two_steps(cols, rows, need, acol, aneed):
                        for b in range(2):
                            if cols[b] is not None:
                                load(g_s, mix_slot(g_s), unit(wg, KT, cols[b]), need[b])
                                load(u_s, mix_slot(u_s), unit(wu, KT, cols[b]), need[2 + b])
                            load(d_s, wslot[:, d_s, :], wd[bass.ds(rows[b], P), :], need[4 + b])
                            if ada is not None:
                                for n in range(2 * b, 2 * b + 2):
                                    ada_unit(ada, n, acol, aneed[n])

                    base = [u[g_s], u[g_s], u[u_s], u[u_s], u[d_s], u[d_s]]
                    with sp.Fori(0, NF // 2 - 1) as i:
                        cols = [sp.snap((2 * i + b) * P + P) for b in range(2)]
                        rows = [sp.snap((2 * i + b) * P) for b in range(2)]
                        need = [sp.snap(2 * i + (base[n] + n % 2 + 1)) for n in range(6)]
                        acol = aneed = None
                        if ada is not None:
                            acol = sp.snap(i * ADA_BLOCK)
                            aneed = [sp.snap(i + u[SLOT_ADA + n] + 1) for n in range(ADA_SLOTS)]
                        two_steps(cols, rows, need, acol, aneed)
                    i = NF // 2 - 1
                    two_steps([(NF - 1) * P, None], [(NF - 2) * P, (NF - 1) * P],
                              [2 * i + base[n] + n % 2 + 1 for n in range(6)],
                              i * ADA_BLOCK, [i + u[SLOT_ADA + n] + 1 for n in range(ADA_SLOTS)])
                elif kind == "ada_units":
                    for n in range(ADA_SLOTS):
                        ada_unit(ph["ada"], n, (ADA_BLOCKS - 1) * ADA_BLOCK,
                                 ADA_BLOCKS + ph["start"].get(f"slot{SLOT_ADA + n}", 0))
                elif kind == "ple":
                    l = ph["layer"]
                    with sp.Fori(0, KT // 2) as i:
                        col = [sp.snap((2 * i + b) * P) for b in range(2)]
                        need = [sp.snap(i + u[SLOT_PLE + b] + 1) for b in range(2)]
                        sneed = [sp.snap(i + u[SLOT_SMALL + 2 + b] + 1) for b in range(2)]
                        for b in range(2):
                            load(SLOT_PLE + b, mix_slot(SLOT_PLE + b), unit(a["ple_w_gate"][l], KT, col[b]), need[b])
                            load(SLOT_SMALL + 2 + b, wsmall[:, 2 + b, :].rearrange("p (k c) -> p k c", k=2),
                                 unit(a["ple_w_proj"][l], 2, col[b]), sneed[b])
            sp.wait_ge(rows_ready, 1)
            sp.dma_start(out[0].rearrange("(t p) d -> p t d", p=P), x_rows[:, :, :]).then_inc(stored, 16)
            sp.wait_ge(stored, 16)

        @block.tensor
        def _(pe):
            for n in range(N_SLOTS):
                pe.sem_inc(slot_used[n], 1)

            def wk(n, k):
                return wslot[:, n, P * k:P * k + P]

            def feature_tile(n, dst, uses, at=None):
                pe.wait_ge(slot_full[n], uses)
                for k in range(KT):
                    if at is not None:
                        pe.wait_ge(sem["h_ready"], at + k + 1)
                    mm = pe.matmul(dst, wk(n, k), hT[:, k, :], start=(k == 0), stop=(k == KT - 1))
                mm.then_inc(slot_used[n], 1)
                return mm

            def token_tiles(n, dst, uses):
                pe.wait_ge(slot_full[n], uses)
                for t in range(TT):
                    for k in range(KT):
                        mm = pe.matmul(dst(t), hT[:, k, P * t:P * t + P], wk(n, k), start=(k == 0), stop=(k == KT - 1))
                mm.then_inc(slot_used[n], 1)

            def three(dst, w, cols, hi, lo, start, stop):
                pe.matmul(dst, w_hi[:, w, cols], hi, start=start, stop=False, skip_group_check=True)
                pe.matmul(dst, w_hi[:, w, cols], lo, start=False, stop=False, skip_group_check=True)
                return pe.matmul(dst, w_lo[:, w, cols], hi, start=False, stop=stop, skip_group_check=True)

            def ada_sum(at, block):
                s = SLOT_ADA + ADA_SLOTS - 1
                pe.wait_ge(slot_used[s], at.get(f"slot{s}", 0) + block + 2)
                pe.wait_ge(consts_ready, 1)
                for m in range(ADA_SLOTS):
                    mm = pe.matmul(B(3, m, m + 1), ada_rows[:, P * m:P * m + P], C("ones", 0, 1), start=True, stop=True)
                mm.then_inc(sem["ada_sums"], 1)

            def k_cols(k):
                return slice(P * k, P * k + P)

            def split_tile(n, part, dst, ready, first=None):
                pe.wait_ge(slot_used[n], ready)
                for k in range(KT):
                    if first is not None:
                        pe.wait_ge(sem["h_parts"], first + k + 1)
                    mm = three(dst, part, k_cols(k), h_hi[:, k, :], h_lo[:, k, :], k == 0, k == KT - 1)
                mm.then_inc(unit_done[n], 1)

            def split_out(part, last=False):
                for m in range(KT):
                    mm = three(acc[:, m, :], part, k_cols(m), y_hi[:, 0:S], y_lo[:, 0:S], False, False)
                    tile_added(mm, m, last)
                return mm

            def clear_acc():
                for m in range(4):
                    pe.matmul(acc[:, 2 * m:2 * m + 2, :].rearrange("p m s -> p (m s)"), zero[0:1, 0:P], zero[0:1, :],
                              start=True, stop=False, skip_group_check=True)

            def tile_added(mm, m, last):
                if last and m in (1, 3, 5):
                    mm.then_inc(sem["tiles_done"], 1)

            def add_out(n, y, last=False):
                for m in range(KT):
                    mm = pe.matmul(acc[:, m, :], wk(n, m), y, start=False, stop=False, skip_group_check=True)
                    tile_added(mm, m, last)
                mm.then_inc(slot_used[n], 1)

            pe.wait_ge(consts_ready, 1)
            pe.wait_ge(x_loaded, 32)
            ident = C("ident")
            for m in range(KT):
                for t in range(TT):
                    mm = pe.transpose(acc[:, m, P * t:P * t + P], x_rows[:, t, P * m:P * m + P], ident)
            mm.then_inc(x_turned, 1)
            pe.wait_ge(loaded, 16 * len(loads))
            for n, rows in enumerate((P, N_B, 96, 96)):
                mm = pe.transpose(B(2, P * n, P * n + rows), prow[0:rows, n, :], const[0:rows, cols["ident"][0]:cols["ident"][0] + rows])
            mm.then_inc(params_turned, 1)

            def attention(ph, at):
                att = ph["att"]
                n = ph["n"]
                g = lambda k: at.get(k, 0)
                normed = att != "sb"

                def proj_qk(i, ki, fresh, first):
                    h = g("h_parts") - KT if first else None
                    split_tile(0, 0, B(0, 0, 256), g("slot0") + i + 2, h)
                    if fresh:
                        split_tile(1, 1, B(0, 256, 512), g("slot1") + ki + 2)

                def scores(i):
                    pe.wait_ge(sem["qk_ready"], g("qk_ready") + i + 1)
                    pe.wait_ge(consts_ready, 1)
                    for hh in range(2):
                        r = slice(64 * hh, 64 * hh + 64)
                        if att == "sb":
                            pe.matmul(bank[:, 2 + hh, 0:256], qk[r, 256:384], qk[r, 0:256], start=True, stop=True)
                            mm = pe.matmul(bank[:, 2 + hh, 256:384], qk[r, 384:512], qk[r, 128:256], start=True, stop=True)
                        else:
                            pe.matmul(bank[:, 2 + hh, 0:128], qk[r, 0:128], qk[r, 256:384], start=True, stop=True)
                            mm = pe.matmul(bank[:, 2 + hh, 128:384], qk[r, 128:256], qk[r, 256:512], start=True, stop=True)
                        mm.then_inc(sem["scores"], 1)

                def middle(i):
                    if att == "sb":
                        for hh in range(2):
                            pe.wait_ge(sem["sb_spm"], g("sb_spm") + 2 * i + hh + 1)
                            pe.matmul(bank[:, 2 + hh, 0:256], C("later"), sm[:, hh, 0:256], start=True, stop=False)
                            pe.matmul(bank[:, 2 + hh, 128:256], C("ones"), sm[:, hh, 256:384], start=False, stop=True)
                            pe.matmul(bank[:, 2 + hh, 256:384], C("later"), sm[:, hh, 256:384], start=True, stop=True)\
                                .then_inc(sem["sb_later"], 1)
                        return
                    heads = 1 if att == "da" else 2
                    for hh in range(heads):
                        pe.wait_ge(sem["p_ready"], g("p_ready") + heads * i + hh + 1)
                        for b in range(3):
                            mm = pe.transpose(bank[:, 2 + hh, P * b:P * b + P], pr[:, hh, P * b:P * b + P], ident)
                        mm.then_inc(sem["p_tr"], 1)

                y_bank = 1 if att == "da" else 3

                def values(i, vi):
                    heads = 1 if att == "da" else 2
                    width = P // heads
                    pe.wait_ge(sem["v_copied"], g("v_copied") + vi + 1)
                    pe.wait_ge(sem["pt_ready"], g("pt_ready") + heads * i + heads)
                    pe.wait_ge(consts_ready, 1)
                    for hh in range(heads):
                        c = slice(width * hh, width * hh + width)
                        pe.matmul(bank[c, y_bank, 0:256], v_sb[:, 0, c], pt[:, hh, 0:256], start=True, stop=False)
                        mm = pe.matmul(bank[c, y_bank, 128:256], v_sb[:, 1, c], pt[:, hh, 256:384], start=False, stop=True)
                    mm.then_inc(sem["pv_done"], 1)

                def proj_v(i, t):
                    if t == 0:
                        loads = 32 if att == "swa" else 16
                        pe.wait_ge(slot_full[2], 16 * (g("slot2") + g("extra2")) + loads * (i + 1))
                        if isinstance(i, int):
                            pe.wait_ge(sem["h_ready"], g("h_ready"))
                    for k in range(KT):
                        mm = pe.matmul(B(1, 256 + P * t, 384 + P * t), hT[:, k, P * t:P * t + P], wk(2, k),
                                       start=(k == 0), stop=(k == KT - 1))
                    if t == 1:
                        mm.then_inc(slot_used[2], 1)

                def norm_sums(i, width):
                    pe.wait_ge(sem["qk_sq"], g("qk_sq") + i + 1)
                    pe.matmul(B(2, 0, width), C("halves"), sq2[:, 0:width], start=True, stop=True).then_inc(sem["qk_ss"], 1)

                def out_sums(i):
                    pe.wait_ge(sem["y_sq"], g("y_sq") + i + 1)
                    pe.matmul(B(2, 0, 256), C("ones"), ysq[:, 0:256], start=True, stop=True).then_inc(sem["y_ss"], 1)

                def out(i, last=False):
                    pe.wait_ge(slot_used[3], g("slot3") + i + 2)
                    pe.wait_ge(sem["y_ready"], g("y_ready") + i + 1)
                    split_out(PART_DOWN, last).then_inc(unit_done[3], 1)

                def whole(i, prior, kv, fresh, new_kv, more):
                    ki = i if kv is None else kv
                    vi = prior if kv is None else kv - 1 if fresh else kv
                    width = 512 if fresh else 256
                    proj_qk(i, ki, fresh, prior is None)
                    if prior is not None:
                        middle(prior)
                        if fresh:
                            pe.wait_ge(sem["v_copied"], g("v_copied") + ki)
                    if fresh:
                        proj_v(ki, 0)
                    if normed:
                        if prior is not None:
                            heads = 1 if att == "da" else 2
                            pe.wait_ge(sem["pt_ready"], g("pt_ready") + heads * prior + 1)
                        norm_sums(i, width)
                    if prior is not None and att != "da":
                        values(prior, vi)
                    if fresh:
                        proj_v(ki, 1)
                    if prior is not None and att == "da":
                        values(prior, vi)
                    if normed:
                        pe.wait_ge(sem["qk_n"], g("qk_n") + i + 1)
                        pe.matmul(B(0, 0, width), C("turn_da" if att == "da" else "turn"), qkn[:, 0:width], start=True, stop=True)\
                            .then_inc(sem["qk_rot"], 1)
                    if prior is not None:
                        if att == "da":
                            out_sums(prior)
                        else:
                            out(prior)
                    if att == "da" and prior is not None:
                        pe.wait_ge(sem["y_rs"], g("y_rs") + prior + 1)
                    scores(i)
                    if att == "da" and prior is not None:
                        out(prior)

                for lo, hi, *seg in segments(att, ph["n"]):
                    if hi - lo == 1:
                        whole(lo, lo - 1 if lo else None, *seg)
                    else:
                        with pe.Fori(0, hi - lo) as j:
                            whole(j + lo, j + (lo - 1), *seg)
                last = n - 1
                middle(last)
                values(last, 1 if att == "swa" else last)
                if att == "da":
                    pe.wait_ge(sem["pt_ready"], g("pt_ready") + n)
                    out_sums(last)
                out(last, att != "da")

            for kind, at, ph in phases:
                g = lambda k: at.get(k, 0)
                full = lambda n: 16 * (g(f"slot{n}") + g(f"extra{n}") + 1)
                if kind == "norm":
                    for k in range(KT):
                        if k % 2 == 0:
                            pe.wait_ge(sem["squares"], g("squares") + k // 2 + 1)
                        mm = pe.matmul(B(0, 0, 256), C("ones"), sqT[:, k, :], start=(k == 0), stop=(k == KT - 1))
                    mm.then_inc(sem["sumsq"], 1)
                    clear_acc()
                elif kind == "att":
                    attention(ph, at)
                elif kind == "ssd":
                    if ph["g"] == 0:
                        for n in range(2):
                            feature_tile(n, B(0, 256 * n, 256 * n + 256), full(n))

                    for n in range(2):
                        feature_tile(2 + n, B(1, 256 * n, 256 * n + 256), full(2 + n))

                    pe.wait_ge(slot_full[SLOT_SMALL], full(SLOT_SMALL))
                    for t in range(TT):
                        for k in range(KT):
                            mm = pe.matmul(B(3, 4 * t, 4 * t + 4), hT[:, k, P * t:P * t + P], wsmall[:, 0, 4 * k:4 * k + 4],
                                           start=(k == 0), stop=(k == KT - 1))
                    mm.then_inc(slot_used[SLOT_SMALL], 1)

                    pe.wait_ge(sem["ssd_da"], g("ssd_da") + 1)
                    da = dts[:, 7, :]
                    pe.matmul(B(3, 16, 24), C("upto"), da, start=True, stop=True)
                    for t in range(TT):
                        for h in range(4):
                            i = 4 * t + h
                            mm = pe.matmul(B(t, P * h, P * h + P), da[:, i:i + 1].broadcast_to([P, P]), C("upto"),
                                           start=True, stop=True)
                    mm.then_inc(sem["ssd_cum"], 1)
                    pe.wait_ge(sem["ssd_act"], g("ssd_act") + 1)
                    for t in range(TT):
                        for j in range(2):
                            mm = pe.transpose(B(2, 256 * t + P * j, 256 * t + P * j + P), xbc[:, j, P * t:P * t + P], ident)
                    mm.then_inc(sem["ssd_xtok"], 1)
                    pe.wait_ge(sem["ssd_cumc"], g("ssd_cumc") + 1)
                    pe.transpose(B(3, 128, 256), xbc[:, 2, 0:P], ident)
                    for t in range(TT):
                        mm = pe.matmul(B(3, 256 + P * t, 384 + P * t), xbc[:, 2, P * t:P * t + P], xbc[:, 3, P * t:P * t + P],
                                       start=True, stop=True)
                    mm.then_inc(sem["ssd_cb"], 1)
                    pe.wait_ge(sem["ssd_dif"], g("ssd_dif") + 1)
                    for n in range(2):
                        feature_tile(4 + n, B(0, 256 * n, 256 * n + 256), full(4 + n))
                    pe.wait_ge(sem["ssd_xe"], g("ssd_xe") + 1)
                    pe.matmul(B(3, 256, 512), b_tok[:, :], xe[:, :, :].rearrange("p h d -> p (h d)"), start=True, stop=True)\
                        .then_inc(sem["ssd_st"], 1)
                    pe.wait_ge(sem["ssd_m"], g("ssd_m") + 1)
                    pe.wait_ge(sem["ssd_stc"], g("ssd_stc") + 1)
                    for h in range(4):
                        j, r = h // 2, slice(64 * (h % 2), 64 * (h % 2) + 64)
                        for t in range(TT):
                            mm = pe.matmul(bank[r, 2, 256 * j + P * t:256 * j + P * t + P], xdt[:, t, h, :],
                                           mt[:, t, P * h:P * h + P], start=True, stop=(t == 0))
                        mm = pe.matmul(bank[r, 2, 256 * j + P:256 * j + 256], prev[:, 64 * h:64 * h + 64],
                                       ce[:, P * h:P * h + P], start=False, stop=True)
                    mm.then_inc(sem["ssd_y"], 1)
                    pe.wait_ge(sem["ssd_z"], g("ssd_z") + 1)
                    feature_tile(0, B(0, 0, 256), full(0) + 16)
                    pe.wait_ge(sem["ssd_sq"], g("ssd_sq") + 1)
                    for j in range(2):
                        mm = pe.matmul(B(3, 0, 256), C("ones"), ysq[:, 256 * j:256 * j + 256], start=(j == 0), stop=(j == 1))
                    mm.then_inc(sem["ssd_ss"], 1)
                    feature_tile(1, B(0, 256, 512), full(1) + 16)
                    pe.wait_ge(sem["ssd_yn"], g("ssd_yn") + 1)
                    for j in range(2):
                        pe.wait_ge(slot_full[6 + j], full(6 + j))
                        add_out(6 + j, y_sb[:, 256 * j:256 * j + 256])
                elif kind == "gla":
                    gg = ph["g"]
                    pe.wait_ge(slot_full[SLOT_SMALL + 1], full(SLOT_SMALL + 1))
                    for k in range(KT):
                        mm = pe.matmul(bank[0:16, 3, 0:256], wsmall[:, 1, 16 * k:16 * k + 16], hT[:, k, :],
                                       start=(k == 0), stop=(k == KT - 1))
                    mm.then_inc(slot_used[SLOT_SMALL + 1], 1)

                    if gg == 1:
                        for n in range(2):
                            feature_tile(n, B(0, 256 * n, 256 * n + 256), full(n))

                    pe.wait_ge(sem["gla_lr"], g("gla_lr") + 1)
                    pe.matmul(B(3, 256, 512), wg2[0:16, ph["layer"], P * gg:P * gg + P], qkc[0:16, 0:256],
                              start=True, stop=True).then_inc(sem["gla_pgk"], 1)
                    for n in range(2):
                        token_tiles(2 + n, lambda t: B(1, 256 * t + P * n, 256 * t + P * n + P), full(2 + n))

                    for n in range(2):
                        feature_tile(4 + n, B(2, 256 * n, 256 * n + 256), full(4 + n))

                    pe.wait_ge(sem["gla_kee"], g("gla_kee") + 1)
                    pe.wait_ge(sem["gla_ev"], g("gla_ev") + 1)
                    for t in range(TT):
                        mm = pe.transpose(B(2, P * t, P * t + P), qkc[:, P * t:P * t + P], ident)
                    mm.then_inc(sem["gla_tr"], 1)
                    pe.wait_ge(sem["gla_dec"], g("gla_dec") + 1)
                    for c in range(4):
                        t, r = c // 2, slice(64 * (c % 2), 64 * (c % 2) + 64)
                        for hh in range(2):
                            d = slice(64 * hh, 64 * hh + 64)
                            mm = pe.matmul(bank[r, hh, P * t + r.start:P * t + r.stop], qk[d, 256 + 64 * c:320 + 64 * c],
                                           qk[d, 64 * c:64 * c + 64], start=True, stop=True)
                    mm.then_inc(sem["gla_att"], 1)
                    pe.wait_ge(sem["gla_kt"], g("gla_kt") + 1)
                    for c in range(3):
                        t, r = c // 2, slice(64 * (c % 2), 64 * (c % 2) + 64)
                        for hh in range(2):
                            d = slice(64 * hh, 64 * hh + 64)
                            dst = bank[d, 3, 0:P] if c == 1 else bank[d, 2, 256 + 64 * c:384 + 64 * c]
                            mm = pe.matmul(dst, qkn[r, P * t + d.start:P * t + d.stop], v_sb[r, t, P * hh:P * hh + P],
                                           start=True, stop=True)
                    mm.then_inc(sem["gla_states"], 1)
                    pe.wait_ge(sem["gla_attm"], g("gla_attm") + 1)
                    pe.wait_ge(sem["gla_st"], g("gla_st") + 1)
                    st = st_sb
                    for hh in range(2):
                        d = slice(64 * hh, 64 * hh + 64)
                        for t in range(TT):
                            pe.matmul(bank[:, hh, 256 + P * t:384 + P * t], v_sb[:, t, P * hh:P * hh + P], attm[:, hh, P * t:P * t + P],
                                      start=True, stop=False)
                            for c in ((1,) if t == 0 else (2, 3)):
                                mm = pe.matmul(bank[:, hh, 256 + 64 * c:320 + 64 * c], st[d, P * (c - 1):P * c],
                                               qk[d, 64 * c:64 * c + 64], start=False, stop=(c != 2))
                    mm.then_inc(sem["gla_o"], 1)
                    pe.wait_ge(sem["gla_sq"], g("gla_sq") + 1)
                    pe.matmul(B(2), C("ones"), ysq[:, :], start=True, stop=True).then_inc(sem["gla_ss"], 1)
                    pe.wait_ge(sem["gla_yn"], g("gla_yn") + 1)
                    for j in range(2):
                        pe.wait_ge(slot_full[6 + j], full(6 + j))
                        add_out(6 + j, y_sb[:, 256 * j:256 * j + 256], last=(gg == 1 and j == 1))
                elif kind == "ffn":
                    ada = ph["ada"]

                    def up(f, b, first=False):
                        for n in range(2):
                            s = SLOT_FF + n
                            pe.wait_ge(slot_used[s], g(f"slot{s}") + f + 1)
                            for k in range(KT):
                                if first and n == 0:
                                    pe.wait_ge(sem["h_parts"], g("h_parts") - KT + k + 1)
                                mm = three(B(b, 256 * n, 256 * n + 256), 2 * b + n, slice(P * k, P * k + P),
                                           h_hi[:, k, :], h_lo[:, k, :], k == 0, k == KT - 1)
                        mm.then_inc(sem["up_done"], 1)

                    def down(f, b, part=PART_DOWN, last=False):
                        s = SLOT_FF + 2
                        pe.wait_ge(slot_used[s], g(f"slot{s}") + f + 2)
                        pe.wait_ge(sem["mid_ready"], g("mid_ready") + f + 1)
                        for m in range(KT):
                            mm = three(acc[:, m, :], part, slice(P * m, P * m + P), mid_hi[:, b, :], mid_lo[:, b, :],
                                       False, False)
                            tile_added(mm, m, last)
                        mm.then_inc(sem["down_done"], 1)

                    def two_chunks(i, block):
                        up(2 * i + 1, 1)
                        if block is not None and ada is not None:
                            ada_sum(at, block)
                        down(2 * i, 0)
                        up(2 * i + 2, 0)
                        down(2 * i + 1, 1)

                    up(0, 0, first=True)
                    two_chunks(0, None)
                    with pe.Fori(1, NF // 2 - 1) as i:
                        two_chunks(i, i - 1)
                    up(NF - 1, 1)
                    if ada is not None:
                        ada_sum(at, NF // 2 - 2)
                    down(NF - 2, 0)
                    down(NF - 1, 1, PART_LAST, last=True)
                    if ada is not None:
                        ada_sum(at, NF // 2 - 1)
                elif kind == "ada_end":
                    if at.get("ple_d"):
                        pe.wait_ge(sem["ple_d"], at["ple_d"])
                    ada_sum(ph["start"], ADA_BLOCKS - 1)

                elif kind == "ple":
                    l = ph["layer"]
                    pe.wait_ge(p_loaded, 16 * (l + 1))
                    for kk in range(2):
                        for t in range(TT):
                            mm = pe.transpose(B(2, 256 * kk + P * t, 256 * kk + P * t + P), p_rows[:, t, P * kk:P * kk + P], ident)
                    mm.then_inc(sem["ple_t"], 1)
                    pe.wait_ge(sem["x_ready"], g("x_ready"))
                    pe.wait_ge(sem["ple_tc"], g("ple_tc") + 1)

                    def ple_tile(i, b, reused):
                        if reused:
                            pe.wait_ge(sem["ple_d"], 2 * i + (g("ple_d") + b - 1))
                        s = SLOT_PLE + b
                        pe.wait_ge(slot_full[s], 16 * (g(f"slot{s}") + i + 1))
                        for k in range(KT):
                            mm = pe.matmul(B(2 * b, 0, 256), wk(s, k), xT[:, k, :], start=(k == 0),
                                           stop=(k == KT - 1))
                        mm.then_inc(slot_used[s], 1)
                        s = SLOT_SMALL + 2 + b
                        pe.wait_ge(slot_full[s], 16 * (g(f"slot{s}") + i + 1))
                        for k in range(2):
                            mm = pe.matmul(B(2 * b + 1, 0, 256), wsmall[:, 2 + b, P * k:P * k + P],
                                           qk[:, 256 * k:256 * k + 256], start=(k == 0), stop=(k == 1))
                        mm.then_inc(slot_used[s], 1)

                    ple_tile(0, 0, False)
                    pe.wait_ge(sem["ada_stored"], ph["start"].get("ada_stored", 0) + ADA_BLOCKS - 1)
                    ple_tile(0, 1, False)
                    with pe.Fori(1, KT // 2) as i:
                        for b in range(2):
                            ple_tile(i, b, True)
                elif kind == "store":
                    pe.wait_ge(sem["x_ready"], g("x_ready"))
                    for t in range(TT):
                        for m in range(KT):
                            mm = pe.transpose(acc[:, 4 * t + m // 2, P * (m % 2):P * (m % 2) + P], xT[:, m, P * t:P * t + P], ident)
                    mm.then_inc(x_turned, 1)

        @block.scalar
        def _(act):
            act.dma_start(x_rows[:, :, :], a["x"][0].rearrange("(t p) d -> p t d", p=P)).then_inc(x_loaded, 16)
            act.dma_start(const[:, :], table_dram).then_inc(x_loaded, 16)
            for dst, src in loads:
                act.dma_start(dst, src).then_inc(loaded, 16)

            def copy(dst, src):
                return act.activation(dst, src, ACT.Copy)

            def inverse_root(dst, src, n):
                act.activation(dst, src, ACT.Ln, scale=1.0 / n, bias=epst[:, 0:1])
                act.drain()
                return act.activation(dst, dst, ACT.Exp, scale=-0.5)

            def log_one_plus_exp(tmp, src, scale=1.0):
                act.activation(tmp, src, ACT.Abs, scale=scale)
                act.drain()
                act.activation(tmp, tmp, ACT.Exp, scale=-1.0)
                act.drain()
                return act.activation(tmp, tmp, ACT.Ln, bias=1.0)

            def load_p(l):
                act.dma_start(p_rows[:, :, :], a["p"][l, 0].rearrange("(t p) d -> p t d", p=P)).then_inc(p_loaded, 16)

            LN_EXP = "natural_log_exp_and_others"
            act.wait_ge(x_turned, 1)
            load_p(0)

            def mix_high(n, part, loads):
                act.wait_ge(slot_full[n], loads)
                copy(w_hi[:, part, :], wslot[:, n, :]).then_inc(slot_high[n], 1)

            def unit_loads(at, att, n, i):
                return 16 * (at.get(f"slot{n}", 0) + at.get(f"extra{n}", 0)) + (32 if att == "swa" and n == 1 else 16) * (i + 1)

            def attention(ph, at):
                att = ph["att"]
                g = lambda k: at.get(k, 0)
                mix_full = lambda n, i: unit_loads(at, att, n, i)
                heads = 1 if att == "da" else 2

                def whole(i, prior, kv, fresh, new_kv, more):
                    ki = i if kv is None else kv
                    width = 512 if fresh else 256
                    if i is not None:
                        last = 1 if fresh else 0
                        act.wait_ge(unit_done[last], g(f"unit_done{last}") + (ki if fresh else i) + 1)
                        if att == "sb":
                            copy(qk[:, :], B(0)).then_inc(sem["qk_ready"], 1)
                        else:
                            act.activation(sq2[:, 0:width], B(0, 0, width), ACT.Square).then_inc(sem["qk_sq"], 1)
                    if prior is not None:
                        for hh in range(heads):
                            if att == "sb":
                                act.wait_ge(sem["sb_la"], g("sb_la") + 2 * prior + hh + 1)
                                act.activation(pt[:, hh, :], pr[:, hh, :], ACT.Exp).then_inc(sem["sb_exp"], 1)
                            else:
                                act.wait_ge(sem["p_tr"], g("p_tr") + heads * prior + hh + 1)
                                copy(pt[:, hh, :], bank[:, 2 + hh, 0:384]).then_inc(sem["pt_ready"], 1)
                    if i is not None and att != "sb":
                        act.wait_ge(sem["qk_ss"], g("qk_ss") + i + 1)
                        inverse_root(rs2[:, 0:width], B(2, 0, width), 64).then_inc(sem["qk_rs"], 1)
                    if prior is not None:
                        act.wait_ge(sem["pv_done"], g("pv_done") + prior + 1)
                        if att == "da":
                            act.activation(ysq[:, 0:256], B(1, 0, 256), ACT.Square).then_inc(sem["y_sq"], 1)
                        else:
                            copy(y_hi[:, 0:256], B(3, 0, 256)).then_inc(sem["y_high"], 1)
                    if i is not None and fresh:
                        act.wait_ge(slot_used[2], g("slot2") + ki + 2)
                        copy(v_sb[:, :, 0:P], B(1, 256, 512).rearrange("p (t d) -> p t d", t=TT)).then_inc(sem["v_copied"], 1)
                    if prior is not None and att == "da":
                        act.wait_ge(sem["y_ss"], g("y_ss") + prior + 1)
                        inverse_root(rs[:, :], B(2, 0, 256), P).then_inc(sem["y_rs"], 1)
                    if i is not None and more:
                        mix_high(0, 0, mix_full(0, i + 1))
                        if new_kv:
                            mix_high(1, 1, mix_full(1, ki + 1))
                    if prior is not None and att == "da":
                        act.wait_ge(sem["y_whole"], g("y_whole") + prior + 1)
                        copy(y_hi[:, 0:256], y_sb[:, 0:256]).then_inc(sem["y_high"], 1)
                    if i is None:
                        return
                    for hh in range(2):
                        if att == "sb":
                            act.wait_ge(sem["s_read"], g("s_read") + 2 * i + hh + 1)
                            log_one_plus_exp(pr[:, hh, :], lb[:, hh, :]).then_inc(sem["sb_log"], 1)
                        else:
                            act.wait_ge(sem["negmax"], g("negmax") + 2 * i + hh + 1)
                            act.activation(pr[:, hh, 0:128], sm[:, hh, 0:128], ACT.Exp, bias=nmx[:, 2 * hh:2 * hh + 1],
                                           accum_out=sums[:, 2 * hh:2 * hh + 1])
                            if att == "swa":
                                act.activation(esink[:, 2 * hh:2 * hh + 2], nmx[:, 2 * hh:2 * hh + 2], ACT.Exp,
                                               bias=sink_now[:, hh:hh + 1])
                            act.activation(pr[:, hh, 128:384], sm[:, hh, 128:384], ACT.Exp,
                                           bias=nmx[:, 2 * hh + 1:2 * hh + 2],
                                           accum_out=sums[:, 2 * hh + 1:2 * hh + 2]).then_inc(sem["exps"], 1)
                    if prior is not None:
                        act.wait_ge(unit_done[3], g("unit_done3") + i)
                    mix_high(3, PART_DOWN, mix_full(3, i))

                for lo, hi, *seg in segments(att, ph["n"]):
                    if hi - lo == 1:
                        whole(lo, lo - 1 if lo else None, *seg)
                    else:
                        with act.Fori(0, hi - lo) as j:
                            whole(j + lo, j + (lo - 1), *seg)
                whole(None, ph["n"] - 1, None, False, False, False)

            def high(n, part, loads):
                act.wait_ge(slot_full[n], loads)
                copy(w_hi[:, part, :], wslot[:, n, :]).then_inc(sem["w_high"], 1)

            for kind, at, ph in phases:
                g = lambda k: at.get(k, 0)
                if kind == "norm":
                    act.preload_act_table_set(LN_EXP)
                    if ph["split"] == "att":
                        for n in range(2):
                            mix_high(n, n, unit_loads(at, ph["att"], n, 0))
                    if ph["split"] == "ffn":
                        for n in range(2):
                            high(SLOT_FF + n, n, 16 * (g(f"slot{SLOT_FF + n}") + 1))
                    for q in range(4):
                        act.wait_ge(sem["x_ready"], g("x_ready") - 3 + q)
                        act.activation(sqT[:, 2 * q:2 * q + 2, :], xT[:, 2 * q:2 * q + 2, :], ACT.Square)\
                           .then_inc(sem["squares"], 1)
                    act.wait_ge(sem["sumsq"], g("sumsq") + 1)
                    inverse_root(rs[:, :], B(0, 0, 256), D).then_inc(sem["rstd"], 1)
                    if ph["split"]:
                        gain = ph["gain"]
                        for k in range(KT):
                            if gain[0] == "two":
                                act.wait_ge(sem["h_scaled"], g("h_scaled") + k + 1)
                                c = 24 * gain[2] + k
                                ins = act.activation(h_hi[:, k, :], sqT[:, k, :], ACT.Identity, bias=mod[:, gain[1], c:c + 1])
                            else:
                                act.wait_ge(sem["h_ready"], g("h_ready") + k + 1)
                                ins = copy(h_hi[:, k, :], hT[:, k, :])
                            ins.then_inc(sem["h_high"], 1)
                elif kind == "setup_2":
                    act.wait_ge(small_ready, 1)
                    act.activation(lam[:, :, 2:4], lam[:, :, 0:2], ACT.Exp)
                    act.activation(a_neg[:, :, :], a_log[:, :, :], ACT.Exp).then_inc(small_exp, 1)
                    act.wait_ge(rope_ready, 1)
                    act.activation(sin1[:, :], turns[:, :], ACT.Sin)
                    act.activation(cos1[:, :], ang2[:, :], ACT.Sin).then_inc(rope_ready, 1)
                    act.wait_ge(params_ready, 1)
                    act.activation(c_act[:, :], pcol[:, 0, C_ROW:SSD_G], ACT.Silu).then_inc(cact_ready, 1)
                    act.preload_act_table_set(LN_EXP)
                elif kind == "att":
                    attention(ph, at)
                elif kind == "ssd":
                    act.wait_ge(sem["ssd_u"], g("ssd_u") + 1)
                    act.activation(dts[:, 1, :], dts[:, 0, :], ACT.Abs)
                    act.drain()
                    act.activation(dts[:, 2, :], dts[:, 1, :], ACT.Exp, scale=-1.0)
                    act.drain()
                    act.activation(dts[:, 3, :], dts[:, 2, :], ACT.Ln, bias=1.0).then_inc(sem["ssd_ln"], 1)
                    act.wait_ge(sem["ssd_conv"], g("ssd_conv") + 1)
                    act.activation(xbc[:, :, :], conv[:, :, :], ACT.Silu).then_inc(sem["ssd_act"], 1)
                    act.preload_act_table_set(LN_EXP)
                    act.wait_ge(sem["ssd_dif"], g("ssd_dif") + 1)
                    act.activation(wexp[:, :], wend[:, :], ACT.Exp)
                    act.activation(dif[:, 0, :], dif[:, 0, :], ACT.Exp).then_inc(sem["ssd_dec"], 1)
                    act.wait_ge(sem["ssd_dif"], g("ssd_dif") + 2)
                    act.activation(dif[:, 1, :], dif[:, 1, :], ACT.Exp)
                    act.activation(ce[:, :], B(1), ACT.Exp).then_inc(sem["ssd_dec"], 1)
                    act.preload_act_table(ACT.Silu)
                    act.wait_ge(slot_used[5], g("slot5") + 2)
                    act.activation(z_sb[:, :, :], B(0).rearrange("p (j s) -> p j s", j=2), ACT.Silu).then_inc(sem["ssd_z"], 1)
                    act.preload_act_table_set(LN_EXP)
                    act.wait_ge(sem["ssd_yg"], g("ssd_yg") + 1)
                    act.activation(ysq[:, :], y_sb[:, :], ACT.Square).then_inc(sem["ssd_sq"], 1)
                    act.wait_ge(sem["ssd_ss"], g("ssd_ss") + 1)
                    inverse_root(rs[:, :], B(3, 0, 256), 256).then_inc(sem["ssd_rs"], 1)
                elif kind == "gla":
                    act.wait_ge(slot_used[SLOT_SMALL + 1], g(f"slot{SLOT_SMALL + 1}") + 2)
                    copy(qkc[0:16, 0:256], bank[0:16, 3, 0:256]).then_inc(sem["gla_lr"], 1)
                    act.wait_ge(sem["gla_u"], g("gla_u") + 1)
                    log_one_plus_exp(sm[:, 1, 0:256], sm[:, 0, 0:256]).then_inc(sem["gla_ls"], 1)
                    act.wait_ge(sem["gla_scan"], g("gla_scan") + 1)
                    act.activation(sq2[:, 0:256], rs2[:, 0:256], ACT.Exp, scale=1.0 / 16)
                    act.activation(sq2[:, 256:512], rs2[:, 0:256], ACT.Exp, scale=-1.0 / 16)
                    act.wait_ge(sem["gla_ked"], g("gla_ked") + 1)
                    act.activation(qkn[:, 256:512], rs2[:, 256:512], ACT.Exp, scale=1.0 / 16).then_inc(sem["gla_e"], 1)
                    act.wait_ge(slot_used[3], g("slot3") + 2)
                    copy(v_sb[:, :, :], B(1).rearrange("p (t d) -> p t d", t=TT))
                    act.wait_ge(slot_used[5], g("slot5") + 2)
                    act.activation(silu_g[:, :, :], B(2).rearrange("p (j s) -> p j s", j=2), ACT.Silu).then_inc(sem["gla_ev"], 1)
                    act.preload_act_table_set(LN_EXP)
                    act.wait_ge(sem["gla_o"], g("gla_o") + 1)
                    act.activation(ysq[:, :].rearrange("p (j s) -> p j s", j=2), bank[:, 0:2, 256:512], ACT.Square)\
                       .then_inc(sem["gla_sq"], 1)
                    act.wait_ge(sem["gla_ss"], g("gla_ss") + 1)
                    inverse_root(rs2[:, :], B(2), P).then_inc(sem["gla_rs"], 1)
                elif kind == "ffn":
                    act.preload_act_table(ACT.Silu)

                    def step(f, b, more=True, first=False):
                        if more:
                            for n in range(2):
                                s = SLOT_FF + n
                                high(s, 2 * (1 - b) + n, 16 * (g(f"slot{s}") + f + 1))
                        act.wait_ge(sem["up_done"], g("up_done") + f + 1)
                        act.activation(silu_g[:, b, :], B(b, 0, 256), ACT.Silu).then_inc(sem["silu_ready"], 1)
                        if not first and more:
                            act.wait_ge(sem["down_done"], g("down_done") + f)
                        high(SLOT_FF + 2, PART_DOWN if more else PART_LAST, 16 * (g(f"slot{SLOT_FF + 2}") + f + 1))
                        act.wait_ge(sem["mid"], g("mid") + f + 1)
                        copy(mid_hi[:, b, :], mid[:, b, :]).then_inc(sem["mid_high"], 1)

                    step(0, 0, first=True)
                    step(1, 1)
                    with act.Fori(1, NF // 2 - 1) as i:
                        for b in range(2):
                            step(2 * i + b, b)
                    step(NF - 2, 0)
                    step(NF - 1, 1, more=False)
                elif kind == "ple":
                    act.wait_ge(sem["ple_t"], g("ple_t") + 1)
                    if ph["layer"] + 1 < DEPTH:
                        load_p(ph["layer"] + 1)
                    copy(qk[:, :], B(2)).then_inc(sem["ple_tc"], 1)
                    act.preload_act_table(ACT.Sigmoid)
                    with act.Fori(0, KT // 2) as i:
                        for b in range(2):
                            s = SLOT_PLE + b
                            act.wait_ge(slot_used[s], g(f"slot{s}") + i + 2)
                            act.activation(silu_g[:, b, :], B(2 * b, 0, 256), ACT.Sigmoid)\
                               .then_inc(sem["ple_s"], 1)

        @block.vector
        def _(dve):
            def stt(out, x, scalar, y, op0=ALU.mult, op1=ALU.mult):
                return dve.scalar_tensor_tensor(out=out, in0=x, scalar=scalar, in1=y, op0=op0, op1=op1)

            dve.memset(zero[:, :], 0.0)
            dve.memset(epst[:, :], EPS)
            dve.memset(attm[:, :, :], 0.0).then_inc(consts_ready, 1)
            dve.wait_ge(x_turned, 1)
            for q in range(4):
                dve.tensor_copy(xT[:, 2 * q:2 * q + 2, :], acc[:, 2 * q:2 * q + 2, :]).then_inc(sem["x_ready"], 1)
            dve.wait_ge(params_turned, 1)
            for n, r in enumerate((P, N_B, 96, 96)):
                last = dve.tensor_copy(pcol[:, n, 0:r], B(2, P * n, P * n + r))
            last.then_inc(params_ready, 1)
            dve.drain()

            def low_of(n, part, count):
                dve.wait_ge(slot_high[n], count)
                dve.tensor_tensor(w_lo[:, part, :], wslot[:, n, :], w_hi[:, part, :], ALU.subtract)\
                   .then_inc(slot_used[n], 1)

            def attention(ph, at):
                att, n, l = ph["att"], ph["n"], ph["layer"]
                g = lambda k: at.get(k, 0)
                mix_low = lambda n, part, i: low_of(n, part, g(f"high{n}") + i + 1)
                if att != "sb":
                    gains = qk_gains(att, l)
                    cos, sin = (cos1[:, :], sin1[:, :]) if att == "da" else (C("cos2"), C("sin2"))
                    mask = C("window") if att == "swa" else C("causal")

                def end_softmax(i):
                    if att == "sb":
                        for hh in range(2):
                            dve.wait_ge(sem["sb_later"], g("sb_later") + 2 * i + hh + 1)
                            dve.tensor_tensor(pr[:, hh, :], lb[:, hh, :], bank[:, 2 + hh, 0:384], ALU.subtract)\
                               .then_inc(sem["sb_la"], 1)
                        for hh in range(2):
                            dve.wait_ge(sem["sb_exp"], g("sb_exp") + 2 * i + hh + 1)
                            dve.tensor_tensor(pt[:, hh, :], pt[:, hh, :], C("past"), ALU.mult).then_inc(sem["pt_ready"], 1)
                        return
                    dve.wait_ge(sem["exps"], g("exps") + 2 * i + 2)
                    if att == "swa":
                        dve.tensor_tensor(sums[:, :], sums[:, :], esink[:, :], ALU.add)
                        dve.drain()
                    dve.reciprocal(rinv[:, :], sums[:, :])
                    dve.drain()
                    if att == "da":
                        dve.tensor_scalar(rinv[:, 2:4], rinv[:, 2:4], neg_lam[:, l:l + 1], None, ALU.mult)
                    for hh in range(1 if att == "da" else 2):
                        dve.tensor_scalar(pr[:, hh, 0:128], pr[:, hh, 0:128], rinv[:, 2 * hh:2 * hh + 1], None, ALU.mult)
                        last = dve.tensor_scalar(pr[:, hh, 128:384], pr[:, hh, 128:384], rinv[:, 2 * hh + 1:2 * hh + 2],
                                                 None, ALU.mult)
                        if att != "da":
                            last.then_inc(sem["p_ready"], 1)
                    if att == "da":
                        dve.drain()
                        stt(pr[:, 0, 0:128], pr[:, 1, 0:128], rinv[:, 2:3], pr[:, 0, 0:128], ALU.mult, ALU.add)
                        stt(pr[:, 0, 128:384], pr[:, 1, 128:384], rinv[:, 3:4], pr[:, 0, 128:384], ALU.mult, ALU.add)\
                            .then_inc(sem["p_ready"], 1)

                def out_low(i):
                    dve.wait_ge(sem["y_high"], g("y_high") + i + 1)
                    dve.tensor_tensor(y_lo[:, 0:256], y_sb[:, 0:256] if att == "da" else B(3, 0, 256), y_hi[:, 0:256],
                                      ALU.subtract).then_inc(sem["y_ready"], 1)

                def end_da(i):
                    dve.wait_ge(sem["y_rs"], g("y_rs") + i + 1)
                    stt(y_sb[:, 0:256], B(1, 0, 256), da_gain[:, l:l + 1], rs[:, :]).then_inc(sem["y_whole"], 1)

                def whole(i, prior, kv, fresh, new_kv, more):
                    ki = i if kv is None else kv
                    sides = 2 if fresh else 1
                    width = 256 * sides

                    def next_low():
                        mix_low(0, 0, i + 1)
                        if new_kv:
                            mix_low(1, 1, ki + 1)

                    if prior is not None:
                        end_softmax(prior)
                        mix_low(3, PART_DOWN, prior)
                    if i is not None and att != "sb":
                        dve.wait_ge(sem["qk_rs"], g("qk_rs") + i + 1)
                        for side in range(sides):
                            c = slice(256 * side, 256 * side + 256)
                            last = stt(qkn[:, c], bank[:, 0, c], gains[side], rs2[:, c])
                        last.then_inc(sem["qk_n"], 1)
                    if prior is not None and att != "da":
                        out_low(prior)
                    if i is None:
                        if att == "da":
                            end_da(prior)
                            out_low(prior)
                        return
                    if att == "sb":
                        if more:
                            next_low()
                        for hh in range(2):
                            z = bank[:, 2 + hh, 0:384]
                            dve.wait_ge(sem["scores"], g("scores") + 2 * i + hh + 1)
                            dve.tensor_scalar(lb[:, hh, :], z, HEAD_SCALE, None, ALU.mult).then_inc(sem["s_read"], 1)
                        dve.drain()
                        for hh in range(2):
                            dve.tensor_scalar(sm[:, hh, :], lb[:, hh, :], 0.0, None, ALU.max)
                        dve.drain()
                        for hh in range(2):
                            dve.wait_ge(sem["sb_log"], g("sb_log") + 2 * i + hh + 1)
                            dve.tensor_tensor(sm[:, hh, :], sm[:, hh, :], pr[:, hh, :], ALU.add)
                            dve.drain()
                            dve.tensor_tensor(lb[:, hh, :], lb[:, hh, :], sm[:, hh, :], ALU.subtract)
                            dve.tensor_tensor(sm[:, hh, :], sm[:, hh, :], C("past"), ALU.mult).then_inc(sem["sb_spm"], 1)
                        return
                    dve.drain()
                    each = lambda ap: ap.rearrange("p (a s) -> p a s", a=sides)
                    dve.tensor_tensor(each(qkc[:, 0:width]), each(qkn[:, 0:width]), per_tile(cos, sides), ALU.mult)
                    dve.wait_ge(sem["qk_rot"], g("qk_rot") + i + 1)
                    dve.tensor_tensor(each(qk[:, 0:width]), each(B(0, 0, width)), per_tile(sin, sides), ALU.mult)
                    dve.drain()
                    dve.tensor_tensor(qk[:, 0:width], qk[:, 0:width], qkc[:, 0:width], ALU.add).then_inc(sem["qk_ready"], 1)
                    if prior is not None and att == "da":
                        end_da(prior)
                    if more:
                        next_low()
                    if prior is not None and att == "da":
                        out_low(prior)
                    if att == "swa":
                        dve.tensor_copy(sink_now[:, :], sinks[:, bass.ds(2 * i, 2)])
                    for hh in range(2):
                        dve.wait_ge(sem["scores"], g("scores") + 2 * i + hh + 1)
                        stt(sm[:, hh, :], bank[:, 2 + hh, 0:384], HEAD_SCALE, mask, ALU.mult, ALU.add)
                        dve.drain()
                        dve.reduce_max(mx[:, 2 * hh:2 * hh + 1], sm[:, hh, 0:128], AX)
                        dve.reduce_max(mx[:, 2 * hh + 1:2 * hh + 2], sm[:, hh, 128:384], AX)
                        dve.drain()
                        if att == "swa":
                            dve.tensor_scalar(nmx[:, 2 * hh:2 * hh + 2], mx[:, 2 * hh:2 * hh + 2], sink_now[:, hh:hh + 1],
                                              -1.0, ALU.max, ALU.mult).then_inc(sem["negmax"], 1)
                        else:
                            dve.tensor_scalar(nmx[:, 2 * hh:2 * hh + 2], mx[:, 2 * hh:2 * hh + 2], -1.0, None,
                                              ALU.mult).then_inc(sem["negmax"], 1)

                for lo, hi, *seg in segments(att, ph["n"]):
                    if hi - lo == 1:
                        whole(lo, lo - 1 if lo else None, *seg)
                    else:
                        with dve.Fori(0, hi - lo) as j:
                            whole(j + lo, j + (lo - 1), *seg)
                whole(None, ph["n"] - 1, None, False, False, False)

            def ada_unit(at, ada, i, n, waits):
                s = SLOT_ADA + n
                for j in range(2):
                    k = 2 * n + j
                    dve.drain()
                    if j == 0:
                        dve.wait_ge(slot_full[s], 16 * (at.get(f"slot{s}", 0) + i + 1))
                    w, c = wslot[:, s, ADA_BLOCK * j:ADA_BLOCK * j + ADA_BLOCK], c_act[:, k:k + 1]
                    if k == 0:
                        last = dve.tensor_scalar(ada_part[:, :], w, c, None, ALU.mult)
                    else:
                        if k == KT - 1 and waits:
                            ada_store(at, ada, i - 1)
                        last = stt((ada_rows if k == KT - 1 else ada_part)[:, :], w, c, ada_part[:, :], ALU.mult, ALU.add)
                last.then_inc(slot_used[s], 1)

            def ada_store(at, ada, block):
                dve.wait_ge(sem["ada_sums"], at.get("ada_sums", 0) + block + 1)
                c = ADA_SLOTS * block
                dve.tensor_tensor(mod[:, ada, bass.ds(c, ADA_SLOTS)], B(3, 0, ADA_SLOTS),
                                  ada_bias[:, ada // 2, bass.ds(48 * (ada % 2) + c, ADA_SLOTS)], ALU.add)\
                   .then_inc(sem["ada_stored"], 1)

            def low(n, part, count):
                dve.wait_ge(sem["w_high"], count)
                dve.tensor_tensor(w_lo[:, part, :], wslot[:, n, :], w_hi[:, part, :], ALU.subtract).then_inc(slot_used[n], 1)

            for kind, at, ph in phases:
                g = lambda k: at.get(k, 0)
                if kind == "norm":
                    gain = ph["gain"]
                    w = gain_of(gain)
                    if ph["split"] == "att":
                        for n in range(2):
                            low_of(n, n, g(f"high{n}") + 1)
                    if ph["split"] == "ffn":
                        for n in range(2):
                            low(SLOT_FF + n, n, g("w_high") + n + 1)
                    dve.wait_ge(sem["rstd"], g("rstd") + 1)
                    shifted = gain[0] == "two"

                    shift = lambda k: mod[:, gain[1], 24 * gain[2] + k:24 * gain[2] + k + 1]

                    def h_low(k):
                        dve.wait_ge(sem["h_high"], g("h_high") + k + 1)
                        if shifted:
                            ins = stt(h_lo[:, k, :], sqT[:, k, :], shift(k), h_hi[:, k, :], ALU.add, ALU.subtract)
                        else:
                            ins = dve.tensor_tensor(h_lo[:, k, :], hT[:, k, :], h_hi[:, k, :], ALU.subtract)
                        ins.then_inc(sem["h_parts"], 1)

                    for k in range(KT + 2):
                        if k < KT:
                            stt((sqT if shifted else hT)[:, k, :], xT[:, k, :], w[:, k:k + 1], rs[:, :])\
                                .then_inc(sem["h_scaled" if shifted else "h_ready"], 1)
                        if k >= 2:
                            h_low(k - 2)
                    if shifted and ph["split"] == "att":
                        for k in range(KT):
                            dve.tensor_scalar(hT[:, k, :], sqT[:, k, :], shift(k), None, ALU.add).then_inc(sem["h_ready"], 1)
                elif kind == "setup_2":
                    dve.wait_ge(loaded, 16 * len(loads))
                    dve.tensor_tensor(lam_tmp[:, :, :, :], lam_in[:, :, 0::2, :], lam_in[:, :, 1::2, :], ALU.mult)
                    dve.drain()
                    dve.tensor_reduce(lam[:, :, 0:2], lam_tmp[:, :, :, :], AX, ALU.add).then_inc(small_ready, 1)
                    dve.wait_ge(small_exp, 1)
                    for l in range(DEPTH):
                        init = 0.8 - 0.6 * math.exp(-0.3 * l)
                        stt(neg_lam[:, l:l + 1], lam[:, l, 3:4], init, lam[:, l, 2:3], ALU.subtract, ALU.subtract)
                        dve.tensor_scalar(da_gain[:, l:l + 1], pcol[:, 1, DA_SUB + l:DA_SUB + l + 1], 1.0 - init, None, ALU.mult)
                    dve.tensor_scalar(a_neg[:, :, :], a_neg[:, :, :], -1.0, None, ALU.mult)
                    for half in range(2):
                        r = slice(64 * half, 64 * half + 64)
                        dve.tensor_copy(skip[r, :, :], skip_all[r, :, half::2])
                    dve.tensor_copy(ang[:, :], pos_i[:, :])
                    dve.drain()
                    dve.tensor_scalar(ang[:, :], ang[:, :], C("inv"), None, ALU.mult)
                    dve.drain()
                    for quarter, dst in ((0.0, turns), (0.25, ang2)):
                        whole = ysq[:, 0:256]
                        dve.tensor_scalar(whole, ang[:, :], 0.5 / math.pi, quarter, ALU.mult, ALU.add)
                        dve.drain()
                        dve.tensor_scalar(whole, whole, 12582912.0, None, ALU.add)
                        dve.drain()
                        dve.tensor_scalar(whole, whole, -12582912.0, None, ALU.add)
                        dve.drain()
                        stt(dst[:, :], whole, -TWO_PI_PARTS[0], ang[:, :], ALU.mult, ALU.add)
                        for part in TWO_PI_PARTS[1:]:
                            dve.drain()
                            stt(dst[:, :], whole, -part, dst[:, :], ALU.mult, ALU.add)
                        dve.drain()
                        dve.tensor_scalar(dst[:, :], dst[:, :], 2 * math.pi * quarter, 3.1415925, ALU.add, ALU.min)
                        dve.drain()
                        last = dve.tensor_scalar(dst[:, :], dst[:, :], -3.1415925, None, ALU.max)
                    last.then_inc(rope_ready, 1)
                    dve.wait_ge(rope_ready, 2)
                elif kind == "att":
                    attention(ph, at)
                elif kind == "ssd":
                    l, gr = ph["layer"], ph["g"]
                    tile_of = (2 * gr, 2 * gr + 1, 4 + gr, 6 + gr)
                    wcol = lambda w, j: pcol[:, 1, 32 * l + 8 * w + tile_of[j]:32 * l + 8 * w + tile_of[j] + 1]
                    for half in range(2):
                        dve.wait_ge(slot_used[1 + 2 * half], g(f"slot{1 + 2 * half}") + 2)
                        for w in range(3, -1, -1):
                            for j in (2 * half, 2 * half + 1):
                                src = B(half, 256 * (j % 2), 256 * (j % 2) + 256)
                                if w == 3:
                                    cb = CONV_B + 8 * l + tile_of[j]
                                    last = dve.tensor_scalar(conv[:, j, :], src, wcol(3, j), pcol[:, 0, cb:cb + 1], ALU.mult, ALU.add)
                                else:
                                    lag = 3 - w
                                    last = stt(conv[:, j, lag:S], src[:, 0:S - lag], wcol(w, j), conv[:, j, lag:S], ALU.mult, ALU.add)
                            if w:
                                dve.drain()
                    last.then_inc(sem["ssd_conv"], 1)
                    u, ab, e, ln, m, dt, lost, da = (dts[:, n, :] for n in range(8))
                    dve.wait_ge(slot_used[SLOT_SMALL], g(f"slot{SLOT_SMALL}") + 2)
                    halves4 = lambda ap: ap.rearrange("p (t h) -> p t h", t=TT)
                    dve.tensor_tensor(halves4(u), halves4(B(3, 0, 8)), per_tile(dt_bias[:, l, 4 * gr:4 * gr + 4], 2), ALU.add)\
                       .then_inc(sem["ssd_u"], 1)
                    dve.drain()
                    dve.tensor_scalar(m, u, 0.0, None, ALU.max)
                    dve.wait_ge(sem["ssd_ln"], g("ssd_ln") + 1)
                    dve.tensor_scalar(dt, e, 1.0, None, ALU.add)
                    dve.drain()
                    stt(lost, dt, 1.0, e, ALU.subtract, ALU.subtract)
                    dve.reciprocal(ab, dt)
                    dve.tensor_tensor(m, m, ln, ALU.add)
                    dve.drain()
                    dve.tensor_tensor(lost, lost, ab, ALU.mult)
                    dve.drain()
                    dve.tensor_tensor(dt, m, lost, ALU.subtract)
                    dve.drain()
                    dve.tensor_tensor(halves4(da), halves4(dt), per_tile(a_neg[:, l, 4 * gr:4 * gr + 4], 2), ALU.mult)\
                       .then_inc(sem["ssd_da"], 1)
                    dve.wait_ge(sem["ssd_cum"], g("ssd_cum") + 1)
                    dve.tensor_copy(cum[:, :], B(3, 16, 24)).then_inc(sem["ssd_cumc"], 1)
                    dve.drain()
                    dve.tensor_tensor(wend[:, :].unsqueeze(2), B(0).rearrange("p (h s) -> p h s", h=4)[:, :, P - 1:P],
                                      cum[:, 0:4].unsqueeze(2), ALU.subtract)
                    for t in range(TT):
                        for h in range(4):
                            last = dve.tensor_scalar(dif[:, t, P * h:P * h + P], B(t, P * h, P * h + P),
                                                     cum[:, 4 * t + h:4 * t + h + 1], 0.0, ALU.subtract, ALU.min)
                        last.then_inc(sem["ssd_dif"], 1)
                    dve.wait_ge(sem["ssd_xtok"], g("ssd_xtok") + 1)
                    for t in range(TT):
                        dve.tensor_tensor(xdt[:, t, :, :], B(2, 256 * t, 256 * t + 256).rearrange("p (h d) -> p h d", h=4),
                                          per_head(dt[:, 4 * t:4 * t + 4], 64), ALU.mult)
                    dve.wait_ge(sem["ssd_dec"], g("ssd_dec") + 1)
                    dve.drain()
                    dve.tensor_tensor(xe[:, :, :], xdt[:, 0, :, :], per_head(wexp[:, :], 64), ALU.mult)
                    dve.wait_ge(sem["ssd_cb"], g("ssd_cb") + 1)
                    dve.tensor_copy(b_tok[:, :], B(3, 128, 256))
                    dve.tensor_tensor(cbm[:, :, :], B(3, 256, 512).rearrange("p (t s) -> p t s", t=TT),
                                      per_tile(C("upto"), TT), ALU.mult).then_inc(sem["ssd_xe"], 1)
                    dve.drain()
                    four = lambda ap: ap.rearrange("p (h s) -> p h s", h=4)
                    dve.tensor_tensor(four(mt[:, 0, :]), four(dif[:, 0, :]), per_tile(cbm[:, 0, :], 4), ALU.mult)
                    dve.wait_ge(sem["ssd_dec"], g("ssd_dec") + 2)
                    dve.tensor_tensor(four(mt[:, 1, :]), four(dif[:, 1, :]), per_tile(cbm[:, 1, :], 4), ALU.mult)
                    dve.tensor_tensor(four(ce[:, :]), four(ce[:, :]), per_tile(xbc[:, 3, P:S], 4), ALU.mult)\
                       .then_inc(sem["ssd_m"], 1)
                    dve.wait_ge(sem["ssd_st"], g("ssd_st") + 1)
                    dve.tensor_copy(prev[:, :], B(3, 256, 512)).then_inc(sem["ssd_stc"], 1)
                    dve.wait_ge(sem["ssd_y"], g("ssd_y") + 1)
                    for j in range(2):
                        c = 2 * gr + j
                        stt(y_sb[:, 256 * j:256 * j + 256], xbc[:, j, :], skip[:, l, c:c + 1], B(2, 256 * j, 256 * j + 256),
                            ALU.mult, ALU.add)
                    dve.drain()
                    dve.wait_ge(sem["ssd_z"], g("ssd_z") + 1)
                    dve.tensor_tensor(y_sb[:, :], y_sb[:, :], z_sb[:, :, :].rearrange("p j s -> p (j s)"), ALU.mult)\
                       .then_inc(sem["ssd_yg"], 1)
                    dve.wait_ge(sem["ssd_rs"], g("ssd_rs") + 1)
                    for j in range(2):
                        c = SSD_G + 4 * l + 2 * gr + j
                        y = y_sb[:, 256 * j:256 * j + 256]
                        last = stt(y, y, pcol[:, 0, c:c + 1], rs[:, :])
                    last.then_inc(sem["ssd_yn"], 1)
                elif kind == "gla":
                    l, gr = ph["layer"], ph["g"]
                    u, m, ls, bc = sm[:, 0, 0:256], pr[:, 0, 0:256], pr[:, 1, 0:256], rs2[:, 0:256]
                    dve.wait_ge(sem["gla_pgk"], g("gla_pgk") + 1)
                    c = B_GATE + 2 * l + gr
                    dve.tensor_scalar(u, B(3, 256, 512), pcol[:, 1, c:c + 1], None, ALU.add).then_inc(sem["gla_u"], 1)
                    dve.drain()
                    dve.tensor_scalar(m, u, 0.0, None, ALU.min)
                    dve.drain()
                    dve.wait_ge(sem["gla_ls"], g("gla_ls") + 1)
                    dve.tensor_tensor(ls, m, sm[:, 1, 0:256], ALU.subtract)
                    dve.drain()
                    dve.tensor_tensor_scan(bc, C("keep"), ls, 0.0, ALU.mult, ALU.add).then_inc(sem["gla_scan"], 1)
                    dve.drain()
                    chunks = lambda ap: ap.rearrange("p (c s) -> p c s", c=4)
                    dve.tensor_tensor(chunks(rs2[:, 256:512]), chunks(bc)[:, :, 63:64].broadcast_to([P, 4, 64]), chunks(bc),
                                      ALU.subtract).then_inc(sem["gla_ked"], 1)
                    dve.wait_ge(sem["gla_e"], g("gla_e") + 1)
                    dve.wait_ge(slot_used[1], g("slot1") + 2)
                    stt(qk[:, 0:256], B(0, 0, 256), HEAD_SCALE, sq2[:, 0:256])
                    dve.tensor_tensor(qk[:, 256:512], B(0, 256, 512), sq2[:, 256:512], ALU.mult).then_inc(sem["gla_dec"], 1)
                    dve.tensor_tensor(qkc[:, 0:256], B(0, 256, 512), qkn[:, 256:512], ALU.mult).then_inc(sem["gla_kee"], 1)
                    dve.wait_ge(sem["gla_tr"], g("gla_tr") + 1)
                    dve.tensor_copy(qkn[:, 0:256], B(2, 0, 256)).then_inc(sem["gla_kt"], 1)
                    dve.wait_ge(sem["gla_att"], g("gla_att") + 1)
                    for r in (0, 64):
                        view = lambda ap: ap[r:r + 64].rearrange("p h (t s) -> p h t s", t=TT)[:, :, :, r:r + 64]
                        tri = C("tri64")[r:r + 64].unsqueeze(1).unsqueeze(1).broadcast_to([64, 2, TT, 64])
                        last = dve.tensor_tensor(view(attm[:, :, :]), view(bank[:, 0:2, 0:256]), tri, ALU.mult)
                    last.then_inc(sem["gla_attm"], 1)
                    dve.wait_ge(sem["gla_states"], g("gla_states") + 1)
                    dve.tensor_copy(st_sb[:, 0:128], B(2, 256, 384))
                    dve.drain()
                    stt(st_sb[:, 128:256], st_sb[:, 0:128], sq2[:, 127:128], B(3, 0, 128), ALU.mult, ALU.add)
                    dve.drain()
                    stt(st_sb[:, 256:384], st_sb[:, 128:256], sq2[:, 191:192], B(2, 384, 512), ALU.mult, ALU.add)\
                        .then_inc(sem["gla_st"], 1)
                    dve.wait_ge(sem["gla_rs"], g("gla_rs") + 1)
                    two = lambda ap: ap.rearrange("p (a s) -> p a s", a=2)
                    stt(two(y_sb[:, :]), bank[:, 0:2, 256:512], pcol[:, 1, GLA_G + l:GLA_G + l + 1], two(rs2[:, :]))
                    dve.drain()
                    dve.tensor_tensor(two(y_sb[:, :]), two(y_sb[:, :]), silu_g[:, :, :], ALU.mult).then_inc(sem["gla_yn"], 1)
                elif kind == "add":
                    name, freed = ph["last"]
                    done = slot_used[int(name[4:])] if name[:4] == "slot" else \
                        unit_done[int(name[9:])] if name[:4] == "unit" else sem[name]
                    for q in range(4):
                        if q < 3:
                            dve.wait_ge(sem["tiles_done"], g("tiles_done") + q + 1)
                        else:
                            dve.wait_ge(done, g(name) + freed)
                        if ph["gate"] is None:
                            last = dve.tensor_tensor(xT[:, 2 * q:2 * q + 2, :], xT[:, 2 * q:2 * q + 2, :],
                                                     acc[:, 2 * q:2 * q + 2, :], ALU.add)
                        else:
                            l, part = ph["gate"]
                            for m in (2 * q, 2 * q + 1):
                                last = stt(xT[:, m, :], acc[:, m, :], mod[:, l, 8 * part + m:8 * part + m + 1], xT[:, m, :],
                                           ALU.mult, ALU.add)
                        last.then_inc(sem["x_ready"], 1)
                elif kind == "ffn":
                    ada = ph["ada"]

                    def step(f, b, i, more=True, waits=True):
                        count = g("w_high") - 1
                        if more:
                            for n, what in enumerate(("gate", "up")):
                                low(SLOT_FF + n, 2 * (1 - b) + n, count + split_index(what, f + 1))
                        dve.wait_ge(sem["silu_ready"], g("silu_ready") + f + 1)
                        dve.tensor_tensor(mid[:, b, :], silu_g[:, b, :], B(b, 256, 512), ALU.mult).then_inc(sem["mid"], 1)
                        low(SLOT_FF + 2, PART_DOWN if more else PART_LAST, count + split_index("down", f))
                        dve.wait_ge(sem["mid_high"], g("mid_high") + f + 1)
                        dve.tensor_tensor(mid_lo[:, b, :], mid[:, b, :], mid_hi[:, b, :], ALU.subtract).then_inc(sem["mid_ready"], 1)
                        if ada is not None:
                            for n in range(2 * b, 2 * b + 2):
                                ada_unit(at, ada, i, n, waits)

                    for b in range(2):
                        step(b, b, 0, waits=False)
                    with dve.Fori(1, NF // 2 - 1) as i:
                        for b in range(2):
                            step(2 * i + b, b, i)
                    step(NF - 2, 0, NF // 2 - 1)
                    step(NF - 1, 1, NF // 2 - 1, more=False)
                elif kind == "ada_units":
                    ada_store(ph["start"], ph["ada"], ADA_BLOCKS - 2)
                    for n in range(ADA_SLOTS):
                        ada_unit(ph["start"], ph["ada"], ADA_BLOCKS - 1, n, False)
                elif kind == "ada_end":
                    ada = ph["ada"]
                    ada_store(ph["start"], ada, ADA_BLOCKS - 1)
                    dve.drain()
                    for n in range(2):
                        c = 32 + 8 * (2 * ada + n)
                        stt(mod_gain[:, ada, n, :], mod[:, ada, 8 + 24 * n:16 + 24 * n], 1.0, pcol[:, 0, c:c + 8], ALU.add, ALU.mult)
                    dve.drain()
                elif kind == "ple":
                    with dve.Fori(0, KT // 2) as i:
                        for b in range(2):
                            s = SLOT_SMALL + 2 + b
                            dve.wait_ge(slot_used[s], g(f"slot{s}") + i + 2)
                            dve.wait_ge(sem["ple_s"], 2 * i + (g("ple_s") + b + 1))
                            dve.tensor_tensor(sqT[:, bass.ds(2 * i + b, 1), :], silu_g[:, b:b + 1, :], bank[:, 2 * b + 1:2 * b + 2, 0:256],
                                              ALU.mult).then_inc(sem["ple_d"], 1)
                    dve.drain()
                    for q in range(4):
                        dve.tensor_tensor(xT[:, 2 * q:2 * q + 2, :], xT[:, 2 * q:2 * q + 2, :], sqT[:, 2 * q:2 * q + 2, :],
                                          ALU.add).then_inc(sem["x_ready"], 1)
                elif kind == "store":
                    dve.wait_ge(x_turned, 2)
                    for t in range(TT):
                        last = dve.tensor_copy(x_rows[:, t, :], acc[:, 4 * t:4 * t + 4, :].rearrange("p m s -> p (m s)"))
                    last.then_inc(rows_ready, 1)


_INS = """x p positions attn_norm w_in da_q_norm da_k_norm da_lambda_q1 da_lambda_k1 da_lambda_q2 da_lambda_k2
da_sub_norm ssd_conv_w ssd_conv_b ssd_dt_bias ssd_a_log ssd_d ssd_norm gla_w_gate2 gla_b_gate gla_norm w_out ffn_norm
w_ffn_gate w_ffn_up w_ffn_down ple_w_proj ple_w_gate c_2 ada_w_2 ada_b_2 norm_gain_2 ffn_w_gate_2 ffn_w_up_2
ffn_w_down_2 sb_w_in_2 sb_w_out_2 moba_w_in_2 moba_qk_gain_2 moba_w_out_2 swa_w_in_2 swa_qk_gain_2 swa_sinks_2
swa_w_out_2""".split()


def kernel(**inputs):
    import numpy as _np
    import concourse.bacc as _bacc
    from concourse import mybir as _mybir
    from concourse.bass_utils import run_bass_kernel_spmd as _run

    nc = _bacc.Bacc("TRN2", target_bir_lowering=False, num_devices=1)
    arrays, aps = {}, {}
    for name in _INS:
        v = _np.ascontiguousarray(inputs[name])
        arrays[f"in_{name}_dram"] = v
        aps[name] = nc.dram_tensor(f"in_{name}_dram", v.shape, _mybir.dt.from_np(v.dtype), kind="ExternalInput").ap()
    table, cols = constants()
    table_dram = nc.inline_tensor(table, "table").ap()
    out = nc.dram_tensor("out_0_dram", (1, S, D), _mybir.dt.float32, kind="ExternalOutput").ap()
    two_stacks(nc, aps, table_dram, cols, out)
    r = _run(nc, [arrays], core_ids=[0])
    return r.results[0]["out_0_dram"]
```
